# Optimizing a Trainium2 kernel written in Bass

```python
import math
import jax, jax.numpy as jnp
from jax import lax
import numpy as np

D_MODEL = 1024
BATCH = 1
SEQ = 1024
DEPTH = 2
DEC_BATCH = 8
DEC_SEQ = 8
PAST_LEN = 2048
PAGE_SIZE = 128

N_EVEN = (DEPTH + 1) // 2
N_ODD = DEPTH // 2
HEAD_DIM = 64
NSA_HEADS = 8
NSA_KV_HEADS = 2
NSA_GROUP = NSA_HEADS // NSA_KV_HEADS
CMP_BLOCK = 64
SEL_BLOCK = CMP_BLOCK
CMP_HIDDEN = 64
SEL_TOPK = 16
NSA_WINDOW = 512
SEL_FORCE = 1.0e4
SSM_HEADS = 8
SSM_HEAD_DIM = 64
SSM_D_INNER = SSM_HEADS * SSM_HEAD_DIM
SSM_GROUPS = 2
SSM_STATE = 128
SSM_CONV = 4
SSM_CHUNK = 128
SSM_CONV_DIM = SSM_D_INNER + 2 * SSM_GROUPS * SSM_STATE
SWA_HEADS = 16
SWA_KV_HEADS = 2
SWA_GROUP = SWA_HEADS // SWA_KV_HEADS
SWA_WINDOW = 128
FFN_HIDDEN = -(-8 * D_MODEL // (3 * 256)) * 256
Q_BLK = 128
RMS_EPS = 1e-6
NSA_WIDTH = NSA_HEADS * HEAD_DIM
NSA_KV_WIDTH = 2 * NSA_KV_HEADS * HEAD_DIM
EVEN_SPLITS = (NSA_WIDTH, NSA_KV_WIDTH, NSA_KV_WIDTH, NSA_KV_WIDTH, 3 * NSA_HEADS, SSM_D_INNER, SSM_CONV_DIM, SSM_HEADS)
EVEN_PROJ = sum(EVEN_SPLITS)
EVEN_MIX = NSA_WIDTH + SSM_D_INNER
SWA_WIDTH = SWA_HEADS * HEAD_DIM
SWA_KV_WIDTH = 2 * SWA_KV_HEADS * HEAD_DIM
ODD_PROJ = SWA_WIDTH + SWA_KV_WIDTH
F32 = jnp.float32

kernel_name = "hybrid_nsa_mamba2_swa_decoder_step"

def rmsnorm(x, g):
    xf = x.astype(F32)
    y = xf * lax.rsqrt(jnp.mean(xf * xf, axis=-1, keepdims=True) + RMS_EPS)
    return (y * g.astype(F32)).astype(x.dtype)

def split_cols(x, sizes):
    return jnp.split(x, np.cumsum(sizes)[:-1].tolist(), axis=-1)

def alibi_slopes(n_heads, n_groups):
    s = 2.0 ** (-8.0 * np.arange(1, n_heads + 1) / n_heads)
    return jnp.asarray(s, F32).reshape(n_groups, n_heads // n_groups)

def masked_softmax(s, mask, sink=None):
    s = jnp.where(mask, s.astype(F32), -jnp.inf)
    m = jnp.max(s, axis=-1, keepdims=True)
    if sink is not None:
        m = jnp.maximum(m, sink)
    m = jnp.where(jnp.isfinite(m), m, 0.0)
    e = jnp.exp(s - m)
    den = jnp.sum(e, axis=-1, keepdims=True)
    if sink is not None:
        den = den + jnp.exp(sink - m)
    return e / jnp.maximum(den, 1e-30)

def gather_pages(pool, page_table):
    b, n_pages = page_table.shape
    rows = pool[page_table]
    return rows.reshape((b, n_pages * pool.shape[1]) + pool.shape[2:])

def banded_attention(q, kv_all, pos0, window, slopes, sinks=None):
    b, L, G, R, D = q.shape
    P = kv_all.shape[1] - L
    qb = math.gcd(L, Q_BLK)
    nc = L // qb
    kl = P + qb
    rows = jnp.arange(nc)[:, None] * qb + jnp.arange(kl)[None, :]
    kv = kv_all[:, rows]
    qc = q.reshape(b, nc, qb, G, R, D)
    s = jnp.einsum('bcqgrd,bckgd->bcqgrk', qc, kv[:, :, :, 0]).astype(F32) * (D ** -0.5)
    dist = P + jnp.arange(qb)[:, None] - jnp.arange(kl)[None, :]
    s = s - slopes[None, None, None, :, :, None] * dist[None, None, :, None, None, :].astype(F32)
    mask = ((dist >= 0) & (dist <= window))[None, None, :, None, None, :] & (pos0 - P + rows >= 0)[None, :, None, None, None, :]
    sk = None if sinks is None else sinks.astype(F32)[None, None, None, :, :, None]
    p = masked_softmax(s, mask, sk)
    o = jnp.einsum('bcqgrk,bckgd->bcqgrd', p.astype(q.dtype), kv[:, :, :, 1])
    return o.reshape(b, L, G, R, D)

def compress_blocks(rows, pe, w1, w2):
    h = jnp.einsum('bnlgd,ldh->bngh', rows + pe[None, None, :, None, :], w1)
    return jnp.einsum('bngh,hd->bngd', jax.nn.gelu(h), w2)

def select_attention(qg, idx, t_pos, kv_blocks, slopes):
    b, L, G, R, D = qg.shape
    K = idx.shape[-1]
    qb = math.gcd(L, Q_BLK)
    nc = L // qb
    bi = jnp.arange(b)[:, None, None, None]
    gi = jnp.arange(G)[None, None, :, None]
    offs = jnp.arange(SEL_BLOCK)

    def attend_block(args):
        qc, ic, tc = args
        kv = kv_blocks[bi, ic, :, :, gi].reshape(b, qb, G, K * SEL_BLOCK, 2, D)
        s_pos = (ic[..., None] * SEL_BLOCK + offs).reshape(b, qb, G, K * SEL_BLOCK)
        dist = (tc[None, :, None, None] - s_pos)[:, :, :, None, :]
        s = jnp.einsum('bqgrd,bqgkd->bqgrk', qc, kv[..., 0, :]).astype(F32) * (D ** -0.5)
        s = s - slopes[None, None, :, :, None] * dist.astype(F32)
        p = masked_softmax(s, dist >= 0)
        return jnp.einsum('bqgrk,bqgkd->bqgrd', p.astype(qc.dtype), kv[..., 1, :])

    xs = (jnp.moveaxis(qg.reshape(b, nc, qb, G, R, D), 1, 0),
          jnp.moveaxis(idx.reshape(b, nc, qb, G, K), 1, 0),
          t_pos.reshape(nc, qb))
    out = lax.map(attend_block, xs)
    return jnp.moveaxis(out, 0, 1).reshape(b, L, G, R, D)

def nsa_mixer(q, gates, kv_cmp_all, kv_slc_all, kv_win_all, pos0, pe_k, w1_k, w2_k, pe_v, w1_v, w2_v):
    b, L = q.shape[:2]
    T = kv_cmp_all.shape[1]
    G, R, D = NSA_KV_HEADS, NSA_GROUP, HEAD_DIM
    slopes = alibi_slopes(NSA_HEADS, NSA_KV_HEADS)
    qg = q.reshape(b, L, G, R, D)
    t_pos = pos0 + jnp.arange(L)
    nb = T // CMP_BLOCK
    blk = kv_cmp_all[:, :nb * CMP_BLOCK].reshape(b, nb, CMP_BLOCK, 2, G, D)
    k_c = compress_blocks(blk[:, :, :, 0], pe_k, w1_k, w2_k)
    v_c = compress_blocks(blk[:, :, :, 1], pe_v, w1_v, w2_v)
    dist_c = t_pos[:, None] - ((jnp.arange(nb) + 1) * CMP_BLOCK - 1)[None, :]
    s_c = jnp.einsum('blgrd,bngd->blgrn', qg, k_c).astype(F32) * (D ** -0.5)
    s_c = s_c - slopes[None, None, :, :, None] * dist_c[None, :, None, None, :].astype(F32)
    p_c = masked_softmax(s_c, (dist_c >= 0)[None, :, None, None, :])
    o_cmp = jnp.einsum('blgrn,bngd->blgrd', p_c.astype(q.dtype), v_c)
    nsel = -(-T // SEL_BLOCK)
    imp = jnp.pad(jnp.sum(p_c, axis=3), ((0, 0), (0, 0), (0, 0), (0, nsel - nb)))
    rel = jnp.arange(nsel)[None, :] - (t_pos // SEL_BLOCK)[:, None]
    score = jnp.where(rel[None, :, None, :] < 0, imp,
                      jnp.where(rel == 0, SEL_FORCE, -SEL_FORCE)[None, :, None, :])
    _, idx = lax.top_k(score, min(SEL_TOPK, nsel))
    kv_pad = jnp.pad(kv_slc_all, ((0, 0), (0, nsel * SEL_BLOCK - T), (0, 0), (0, 0), (0, 0)))
    kv_blocks = kv_pad.reshape(b, nsel, SEL_BLOCK, 2, G, D)
    o_slc = select_attention(qg, idx, t_pos, kv_blocks, slopes)
    o_win = banded_attention(qg, kv_win_all, pos0, NSA_WINDOW, slopes)
    g = gates.reshape(b, L, G, R, 3)
    o = g[..., 0:1] * o_cmp + g[..., 1:2] * o_slc + g[..., 2:3] * o_win
    return o.reshape(b, L, NSA_WIDTH)

def ssd_scan(x, dt, a, bm, cm, s0):
    b, L, H, P = x.shape
    q = math.gcd(L, SSM_CHUNK)
    nc = L // q
    hpg = SSM_HEADS // SSM_GROUPS
    xdt = (x.astype(F32) * dt[..., None]).reshape(b, nc, q, H, P)
    bh = jnp.repeat(bm.astype(F32), hpg, axis=2).reshape(b, nc, q, H, SSM_STATE)
    ch = jnp.repeat(cm.astype(F32), hpg, axis=2).reshape(b, nc, q, H, SSM_STATE)
    acum = jnp.cumsum((dt * a).reshape(b, nc, q, H), axis=2)
    causal = jnp.tril(jnp.ones((q, q), bool))[None, None, :, :, None]
    seg = acum[:, :, :, None, :] - acum[:, :, None, :, :]
    lmat = jnp.where(causal, jnp.exp(jnp.where(causal, seg, 0.0)), 0.0)
    cb = jnp.einsum('bcihn,bcjhn->bcijh', ch, bh)
    y_diag = jnp.einsum('bcijh,bcjhp->bcihp', cb * lmat, xdt)
    decay_end = jnp.exp(acum[:, :, -1:, :] - acum)
    chunk_states = jnp.einsum('bcjhn,bcjh,bcjhp->bchpn', bh, decay_end, xdt)
    chunk_decay = jnp.exp(acum[:, :, -1, :])

    def step(s, inp):
        st, dec = inp
        return s * dec[:, :, None, None] + st, s

    s_final, starts = lax.scan(step, s0.astype(F32), (jnp.moveaxis(chunk_states, 1, 0), jnp.moveaxis(chunk_decay, 1, 0)))
    starts = jnp.moveaxis(starts, 0, 1)
    y_off = jnp.einsum('bcihn,bchpn,bcih->bcihp', ch, starts, jnp.exp(acum))
    y = (y_diag + y_off).reshape(b, L, H, P)
    return y.astype(x.dtype), s_final.astype(s0.dtype)

def mamba_mixer(z, xbc, dt_raw, conv0, ssm0, conv_w, conv_b, dt_bias, a_log, d_skip, norm_g):
    b, L = z.shape[:2]
    xpad = jnp.concatenate([conv0.astype(xbc.dtype), xbc], axis=1)
    acc = conv_b
    for k in range(SSM_CONV):
        acc = acc + xpad[:, k:k + L] * conv_w[k]
    new_conv = xpad[:, L:]
    xs, bm, cm = split_cols(jax.nn.silu(acc), (SSM_D_INNER, SSM_GROUPS * SSM_STATE, SSM_GROUPS * SSM_STATE))
    x = xs.reshape(b, L, SSM_HEADS, SSM_HEAD_DIM)
    dt = jax.nn.softplus(dt_raw.astype(F32) + dt_bias.astype(F32))
    a = -jnp.exp(a_log.astype(F32))
    y, s_final = ssd_scan(x, dt, a, bm.reshape(b, L, SSM_GROUPS, SSM_STATE), cm.reshape(b, L, SSM_GROUPS, SSM_STATE), ssm0)
    y = (y + d_skip[None, None, :, None] * x).reshape(b, L, SSM_D_INNER)
    y = rmsnorm(y * jax.nn.silu(z), norm_g)
    return y, s_final, new_conv

def even_layer(x, pos0, past_cmp, past_slc, win_buf, win_out_len, conv0, ssm0, p):
    (norm_g, w_in, w_out, pe_k, w1_k, w2_k, pe_v, w1_v, w2_v,
     conv_w, conv_b, dt_bias, a_log, d_skip, ssm_norm) = p
    b, L = x.shape[:2]
    h = rmsnorm(x, norm_g)
    q, kvc, kvs, kvw, gt, z, xbc, dtr = split_cols(h @ w_in, EVEN_SPLITS)
    kv_shape = (b, L, 2, NSA_KV_HEADS, HEAD_DIM)
    kvc, kvs, kvw = kvc.reshape(kv_shape), kvs.reshape(kv_shape), kvw.reshape(kv_shape)
    kv_win_all = jnp.concatenate([win_buf.astype(x.dtype), kvw], axis=1)
    o_nsa = nsa_mixer(q.reshape(b, L, NSA_HEADS, HEAD_DIM), jax.nn.sigmoid(gt).reshape(b, L, NSA_HEADS, 3),
                      jnp.concatenate([past_cmp.astype(x.dtype), kvc], axis=1),
                      jnp.concatenate([past_slc.astype(x.dtype), kvs], axis=1),
                      kv_win_all, pos0, pe_k, w1_k, w2_k, pe_v, w1_v, w2_v)
    o_ssm, ssm_new, conv_new = mamba_mixer(z, xbc, dtr, conv0, ssm0, conv_w, conv_b, dt_bias, a_log, d_skip, ssm_norm)
    x = x + jnp.concatenate([o_nsa, o_ssm], axis=-1) @ w_out
    return x, (kvc, kvs, kv_win_all[:, -win_out_len:], ssm_new, conv_new)

def odd_layer(x, pos0, swa_buf, out_len, p):
    norm_g, w_in, w_out, sinks = p
    b, L = x.shape[:2]
    h = rmsnorm(x, norm_g)
    q, kv = split_cols(h @ w_in, (SWA_WIDTH, SWA_KV_WIDTH))
    kv_all = jnp.concatenate([swa_buf.astype(x.dtype), kv.reshape(b, L, 2, SWA_KV_HEADS, HEAD_DIM)], axis=1)
    o = banded_attention(q.reshape(b, L, SWA_KV_HEADS, SWA_GROUP, HEAD_DIM), kv_all, pos0, SWA_WINDOW,
                         alibi_slopes(SWA_HEADS, SWA_KV_HEADS), sinks.reshape(SWA_KV_HEADS, SWA_GROUP))
    x = x + o.reshape(b, L, SWA_WIDTH) @ w_out
    return x, kv_all[:, -out_len:]

def ffn(x, norm_g, w_gu, w_down):
    h = rmsnorm(x, norm_g)
    g, u = jnp.split(h @ w_gu, 2, axis=-1)
    return x + (jax.nn.silu(g) * u) @ w_down

def setup_inputs(seed: int = 0) -> dict:
    key = jax.random.key(seed)
    ks = iter(jax.random.split(key, 48))

    def nrm(shape, scale=1.0):
        return jax.random.normal(next(ks), shape, jnp.float32) * scale

    n_pages = PAST_LEN // PAGE_SIZE
    n_pool = (DEC_BATCH * n_pages * 5) // 4
    win_nsa = min(NSA_WINDOW, PAST_LEN)
    win_swa = min(SWA_WINDOW, PAST_LEN)
    kv_nsa = (2, NSA_KV_HEADS, HEAD_DIM)
    kv_swa = (2, SWA_KV_HEADS, HEAD_DIM)
    page_table = jax.random.permutation(next(ks), n_pool)[: DEC_BATCH * n_pages].reshape(DEC_BATCH, n_pages).astype(jnp.int32)
    dt0 = jnp.exp(jax.random.uniform(next(ks), (N_EVEN, SSM_HEADS), jnp.float32, math.log(1e-3), math.log(1e-1)))
    a0 = jax.random.uniform(next(ks), (N_EVEN, SSM_HEADS), jnp.float32, 1.0, 16.0)
    return {
        "x_prompt": nrm((BATCH, SEQ, D_MODEL)),
        "x_sample": nrm((DEC_BATCH, DEC_SEQ, D_MODEL)),
        "cache_nsa_cmp_kv": nrm((N_EVEN, n_pool, PAGE_SIZE) + kv_nsa),
        "cache_nsa_slc_kv": nrm((N_EVEN, n_pool, PAGE_SIZE) + kv_nsa),
        "state_nsa_win_kv": nrm((N_EVEN, DEC_BATCH, win_nsa) + kv_nsa),
        "state_ssm": nrm((N_EVEN, DEC_BATCH, SSM_HEADS, SSM_HEAD_DIM, SSM_STATE), 0.5),
        "state_ssm_conv": nrm((N_EVEN, DEC_BATCH, SSM_CONV - 1, SSM_CONV_DIM)),
        "state_swa_kv": nrm((N_ODD, DEC_BATCH, win_swa) + kv_swa),
        "page_table": page_table,
        "norm_mix": 1.0 + nrm((DEPTH, D_MODEL), 0.02),
        "norm_ffn": 1.0 + nrm((DEPTH, D_MODEL), 0.02),
        "norm_final": 1.0 + nrm((D_MODEL,), 0.02),
        "w_in_even": nrm((N_EVEN, D_MODEL, EVEN_PROJ), D_MODEL ** -0.5),
        "w_out_even": nrm((N_EVEN, EVEN_MIX, D_MODEL), EVEN_MIX ** -0.5),
        "cmp_pe_k": nrm((N_EVEN, CMP_BLOCK, HEAD_DIM), 0.1),
        "cmp_w1_k": nrm((N_EVEN, CMP_BLOCK, HEAD_DIM, CMP_HIDDEN), (CMP_BLOCK * HEAD_DIM) ** -0.5),
        "cmp_w2_k": nrm((N_EVEN, CMP_HIDDEN, HEAD_DIM), CMP_HIDDEN ** -0.5),
        "cmp_pe_v": nrm((N_EVEN, CMP_BLOCK, HEAD_DIM), 0.1),
        "cmp_w1_v": nrm((N_EVEN, CMP_BLOCK, HEAD_DIM, CMP_HIDDEN), (CMP_BLOCK * HEAD_DIM) ** -0.5),
        "cmp_w2_v": nrm((N_EVEN, CMP_HIDDEN, HEAD_DIM), CMP_HIDDEN ** -0.5),
        "ssm_conv_w": nrm((N_EVEN, SSM_CONV, SSM_CONV_DIM), SSM_CONV ** -0.5),
        "ssm_conv_b": nrm((N_EVEN, SSM_CONV_DIM), 0.02),
        "ssm_dt_bias": dt0 + jnp.log(-jnp.expm1(-dt0)),
        "ssm_a_log": jnp.log(a0),
        "ssm_d": 1.0 + nrm((N_EVEN, SSM_HEADS), 0.1),
        "ssm_norm": 1.0 + nrm((N_EVEN, SSM_D_INNER), 0.02),
        "w_in_odd": nrm((N_ODD, D_MODEL, ODD_PROJ), D_MODEL ** -0.5),
        "w_out_odd": nrm((N_ODD, SWA_WIDTH, D_MODEL), SWA_WIDTH ** -0.5),
        "swa_sinks": nrm((N_ODD, SWA_HEADS), 0.5),
        "w_gate_up": nrm((DEPTH, D_MODEL, 2 * FFN_HIDDEN), D_MODEL ** -0.5),
        "w_down": nrm((DEPTH, FFN_HIDDEN, D_MODEL), FFN_HIDDEN ** -0.5),
    }

def reference(x_prompt, x_sample, cache_nsa_cmp_kv, cache_nsa_slc_kv, state_nsa_win_kv, state_ssm, state_ssm_conv,
              state_swa_kv, page_table, norm_mix, norm_ffn, norm_final, w_in_even, w_out_even,
              cmp_pe_k, cmp_w1_k, cmp_w2_k, cmp_pe_v, cmp_w1_v, cmp_w2_v,
              ssm_conv_w, ssm_conv_b, ssm_dt_bias, ssm_a_log, ssm_d, ssm_norm,
              w_in_odd, w_out_odd, swa_sinks, w_gate_up, w_down):
    bp, lp = x_prompt.shape[:2]
    bs = x_sample.shape[0]
    past_len = page_table.shape[1] * cache_nsa_cmp_kv.shape[2]
    dt = x_prompt.dtype
    kv_nsa = (2, NSA_KV_HEADS, HEAD_DIM)
    xp, xs = x_prompt, x_sample
    p_cmp, p_slc, p_win, p_ssm, p_conv, p_swa = [], [], [], [], [], []
    s_cmp, s_slc, s_win, s_ssm, s_conv, s_swa = [], [], [], [], [], []
    for layer in range(DEPTH):
        if layer % 2 == 0:
            e = layer // 2
            p = (norm_mix[layer], w_in_even[e], w_out_even[e], cmp_pe_k[e], cmp_w1_k[e], cmp_w2_k[e],
                 cmp_pe_v[e], cmp_w1_v[e], cmp_w2_v[e], ssm_conv_w[e], ssm_conv_b[e], ssm_dt_bias[e],
                 ssm_a_log[e], ssm_d[e], ssm_norm[e])
            xp, (kc, kslc, kw, sh, cv) = even_layer(
                xp, 0, jnp.zeros((bp, 0) + kv_nsa, dt), jnp.zeros((bp, 0) + kv_nsa, dt),
                jnp.zeros((bp, NSA_WINDOW) + kv_nsa, dt), min(NSA_WINDOW, lp),
                jnp.zeros((bp, SSM_CONV - 1, SSM_CONV_DIM), dt),
                jnp.zeros((bp, SSM_HEADS, SSM_HEAD_DIM, SSM_STATE), dt), p)
            p_cmp.append(kc); p_slc.append(kslc); p_win.append(kw); p_ssm.append(sh); p_conv.append(cv)
            xs, (kc, kslc, kw, sh, cv) = even_layer(
                xs, past_len, gather_pages(cache_nsa_cmp_kv[e], page_table),
                gather_pages(cache_nsa_slc_kv[e], page_table),
                state_nsa_win_kv[e], state_nsa_win_kv.shape[2], state_ssm_conv[e], state_ssm[e], p)
            s_cmp.append(kc); s_slc.append(kslc); s_win.append(kw); s_ssm.append(sh); s_conv.append(cv)
        else:
            o = layer // 2
            p = (norm_mix[layer], w_in_odd[o], w_out_odd[o], swa_sinks[o])
            xp, kw = odd_layer(xp, 0, jnp.zeros((bp, SWA_WINDOW, 2, SWA_KV_HEADS, HEAD_DIM), dt), min(SWA_WINDOW, lp), p)
            p_swa.append(kw)
            xs, kw = odd_layer(xs, past_len, state_swa_kv[o], state_swa_kv.shape[2], p)
            s_swa.append(kw)
        xp = ffn(xp, norm_ffn[layer], w_gate_up[layer], w_down[layer])
        xs = ffn(xs, norm_ffn[layer], w_gate_up[layer], w_down[layer])
    y_prompt = rmsnorm(xp, norm_final)
    y_sample = rmsnorm(xs, norm_final)
    return (y_prompt, y_sample,
            jnp.stack(p_cmp), jnp.stack(p_slc), jnp.stack(p_win), jnp.stack(p_ssm), jnp.stack(p_conv), jnp.stack(p_swa),
            jnp.stack(s_cmp), jnp.stack(s_slc), jnp.stack(s_win), jnp.stack(s_ssm), jnp.stack(s_conv), jnp.stack(s_swa))


_drawn_inputs = setup_inputs


def setup_inputs(seed=0):
    import zlib

    import numpy as np

    out = dict(_drawn_inputs(seed))
    spreads = {}
    factors = {'norm_ffn': 3.321,
     'norm_final': 7.489,
     'cmp_pe_k': 50.071,
     'ssm_norm': 4.0,
     'swa_sinks': 18.956,
     'cmp_w1_k': 2.892,
     'cmp_w2_k': 2.976,
     'cmp_pe_v': 4.868}
    for name, (base, spread) in spreads.items():
        noise = np.random.default_rng([zlib.crc32(name.encode()), seed]).standard_normal(out[name].shape)
        drawn = base * np.exp(spread * noise) if base else spread * noise
        out[name] = __import__('jax').numpy.asarray(drawn.astype(out[name].dtype))
    for name, factor in factors.items():
        out[name] = (out[name] * factor).astype(out[name].dtype)
    return out
```

```python
from contextlib import ExitStack

import numpy as np

import concourse.bass as bass
from concourse import mybir

F32 = mybir.dt.float32
I32 = mybir.dt.int32
ALU = mybir.AluOpType
ACT = mybir.ActivationFunctionType
AX_X = mybir.AxisListType.X

P = 128
HALF = 64
D_MODEL = 1024
KC = D_MODEL // P
SEQ = 1024
NB = 8
DL = 8
TS = NB * DL
T = SEQ + TS
PT = SEQ // P
NT = PT + 1
PAST = 2048
PAGE = 128
NPAGE = PAST // PAGE
ALLPAGES = NB * NPAGE
HD = 64
G = 2
R0 = 4
R1 = 8
BLK = 64
NCB = PAST // BLK
PCB = SEQ // BLK
TOPK = 16
WIN0 = 512
WIN1 = 128
SH = 8
SN = 128
SX = 512
XC = 8
CONV = 4
FFN = 2816
FC = FFN // P
EPS = 1e-6
NEG = -1.0e30
FLOOR = -1.0e25
SPLIT = ((0, 368), (368, 736), (736, T))
WCOL = 256
SLOTS = 3
KVW = 3 * 256
KVG = KVW + 24
COL_KV = 512
COL_Z = COL_KV + KVG
COL_X = COL_Z + SX
COL_DT = COL_X + 1024
XPAD = CONV - 1
XS0 = XPAD + SEQ
XW = XS0 + NB * (XPAD + DL)
PG = 32

STAGES = ["setup", "cache", "load", "norm_mix0", "proj0", "prep", "conv", "ssm", "ssm_norm", "cmp", "attn", "dec",
          "out0", "norm_ffn0", "up0", "down0", "norm_mix1", "proj1", "swa", "swa_dec",
          "out1", "norm_ffn1", "up1", "down1", "norm_fin", "store"]
END = {name: 4 * (n + 1) for n, name in enumerate(STAGES)}


def slopes(n):
    return 2.0 ** (-8.0 * np.arange(1, n + 1) / n)


def constants():
    f = np.float32
    c = {}
    p = np.arange(P)
    c["ident"] = np.eye(P)
    s0, s1 = slopes(G * R0), slopes(G * R1)
    rel = np.arange(SEQ) - (SEQ - P)
    dist = p[:, None] - rel[None, :]
    c["bias_slc"] = np.stack([np.where(dist >= 0, -s0[g * R0] * dist, NEG) for g in range(G)], 1)
    dw = dist[:, SEQ - WIN0 - P:]
    c["bias_win"] = np.stack([np.where((dw >= 0) & (dw <= WIN0), -s0[g * R0] * dw, NEG) for g in range(G)], 1)
    d1 = dist[:, SEQ - 2 * P:]
    c["bias_swa"] = np.stack([np.where((d1 >= 0) & (d1 <= WIN1), -s1[g * R1 + r] * d1, NEG)
                              for r in range(R1) for g in range(G)], 1)
    tc = np.arange(PT)[None, :, None] * P + p[:, None, None] - ((np.arange(PCB) + 1) * BLK - 1)[None, None]
    c["bias_cmp"] = np.stack([np.where(tc >= 0, -s0[g * R0 + r] * tc, NEG)
                              for r in range(R0) for g in range(G)], 2)
    hh = p // PCB
    c["cmp_diag"] = (hh[:, None] == np.arange(SX)[None, :] // HD) * 1.0
    b2, g, r, t = p // 64, p // 32 % 2, p // 8 % 4, p % 8
    sl = s0[g * R0 + r]
    c["dec_off"] = sl[:, None] * np.arange(BLK)[None]
    c["dec_blk"] = -sl[:, None] * (PAST + t[:, None] - BLK * np.arange(NCB)[None])
    dw = WIN0 + t[:, None] - np.arange(WIN0)[None]
    c["dec_win"] = np.where(dw <= WIN0, -sl[:, None] * dw, NEG)
    c["dec_cmp"] = -sl[:, None] * (PAST + t[:, None] - ((np.arange(NCB) + 1) * BLK - 1)[None])
    j = np.arange(TS)
    bp = np.arange(NB // 2)
    own = (j // DL)[None, None] == (2 * bp[None, :, None] + b2[:, None, None])
    dn = t[:, None, None] - (j % DL)[None, None]
    c["dec_new"] = np.where(own & (dn >= 0), -sl[:, None, None] * dn, NEG)
    q = 64 * b2 + 32 * g + t
    c["over_heads"] = (q[:, None] == q[None, :]) * 1.0
    c["earlier"] = np.broadcast_to(np.arange(NCB)[None, :] < np.arange(NCB)[:, None], (P, NCB, NCB)) * 1.0
    c["tok_rows"] = ((j[:, None, None]) == (DL * (2 * bp[None, :, None] + b2[None, None]) + t[None, None])) * 1.0
    c["gate_pick"] = ((np.arange(G * R0)[None, :] == (g * R0 + r)[:, None])[:, :, None] * np.ones(3)).reshape(P, 24)
    g1, r1 = p // 64, p // 8 % 8
    sl1 = s1[g1 * R1 + r1]
    dw = WIN1 + t[:, None] - np.arange(WIN1)[None]
    c["swa_buf"] = np.where(dw <= WIN1, -sl1[:, None] * dw, NEG)
    own = (j // DL)[None, None] == np.arange(NB)[None, :, None]
    dn = t[:, None, None] - (j % DL)[None, None]
    c["swa_new"] = np.where(own & (dn >= 0), -sl1[:, None, None] * dn, NEG)
    c["causal"] = (p[:, None] <= p[None, :]) * 1.0
    c["causal8"] = ((j[:, None] <= j[None, :]) & (j[:, None] // DL == j[None, :] // DL)) * 1.0
    c["own_seq"] = (j[:, None] // DL == np.arange(NB)[None, :]) * 1.0
    h = np.arange(SH)
    c["head_rows"] = ((h[:, None, None] == h[None, :, None]) * np.ones(P)).reshape(SH, SH * P)
    c["pair_rows"] = ((h[:, None, None] == 2 * np.arange(SH // 2)[None, :, None] + (p // HALF)[None, None]) * 1.0)
    c["last_tok"] = (j[:, None] == (j[None, :] // DL) * DL + DL - 1) * 1.0
    tt = np.arange(T)
    keep = np.where(tt < SEQ, tt % P != 0, tt % DL != 0)
    c["keep"] = np.broadcast_to(keep, (SH, T)) * 1.0
    return {k: np.ascontiguousarray(v.astype(f)) for k, v in c.items()}


INPUTS = ["x_prompt", "x_sample", "cache_nsa_cmp_kv", "cache_nsa_slc_kv", "state_nsa_win_kv", "state_ssm",
          "state_ssm_conv", "state_swa_kv", "page_table", "norm_mix", "norm_ffn", "norm_final", "w_in_even",
          "w_out_even", "cmp_pe_k", "cmp_w1_k", "cmp_w2_k", "cmp_pe_v", "cmp_w1_v", "cmp_w2_v", "ssm_conv_w",
          "ssm_conv_b", "ssm_dt_bias", "ssm_a_log", "ssm_d", "ssm_norm", "w_in_odd", "w_out_odd", "swa_sinks",
          "w_gate_up", "w_down"]
KV = (2, G, HD)
OUTPUTS = [("y_prompt", (1, SEQ, D_MODEL)), ("y_sample", (NB, DL, D_MODEL)),
           ("cmp_prompt", (1, 1, SEQ) + KV), ("slc_prompt", (1, 1, SEQ) + KV), ("win_prompt", (1, 1, WIN0) + KV),
           ("ssm_prompt", (1, 1, SH, HD, SN)), ("conv_prompt", (1, 1, XPAD, 1024)),
           ("swa_prompt", (1, 1, WIN1) + KV),
           ("cmp_sample", (1, NB, DL) + KV), ("slc_sample", (1, NB, DL) + KV), ("win_sample", (1, NB, WIN0) + KV),
           ("ssm_sample", (1, NB, SH, HD, SN)), ("conv_sample", (1, NB, XPAD, 1024)),
           ("swa_sample", (1, NB, WIN1) + KV)]


class Chain:

    def __init__(self, engine, sem):
        self.engine, self.sem, self.n = engine, sem, 0

    def __call__(self, instruction):
        self.n += 1
        instruction.then_inc(self.sem, 1)
        self.engine.wait_ge(self.sem, self.n)


def build(nc, d, const):
    ctx = ExitStack()
    with ctx:
        def sb(name, shape, dt=F32):
            return ctx.enter_context(nc.sbuf_tensor(name, shape, dt))

        sems = {}

        def sem(name):
            if name not in sems:
                sems[name] = ctx.enter_context(nc.semaphore(name))
            return sems[name]

        arena = sb("arena", [P, 48304])
        x0, h0, kv0, q0, z0, b0, w0 = 0, 8704, 17408, 24536, 28888, 33240, 42160

        def at(start, *shape, parts=P):
            size = int(np.prod(shape))
            v = arena[0:parts, start:start + size]
            if len(shape) == 2:
                v = v.rearrange("p (a b) -> p a b", a=shape[0])
            if len(shape) == 3:
                v = v.rearrange("p (a b c) -> p a b c", a=shape[0], b=shape[1])
            if len(shape) == 4:
                v = v.rearrange("p (a b c e) -> p a b c e", a=shape[0], b=shape[1], c=shape[2])
            return v

        xT = at(x0, KC, T)
        hT = at(h0, KC, T)
        kvt = at(kv0, NT, KVG)
        qT = at(q0, R0, T)
        zT = at(z0, R0, T)
        xbc = at(b0, XC, XW)
        xc = at(h0, XC, T)
        oN = at(b0, R0, T)
        wp = [at(w0 + s * KC * WCOL, KC, WCOL) for s in range(SLOTS)]
        act_h = at(kv0, FC, T)
        qT1 = at(b0, R1, T)
        kvt1 = at(kv0, NT, 256)
        kT1 = at(q0, 1, T)[:, 0]

        ident = sb("ident", [P, P])
        ones = sb("ones", [P, P])
        cols = sb("cols", [P, 84])
        row24 = sb("row24", [1, 24])
        eps_c = sb("eps_c", [P, 1])
        kcT = sb("kcT", [P, NB * NCB])
        vc = sb("vc", [NCB, NB, P])
        w2 = sb("w2", [P, 2, HD])
        peb = sb("peb", [P, 2])
        sqr = sb("sqr", [P, 2, 368])
        rstd = sb("rstd", [P, 3, 368])
        gates = sb("gates", [P, NT, 24])
        sinks = sb("sinks", [P, R1, G])
        sink_col = sb("sink_col", [P, 1])
        qbd = sb("qbd", [P, NB, 64])
        head_c = sb("head_c", [SH, 4])
        d_col = sb("d_col", [P, 4])
        table = sb("table", [1, ALLPAGES], I32)
        dtok = sb("dtok", [P, NT, 16])
        small = sb("small", [P, 64])
        ps = ctx.enter_context(nc.psum_tensor("ps", [P, 8, 512], F32))

        stage_end = sem("stage_end")
        w_ready = [sem(f"w_ready{s}") for s in range(SLOTS)]
        panel_done = []
        unit_ready = [sem("unit_ready0"), sem("unit_ready1")]
        unit_free = [sem("unit_free0"), sem("unit_free1")]
        stored = sem("stored")
        consts_in = sem("consts_in")

        w_in0 = d["w_in_even"][0].rearrange("(c p) n -> p c n", p=P)
        w_in1 = d["w_in_odd"][0].rearrange("(c p) n -> p c n", p=P)
        w_gu = [d["w_gate_up"][l].rearrange("(c p) n -> p c n", p=P) for l in range(2)]
        w_dn = [d["w_down"][l].rearrange("(c p) n -> p c n", p=P) for l in range(2)]
        cmp_pages = d["cache_nsa_cmp_kv"][0].rearrange("n p a g e -> n p (a g e)")
        slc_pages = d["cache_nsa_slc_kv"][0].rearrange("n p a g e -> n p (a g e)")

        panels = []
        for m in range(4):
            n = min(WCOL, KVG - m * WCOL)
            panels.append(lambda w, m=m, n=n: [(w[:, :, 0:n], w_in0[:, :, COL_KV + m * WCOL:COL_KV + m * WCOL + n])])

        def query_panel(src, heads, rp):
            def pieces(w):
                out = []
                for r in range(2):
                    for g in range(G):
                        c = (g * heads + 2 * rp + r) * HD
                        out.append((w[:, :, r * P + g * HD:r * P + g * HD + HD], src[:, :, c:c + HD]))
                return out
            return pieces

        for rp in range(2):
            panels.append(query_panel(w_in0, R0, rp))
        for m in range(6):
            c = (COL_Z + m * WCOL)
            panels.append(lambda w, c=c: [(w[:, :, :], w_in0[:, :, c:c + WCOL])])
        panels.append(lambda w: [(w[:, :, 0:SH], w_in0[:, :, COL_DT:COL_DT + SH])])

        def out_panel0(m):
            src = d["w_out_even"][0]
            def pieces(w):
                n = slice(m * WCOL, (m + 1) * WCOL)
                out = [(w[g * HD:(g + 1) * HD, 0:R0, :],
                        src[g * 256:(g + 1) * 256, n].rearrange("(r e) n -> e r n", e=HD)) for g in range(G)]
                return out + [(w[:, R0:, :], src[512:1024, n].rearrange("(c p) n -> p c n", p=P))]
            return pieces

        def out_panel1(m):
            src = d["w_out_odd"][0]
            def pieces(w):
                n = slice(m * WCOL, (m + 1) * WCOL)
                return [(w[g * HD:(g + 1) * HD, :, :],
                         src[g * 512:(g + 1) * 512, n].rearrange("(r e) n -> e r n", e=HD)) for g in range(G)]
            return pieces

        def ffn_panels(l):
            for m in range(FFN // WCOL):
                for off in (0, FFN):
                    c = off + m * WCOL
                    panels.append(lambda w, c=c: [(w[:, :, :], w_gu[l][:, :, c:c + WCOL])])
            for n in range(4):
                for k in range(0, FC, 8):
                    e = min(k + 8, FC)
                    panels.append(lambda w, n=n, k=k, e=e: [
                        (w[:, 0:e - k, :], w_dn[l][:, k:e, n * WCOL:(n + 1) * WCOL])])

        for m in range(4):
            panels.append(out_panel0(m))
        ffn_panels(0)
        panels.append(lambda w: [(w[:, :, :], w_in1[:, :, 1024:1280])])
        for rp in range(4):
            panels.append(query_panel(w_in1, R1, rp))
        for m in range(4):
            panels.append(out_panel1(m))
        ffn_panels(1)
        w_count = []
        total = [0] * SLOTS
        for n, p in enumerate(panels):
            total[n % SLOTS] += 16 * len(p(wp[0]))
            w_count.append(total[n % SLOTS])

        class Engine:

            def __init__(self, e, ns, chain):
                self.e, self.ns, self.stage, self.panel, self.seen = e, ns, 0, 0, [0, 0]
                self.chain = Chain(e, sem(f"chain_{chain}"))
                self.count = {}

            def end_stage(self, name):
                assert STAGES[self.stage] == name, name
                self.stage += 1
                self.ns.drain().then_inc(stage_end, 1)
                self.e.wait_ge(stage_end, 4 * self.stage)

            def after(self, name, n=1):
                v = self.count.get(name, 0)
                self.count[name] = v + n
                return v

            def next_panel(self):
                n = self.panel
                self.panel += 1
                self.e.wait_ge(w_ready[n % SLOTS], w_count[n])
                return wp[n % SLOTS]

            def free_panel(self, semaphore, value):
                panel_done.append((semaphore, value))

            def unit_start(self, s):
                if self.seen[s]:
                    self.e.wait_ge(unit_free[s], self.seen[s])
                self.seen[s] += 1

            def pass_unit(self, s, n=1):
                self.seen[s] += n

            def unit_wait(self, s):
                self.seen[s] += 1
                self.e.wait_ge(unit_ready[s], self.seen[s])

        def gain(kind, l=0):
            return {"mix": KC * l, "ffn": 2 * KC + KC * l, "final": 4 * KC, "ssm": 5 * KC}[kind]

        CONV_W, CONV_B = 44, 76

        PGC = PG + 1
        xg = [at(h0 + s * PGC * 256, PGC, 256) for s in range(2)]
        w1b = [at(h0 + 2 * PGC * 256 + s * BLK * P, BLK, P) for s in range(2)]
        hid = at(x0, 2, NPAGE * NB * G)
        vcT = at(x0 + 512, 1, NB * NCB)[:, 0]
        xin = [at(kv0 + s * D_MODEL, D_MODEL, 1)[:, :, 0] for s in range(2)]
        dtraw = rstd[0:SH].rearrange("p a b -> p (a b)")[:, 0:T]
        acum = dtraw
        hv = [at(h0 + i * T, 1, T, parts=SH)[:, 0] for i in range(6)]
        conv_in = at(h0 + 6 * T, 1, 1024, parts=NB * XPAD)[:, 0]
        conv_out = at(h0 + 7 * T, 1, 1024, parts=(NB + 1) * XPAD)[:, 0]
        rows84 = at(x0, 1, P, parts=84)[:, 0]
        sinkx = at(x0 + P, 1, P, parts=1)[:, 0]
        cst = sqr[:].rearrange("p a b -> p (a b)")
        causal, causal8 = cst[:, 0:128], cst[0:TS, 128:192]
        own_seq, last_tok = cst[0:TS, 192:200], cst[0:TS, 200:264]
        m_seg = at(b0, SH, P)
        m_eac = at(b0 + 1024, SH, P)
        m_cb = at(b0 + 2048, G, P)
        m_xdt = at(b0 + 2304, SH, HD)
        m_xw = at(b0 + 2816, SH, HD)
        m_bt = at(b0 + 3328, G, P)
        m_st = at(b0 + 3584, SH, HD)
        s0_in = at(b0 + 4096, NB, 4, SN)
        s0t = at(b0 + 8192, 1, 512)[:, 0]
        m_bd = [at(b0 + g * 1024, NB, SN, parts=TS) for g in range(G)]
        conv_pack = cst[:, 264:264 + XC * 27].rearrange("p (c k) -> p c k", c=XC)
        free_b = b0 + R0 * T

        loads = {
            "setup_in": [(ident[:], const["ident"]),
                         (rows84[0:16], d["norm_mix"].rearrange("l (c p) -> (l c) p", p=P)),
                         (rows84[16:32], d["norm_ffn"].rearrange("l (c p) -> (l c) p", p=P)),
                         (rows84[32:40], d["norm_final"].rearrange("(c p) -> c p", p=P)),
                         (rows84[40:44], d["ssm_norm"][0].rearrange("(c p) -> c p", p=P)),
                         (rows84[44:76], d["ssm_conv_w"][0].rearrange("k (c p) -> (k c) p", p=P)),
                         (rows84[76:84], d["ssm_conv_b"][0].rearrange("(c p) -> c p", p=P)),
                         (row24[0:1, 0:16], d["swa_sinks"]), (row24[0:1, 16:24], d["ssm_d"]),
                         (head_c[:, 0:1], d["ssm_dt_bias"][0].rearrange("(h a) -> h a", a=1)),
                         (head_c[:, 1:2], d["ssm_a_log"][0].rearrange("(h a) -> h a", a=1)),
                         (w2[0:HD, 0], d["cmp_w2_k"][0]), (w2[HD:, 0], d["cmp_w2_k"][0]),
                         (w2[0:HD, 1], d["cmp_w2_v"][0]), (w2[HD:, 1], d["cmp_w2_v"][0])],
            "table_in": [(table[:], d["page_table"].rearrange("b n -> (b n)").rearrange("(a n) -> a n", a=1))],
        }
        block = ctx.enter_context(nc.Block())

        def load(e, name, after=None):
            if after:
                e.wait_ge(stage_end, END[after])
            for dst, src in loads[name]:
                e.dma_start(dst, src).then_inc(sem(name), 16)

        def loaded(e, name):
            e.wait_ge(sem(name), 16 * len(loads[name]))

        def setup_pe(pe, E):
            loaded(pe, "setup_in")
            pe.wait_ge(sem("ones_set"), 1)
            nc.tensor.transpose(ps[:, 0, 0:84], rows84, ident[0:84, 0:84])
            nc.tensor.matmul(ps[:, 0, 128:152], ones[0:1, :], row24[0:1, :], start=True, stop=True)\
                .then_inc(sem("setup_mm"), 1)
            pe.wait_ge(sem("sinkx_set"), 1)
            nc.tensor.matmul(ps[:, 1, 0:1], sinkx, ones[0:1, 0:1], start=True, stop=True)\
                .then_inc(sem("setup_mm"), 1)

        def setup_dve(dve, E):
            nc.vector.memset(ones[:], 1.0).then_inc(sem("ones_set"), 1)
            nc.vector.memset(eps_c[:], EPS)
            loaded(dve, "setup_in")
            nc.vector.tensor_copy(sinkx.rearrange("p (h t) -> p h t", t=DL),
                                  row24[0:1, 0:16].unsqueeze(2).to_broadcast([1, 16, DL])).then_inc(sem("sinkx_set"), 1)
            dve.wait_ge(sem("setup_mm"), 2)
            nc.vector.tensor_copy(cols[:], ps[:, 0, 0:84])
            nc.vector.tensor_copy(sinks[:], ps[:, 0, 128:144].rearrange("p (g r) -> p r g", g=G))
            for h2 in range(2):
                half = slice(h2 * HD, (h2 + 1) * HD)
                nc.vector.tensor_copy(d_col[half, :], ps[half, 0, 144 + h2:152:2])
            nc.vector.tensor_copy(sink_col[:], ps[:, 1, 0:1])

        def setup_act(act, E):
            loaded(act, "setup_in")
            E.chain(nc.scalar.activation(head_c[:, 2:3], head_c[:, 1:2], ACT.Exp))
            nc.scalar.mul(head_c[:, 2:3], head_c[:, 2:3], -1.0)

        NG = ALLPAGES // PG
        NCOL = PGC * G

        def cache_sp(sp):
            for kv, (w, pe_) in enumerate((("cmp_w1_k", "cmp_pe_k"), ("cmp_w1_v", "cmp_pe_v"))):
                for b in range(2):
                    half = slice(b * BLK, (b + 1) * BLK)
                    sp.wait_ge(sem("w1_zero"), 2)
                    sp.dma_start(w1b[kv][half, :, b * HD:(b + 1) * HD], d[w][0]).then_inc(sem("w1_in"), 16)
                    for s in range(2):
                        for g in range(G):
                            c = kv * P + g * HD
                            sp.dma_start(xg[s][half, PG, c:c + HD], d[pe_][0]).then_inc(sem("pe_in"), 16)
            for n in range(NG):
                if n >= 2:
                    sp.wait_ge(sem("hid_mm"), 2 * (n - 1))
                for j in range(0, PG, 8):
                    pages = [sp.value_load(table[0:1, n * PG + j + i:n * PG + j + i + 1], min_val=0, max_val=159)
                             for i in range(8)]
                    for i, page in enumerate(pages):
                        sp.dma_start(xg[n % 2][:, j + i, :], cmp_pages[bass.ds(page, 1)].rearrange("a p n -> p (a n)"))\
                            .then_inc(sem(f"pages_in{n % 2}"), 16)

        def cache_pool(pool, E):
            for kv in range(2):
                nc.gpsimd.memset(w1b[kv][:], 0.0).then_inc(sem("w1_zero"), 1)

        def cache_pe(pe, E):
            pe.wait_ge(sem("w1_in"), 64)
            pe.wait_ge(sem("pe_in"), 16 * 16)
            for n in range(NG):
                pe.wait_ge(sem(f"pages_in{n % 2}"), 16 * PG * (n // 2 + 1))
                if n >= 2:
                    pe.wait_ge(sem("hid_out"), 2 * (n - 1))
                for kv in range(2):
                    for e in range(HD):
                        mm = nc.tensor.matmul(ps[:, 2 * (n % 2) + kv, 0:NCOL], w1b[kv][:, e, :],
                                              xg[n % 2][:, :, kv * P + e:(kv + 1) * P:HD],
                                              start=e == 0, stop=e == HD - 1)
                    mm.then_inc(sem("hid_mm"), 1)
            pe.wait_ge(sem("hid_out"), 2 * NG)
            for kv in range(2):
                for b in range(2):
                    for g in range(G):
                        half = slice(b * HD, (b + 1) * HD)
                        rhs = hid[half, kv].rearrange("p (n g) -> p n g", g=G)[:, :, g]
                        mm = nc.tensor.matmul(ps[g * HD:(g + 1) * HD, 4 + 2 * kv + b, 0:ALLPAGES], w2[half, kv], rhs,
                                              start=True, stop=True)
            mm.then_inc(sem("blocks_mm"), 1)
            pe.wait_ge(sem("blocks_out"), 1)
            for b in range(NB):
                mm = nc.tensor.transpose(ps[0:NCB, b // 4, (b % 4) * P:(b % 4 + 1) * P], vcT[:, b * NCB:(b + 1) * NCB],
                                         ident[:])
            mm.then_inc(sem("blocks_mm"), 1)

        def cache_act(act, E):
            for n in range(NG):
                for kv in range(2):
                    bank = ps[:, 2 * (n % 2) + kv]
                    act.wait_ge(sem("hid_mm"), 2 * n + kv + 1)
                    if n == 0:
                        E.chain(nc.scalar.copy(peb[:, kv:kv + 1], bank[:, PG * G:PG * G + 1]))
                    nc.scalar.activation(hid[:, kv, n * PG * G:(n + 1) * PG * G], bank[:, 0:PG * G],
                                         ACT.Gelu_apprx_tanh, bias=peb[:, kv:kv + 1]).then_inc(sem("hid_out"), 1)

        def cache_dve(dve, E):
            dve.wait_ge(sem("blocks_mm"), 1)
            for b in range(2):
                nc.vector.tensor_copy(kcT[:].rearrange("p (n b) -> p n b", b=2)[:, :, b], ps[:, 4 + b, 0:ALLPAGES])
                mm = nc.vector.tensor_copy(vcT.rearrange("p (n b) -> p n b", b=2)[:, :, b], ps[:, 6 + b, 0:ALLPAGES])
            mm.then_inc(sem("blocks_out"), 1)
            dve.wait_ge(sem("blocks_mm"), 2)
            for h in range(2):
                nc.vector.tensor_copy(vc[:, 4 * h:4 * h + 4, :], ps[0:NCB, h].rearrange("p (b c) -> p b c", b=4))

        def tile_n(i):
            return P if i < PT else TS

        def load_sp(sp):
            sp.wait_ge(stage_end, END["cache"])
            for i in range(NT):
                if i >= 2:
                    sp.wait_ge(sem("x_used"), i - 1)
                src = d["x_prompt"][0, i * P:(i + 1) * P] if i < PT else d["x_sample"].rearrange("b t n -> (b t) n")
                sp.dma_start(xin[i % 2][0:tile_n(i)], src).then_inc(sem(f"x_in{i % 2}"), 16)

        def load_pe(pe, E):
            for i in range(NT):
                n = tile_n(i)
                pe.wait_ge(sem(f"x_in{i % 2}"), 16 * (i // 2 + 1))
                if i >= 2:
                    pe.wait_ge(sem("x_copied"), i - 1)
                    pe.wait_ge(sem("x_copied_a"), i - 1)
                for c in range(KC):
                    mm = nc.tensor.transpose(ps[:, 2 * (i % 2) + c // 4, (c % 4) * n:(c % 4 + 1) * n],
                                             xin[i % 2][0:n, c * P:(c + 1) * P], ident[0:n, 0:n])
                mm.then_inc(sem("x_used"), 1)

        def load_dve(dve, E):
            for i in range(NT):
                n = tile_n(i)
                dve.wait_ge(sem("x_used"), i + 1)
                nc.vector.tensor_copy(xT[:, 0:4, i * P:i * P + n],
                                      ps[:, 2 * (i % 2), 0:4 * n].rearrange("p (c t) -> p c t", c=4))\
                    .then_inc(sem("x_copied"), 1)

        def load_act(act, E):
            for i in range(NT):
                n = tile_n(i)
                act.wait_ge(sem("x_used"), i + 1)
                nc.scalar.copy(xT[:, 4:8, i * P:i * P + n],
                               ps[:, 2 * (i % 2) + 1, 0:4 * n].rearrange("p (c t) -> p c t", c=4))\
                    .then_inc(sem("x_copied_a"), 1)

        def norm_pe(pe, E, n):
            for s, (a, b) in enumerate(SPLIT):
                for c in range(n):
                    k = E.after("norm_sq")
                    pe.wait_ge(sem("norm_sq"), k + 1)
                    mm = nc.tensor.matmul(ps[:, s, 0:b - a], ones[:], sqr[:, c % 2, 0:b - a],
                                          start=c == 0, stop=c == n - 1)
                    mm.then_inc(sem("norm_mm"), 1)

        def norm_act(act, E, n, src, width):
            for s, (a, b) in enumerate(SPLIT):
                for c in range(n):
                    k = E.after("norm_mm")
                    if k >= 2:
                        act.wait_ge(sem("norm_mm"), k - 1)
                    nc.scalar.activation(sqr[:, c % 2, 0:b - a], src(c)[:, a:b], ACT.Square)\
                        .then_inc(sem("norm_sq"), 1)
                act.wait_ge(sem("norm_mm"), E.after("norm_mm", 0))
                E.chain(nc.scalar.activation(rstd[:, s, 0:b - a], ps[:, s, 0:b - a], ACT.Ln,
                                             scale=1.0 / width, bias=eps_c[:]))
                nc.scalar.activation(rstd[:, s, 0:b - a], rstd[:, s, 0:b - a], ACT.Exp, scale=-0.5)\
                    .then_inc(sem("norm_rstd"), 1)

        def norm_dve(dve, E, n, src, dst, gain0):
            for s, (a, b) in enumerate(SPLIT):
                dve.wait_ge(sem("norm_rstd"), E.after("norm_rstd") + 1)
                for c in range(n):
                    nc.vector.scalar_tensor_tensor(out=dst(c)[:, a:b], in0=src(c)[:, a:b],
                                                   scalar=cols[:, gain0 + c:gain0 + c + 1],
                                                   in1=rstd[:, s, 0:b - a], op0=ALU.mult, op1=ALU.mult)

        def dense_unit(pe, E, s, chunks, weight, rhs, first=True, last=True, wait=True):
            if wait:
                E.unit_start(s)
            for n, k in enumerate(chunks):
                for j, (a, b) in enumerate(SPLIT):
                    w = weight(n)
                    mm = nc.tensor.matmul(ps[0:w.shape[-1], 3 * s + j, 0:b - a], w, rhs(k)[:, a:b],
                                          start=first and n == 0, stop=last and n == len(chunks) - 1)
            return mm

        def token_major_pe(pe, E, widths):
            unit = 0
            for n in widths:
                w = E.next_panel()
                for i in range(NT):
                    s = unit % 2
                    unit += 1
                    E.unit_start(s)
                    for k in range(KC):
                        mm = nc.tensor.matmul(ps[0:tile_n(i), 3 * s, 0:n], hT[:, k, i * P:i * P + tile_n(i)],
                                              w[:, k, 0:n], start=k == 0, stop=k == KC - 1)
                    mm.then_inc(unit_ready[s], 1)
                E.free_panel(unit_ready[s], E.seen[s])

        def token_major_out(E, ns, copy, which, widths, dst):
            unit = 0
            for m, n in enumerate(widths):
                for i in range(NT):
                    s = unit % 2
                    unit += 1
                    if s != which:
                        E.pass_unit(s)
                    else:
                        E.unit_wait(s)
                        copy(dst[0:tile_n(i), i, m * 256:m * 256 + n], ps[0:tile_n(i), 3 * s, 0:n])\
                            .then_inc(unit_free[s], 1)

        KV_WIDTHS = [min(WCOL, KVG - m * WCOL) for m in range(4)]
        EVEN = [("q", r) for r in range(4)] + [("z", c) for c in range(4)] + [("x", c) for c in range(XC)] + [("dt", 0)]

        def proj0_pe(pe, E):
            token_major_pe(pe, E, KV_WIDTHS)
            for u, (kind, c) in enumerate(EVEN):
                if u % 2 == 0:
                    w = E.next_panel()
                m = SH if kind == "dt" else P
                mm = dense_unit(pe, E, u % 2, range(KC), lambda n: w[:, n, (u % 2) * P:(u % 2) * P + m], lambda k: hT[:, k])
                mm.then_inc(unit_ready[u % 2], 1)
                if u % 2 == 1 or kind == "dt":
                    E.free_panel(unit_ready[u % 2], E.seen[u % 2])

        def proj0_out(E, which, scaled, copy):
            for u, (kind, c) in enumerate(EVEN):
                if u % 2 != which:
                    E.pass_unit(u % 2)
                    continue
                E.unit_wait(which)
                for j, (a, b) in enumerate(SPLIT):
                    src = ps[0:SH if kind == "dt" else P, 3 * which + j, 0:b - a]
                    if kind == "q":
                        i = scaled(qT[:, c, a:b], src, HD ** -0.5)
                    elif kind == "z":
                        i = copy(zT[:, c, a:b], src)
                    elif kind == "dt":
                        i = copy(dtraw[:, a:b], src)
                    else:
                        e = min(b, SEQ)
                        i = copy(xbc[:, c, XPAD + a:XPAD + e], src[:, 0:e - a])
                        if b > SEQ:
                            dst = xbc[:, c, XS0:].rearrange("p (b t) -> p b t", b=NB)[:, :, XPAD:]
                            i = copy(dst, src[:, SEQ - a:].rearrange("p (b t) -> p b t", b=NB))
                i.then_inc(unit_free[which], 1)

        def proj0_act(act, E):
            token_major_out(E, nc.scalar, nc.scalar.copy, 0, KV_WIDTHS, kvt)
            proj0_out(E, 0, nc.scalar.mul, nc.scalar.copy)

        def proj0_dve(dve, E):
            token_major_out(E, nc.vector, nc.vector.tensor_copy, 1, KV_WIDTHS, kvt)
            proj0_out(E, 1, nc.vector.tensor_scalar_mul, nc.vector.tensor_copy)

        loads["prep_in"] = [(conv_in, d["state_ssm_conv"][0].rearrange("b k n -> (b k) n")),
                            (hv[5], const["keep"])]
        tail = xbc[:, :, XS0:].rearrange("p c (b t) -> p c b t", b=NB)

        def prep_pe(pe, E):
            loaded(pe, "prep_in")
            for c in range(XC):
                mm = nc.tensor.transpose(ps[:, 0, c * 24:(c + 1) * 24], conv_in[:, c * P:(c + 1) * P], ident[0:24, 0:24])
            mm.then_inc(sem("conv_tr"), 1)
            pe.wait_ge(sem("conv_packed"), 1)
            for c in range(XC):
                mm = nc.tensor.transpose(ps[0:27, 1 + c // 4, (c % 4) * P:(c % 4 + 1) * P], conv_pack[:, c], ident[:])
            mm.then_inc(sem("conv_tr"), 1)
            pe.wait_ge(sem("dt_done"), 1)
            for i in range(NT):
                n = tile_n(i)
                nc.tensor.transpose(ps[0:n, 3, i * 16:i * 16 + 8], hv[4][:, i * P:i * P + n], ident[0:SH, 0:SH])
                mm = nc.tensor.transpose(ps[0:n, 3, i * 16 + 8:i * 16 + 16], acum[:, i * P:i * P + n], ident[0:SH, 0:SH])
            mm.then_inc(sem("dtok_tr"), 1)

        def prep_act(act, E):
            nc.scalar.activation(gates[:, 0:PT], kvt[:, 0:PT, KVW:KVG], ACT.Sigmoid)
            nc.scalar.activation(gates[0:TS, PT], kvt[0:TS, PT, KVW:KVG], ACT.Sigmoid)
            for c in range(R0):
                nc.scalar.activation(zT[:, c], zT[:, c], ACT.Silu)
            act.wait_ge(sem("abs_dt"), 1)
            nc.scalar.activation(hv[1], hv[1], ACT.Exp, scale=-1.0).then_inc(sem("exp_dt"), 1)

        def prep_dve(dve, E):
            v, ch = nc.vector, E.chain
            ch(v.tensor_scalar(hv[0], dtraw, head_c[:, 0:1], None, ALU.add))
            ch(v.tensor_scalar(hv[1], hv[0], -1.0, None, ALU.mult))
            v.tensor_tensor(hv[1], hv[1], hv[0], ALU.max).then_inc(sem("abs_dt"), 1)
            v.tensor_scalar(hv[4], hv[0], 0.0, None, ALU.max)
            dve.wait_ge(sem("conv_tr"), 1)
            v.tensor_copy(tail[:, :, :, 0:XPAD], ps[:, 0, 0:192].rearrange("p (c b k) -> p c b k", c=XC, b=NB))
            v.memset(xbc[:, :, 0:XPAD], 0.0)
            v.tensor_copy(conv_pack[:, :, 0:XPAD], xbc[:, :, SEQ:SEQ + XPAD])
            for k in range(XPAD):
                i = v.tensor_copy(conv_pack[:, :, XPAD + k:27:XPAD], tail[:, :, :, DL + k])
            i.then_inc(sem("conv_packed"), 1)
            dve.wait_ge(sem("exp_dt"), 1)
            ch(v.tensor_scalar(hv[2], hv[1], 2.0, None, ALU.add))
            ch(v.reciprocal(hv[2], hv[2]))
            ch(v.tensor_tensor(hv[1], hv[1], hv[2], ALU.mult))
            ch(v.tensor_tensor(hv[2], hv[1], hv[1], ALU.mult))
            ch(v.tensor_scalar(hv[3], hv[2], 1.0 / 15, None, ALU.mult))
            for k in (13, 11, 9, 7, 5, 3):
                ch(v.scalar_tensor_tensor(out=hv[3], in0=hv[3], scalar=1.0 / k, in1=hv[2], op0=ALU.add, op1=ALU.mult))
            ch(v.scalar_tensor_tensor(out=hv[3], in0=hv[3], scalar=1.0, in1=hv[1], op0=ALU.add, op1=ALU.mult))
            ch(v.scalar_tensor_tensor(out=hv[4], in0=hv[3], scalar=2.0, in1=hv[4], op0=ALU.mult, op1=ALU.add))
            ch(v.tensor_scalar(hv[0], hv[4], head_c[:, 2:3], None, ALU.mult))
            loaded(dve, "prep_in")
            v.tensor_tensor_scan(acum, hv[5], hv[0], 0.0, ALU.mult, ALU.add).then_inc(sem("dt_done"), 1)
            dve.wait_ge(sem("conv_tr"), 2)
            for h in range(2):
                i = v.tensor_copy(conv_out[:, h * 512:(h + 1) * 512], ps[0:27, 1 + h])
            i.then_inc(sem("conv_rows"), 1)
            dve.wait_ge(sem("dtok_tr"), 1)
            v.tensor_copy(dtok[:, 0:PT], ps[:, 3, 0:PT * 16].rearrange("p (i h) -> p i h", h=16))
            v.tensor_copy(dtok[0:TS, PT], ps[0:TS, 3, PT * 16:NT * 16])

        stores = [0]

        def store(e, dst, src):
            stores[0] += 1
            e.dma_start(dst, src).then_inc(stored, 16)

        def rows(x):
            return x.rearrange("t a g e -> t (a g e)")

        def prep_pool(pool, E):
            names = (("cmp_prompt", "cmp_sample"), ("slc_prompt", "slc_sample"))
            for n, (pr, sa) in enumerate(names):
                c = slice(n * 256, (n + 1) * 256)
                store(pool, rows(d[pr][0, 0]).rearrange("(i p) n -> p i n", p=P), kvt[:, 0:PT, c])
                store(pool, d[sa][0].rearrange("b t a g e -> (b t) (a g e)"), kvt[0:TS, PT, c])
            store(pool, rows(d["win_prompt"][0, 0]).rearrange("(i p) n -> p i n", p=P), kvt[:, 4:PT, 512:768])
            for b in range(NB):
                store(pool, rows(d["win_sample"][0, b])[WIN0 - DL:], kvt[b * DL:(b + 1) * DL, PT, 512:768])
            store(pool, d["win_sample"][0, :, 0:WIN0 - DL].rearrange("b t a g e -> b (t a g e)"),
                  d["state_nsa_win_kv"][0, :, DL:].rearrange("b t a g e -> b (t a g e)"))
            store(pool, d["swa_sample"][0, :, 0:WIN1 - DL].rearrange("b t a g e -> b (t a g e)"),
                  d["state_swa_kv"][0, :, DL:].rearrange("b t a g e -> b (t a g e)"))
            pool.wait_ge(sem("conv_rows"), 1)
            pool.dma_start(d["conv_prompt"][0, 0], conv_out[0:XPAD]).then_inc(sem("conv_stored"), 16)
            pool.dma_start(d["conv_sample"][0].rearrange("b k n -> (b k) n"), conv_out[XPAD:27])\
                .then_inc(sem("conv_stored"), 16)

        def conv_taps(c):
            for part in range(2):
                out = xc[:, c, 0:SEQ] if part == 0 else xc[:, c, SEQ:].rearrange("p (b t) -> p b t", b=NB)
                taps = [xbc[:, c, k:k + SEQ] if part == 0 else tail[:, c, :, k:k + DL] for k in range(CONV)]
                yield out, taps

        def conv_act(act, E):
            act.wait_ge(sem("conv_stored"), 32)
            for c in range(XC):
                for out, taps in conv_taps(c):
                    i = nc.scalar.activation(out, taps[0], ACT.Identity, scale=cols[:, CONV_W + c:CONV_W + c + 1],
                                             bias=cols[:, CONV_B + c:CONV_B + c + 1])
                i.then_inc(sem("conv_first"), 1)
            for c in range(XC):
                act.wait_ge(sem("conv_sum"), c + 1)
                nc.scalar.activation(xc[:, c], xc[:, c], ACT.Silu)

        def conv_dve(dve, E):
            for c in range(XC):
                dve.wait_ge(sem("conv_first"), c + 1)
                for k in range(1, CONV):
                    w = cols[:, CONV_W + k * XC + c:CONV_W + k * XC + c + 1]
                    for out, taps in conv_taps(c):
                        i = nc.vector.scalar_tensor_tensor(out=out, in0=taps[k], scalar=w, in1=out,
                                                           op0=ALU.mult, op1=ALU.add)
                    if k < CONV - 1:
                        E.chain(i)
                i.then_inc(sem("conv_sum"), 1)

        loads["ssm_in"] = [(causal, const["causal"]), (causal8, const["causal8"]), (own_seq, const["own_seq"]),
                           (last_tok, const["last_tok"])]
        loads["ssm_state_in"] = [(s0_in[:, b], d["state_ssm"][0, b].rearrange("(c h) e n -> (h e) c n", h=2))
                                 for b in range(NB)]

        def toks(i):
            return slice(i * P, i * P + tile_n(i))

        def ssm_pe(pe, E):
            loaded(pe, "ssm_in")
            for c in range(NT):
                n, t = tile_n(c), toks(c)
                if c:
                    pe.wait_ge(sem("ssm_seg"), c)
                    pe.wait_ge(sem("ssm_act"), c)
                for j in range(4):
                    nc.tensor.transpose(ps[0:n, 0, j * P:(j + 1) * P], xc[:, j, t], ident[:])
                for g in range(G):
                    nc.tensor.transpose(ps[0:n, 1, g * P:(g + 1) * P], xc[:, 4 + g, t], ident[:])
                    nc.tensor.matmul(ps[0:n, 2, g * P:g * P + n], xc[:, 4 + g, t], xc[:, 6 + g, t], start=True, stop=True)
                if c == PT:
                    nc.tensor.matmul(ps[0:TS, 1, 256:264], last_tok, dtok[0:TS, PT, 8:16], start=True, stop=True)
                    for h in range(SH):
                        j = h // 2
                        nc.tensor.matmul(ps[h % 2 * HD:(h % 2 + 1) * HD, 1, 272 + 8 * j:280 + 8 * j],
                                         ident[0:SH, h:h + 1].to_broadcast([SH, HD]),
                                         acum[:, SEQ + DL - 1:T:DL], start=True, stop=True)
                for h in range(SH):
                    mm = nc.tensor.matmul(ps[:, 3 + h // 4, (h % 4) * n:(h % 4 + 1) * n],
                                          ident[0:SH, h:h + 1].to_broadcast([SH, P]), acum[:, t], start=True, stop=True)
                mm.then_inc(sem("ssm_pre"), 1)
                pe.wait_ge(sem("ssm_ops"), c + 1)
                if c:
                    pe.wait_ge(sem("ssm_post_out"), min(c, PT))
                if c < PT:
                    for g in range(G):
                        nc.tensor.matmul(ps[:, 5, g * 256:(g + 1) * 256], m_bt[0:n, g], m_xw[0:n, 4 * g:4 * g + 4],
                                         start=True, stop=True)
                    for h in range(SH):
                        out = ps[h % 2 * HD:(h % 2 + 1) * HD, 6, h // 2 * P:h // 2 * P + n]
                        if c:
                            nc.tensor.matmul(out, m_st[:, h], m_eac[:, h, 0:n], start=True, stop=False)
                        mm = nc.tensor.matmul(out, m_xdt[0:n, h], m_seg[0:n, h, 0:n], start=c == 0, stop=True)
                    mm.then_inc(sem("ssm_post"), 1)
                if c == PT - 1:
                    pe.wait_ge(sem("ssm_post_out"), PT)
                    for j in range(4):
                        mm = nc.tensor.transpose(ps[:, 5, j * P:(j + 1) * P], m_st[:, 2 * j:2 * j + 2], ident[:])
                    mm.then_inc(sem("ssm_fin_tr"), 1)
            loaded(pe, "ssm_state_in")
            pe.wait_ge(sem("ssm_fin"), 1)
            for h in range(SH):
                nc.tensor.matmul(ps[h % 2 * HD:(h % 2 + 1) * HD, 6, h // 2 * TS:(h // 2 + 1) * TS], m_xdt[0:TS, h],
                                 m_seg[0:TS, h, 0:TS], start=h < 2, stop=False, skip_group_check=True)
            for b in range(NB + 1):
                if b < NB:
                    for j in range(4):
                        mm = nc.tensor.transpose(ps[:, 5 + 2 * (b % 2), j * P:(j + 1) * P], s0_in[:, b, j], ident[:])
                    mm.then_inc(sem("s0_tr"), 1)
                if b:
                    pe.wait_ge(sem("s0t_ready"), b)
                    for h in range(SH):
                        o = h // 2 * TS + (b - 1) * DL
                        mm = nc.tensor.matmul(ps[h % 2 * HD:(h % 2 + 1) * HD, 6, o:o + DL], s0t[:, h * HD:(h + 1) * HD],
                                              m_eac[:, h, (b - 1) * DL:b * DL], start=False, stop=b == NB,
                                              skip_group_check=True)
                    mm.then_inc(sem("s0t_used"), 1)
            pe.wait_ge(sem("bd_ready"), 1)
            for j in range(4):
                if j >= 2:
                    pe.wait_ge(sem("s_new"), j - 1)
                for k in range(2):
                    mm = nc.tensor.matmul(ps[:, 2 * (j % 2) + k], m_xw[0:TS, 2 * j:2 * j + 2],
                                          m_bd[j // 2][:, 4 * k:4 * k + 4], start=True, stop=True)
                mm.then_inc(sem("s_new_mm"), 1)

        def ssm_dve(dve, E):
            v, ch = nc.vector, E.chain
            loaded(dve, "ssm_in")
            for c in range(NT):
                n, t = tile_n(c), toks(c)
                dve.wait_ge(sem("ssm_pre"), c + 1)
                if c:
                    dve.wait_ge(sem("ssm_post_out"), min(c, PT))
                v.tensor_tensor(m_xdt[0:n], ps[0:n, 0].rearrange("p (h e) -> p h e", h=SH),
                                dtok[0:n, c, 0:8].unsqueeze(2).to_broadcast([n, SH, HD]), ALU.mult)
                if c == PT:
                    v.tensor_tensor(small[0:n, 0:8], ps[0:n, 1, 256:264], dtok[0:n, c, 8:16], ALU.subtract)
                v.tensor_tensor(m_cb[0:n, :, 0:n], ps[0:n, 2, 0:256].rearrange("p (g t) -> p g t", g=G)[:, :, 0:n],
                                (causal if c < PT else causal8).unsqueeze(1).to_broadcast([n, G, n]), ALU.mult)
                for g in range(G):
                    ac = ps[0:n, 3 + g, 0:4 * n].rearrange("p (h t) -> p h t", h=4)
                    dt = dtok[0:n, c, 8 + 4 * g:12 + 4 * g]
                    if c < PT:
                        v.tensor_tensor(small[0:n, 4 * g:4 * g + 4], ac[:, :, n - 1], dt, ALU.subtract)
                    i = v.tensor_tensor(m_seg[0:n, 4 * g:4 * g + 4, 0:n], ac, dt.unsqueeze(2).to_broadcast([n, 4, n]),
                                        ALU.subtract)
                i.then_inc(sem("ssm_seg"), 1)
                dve.wait_ge(sem("ssm_seg"), c + 1)
                v.tensor_scalar(m_seg[0:n, :, 0:n], m_seg[0:n, :, 0:n], 0.0, None, ALU.min).then_inc(sem("ssm_min"), 1)
                dve.wait_ge(sem("ssm_de"), c + 1)
                v.tensor_tensor(m_xw[0:n], m_xdt[0:n], small[0:n, 0:8].unsqueeze(2).to_broadcast([n, SH, HD]), ALU.mult)
                if c < PT:
                    ch(v.tensor_copy(small[:, 16:24], m_eac[:, :, n - 1]))
                for g in range(G):
                    e = m_eac[:, 4 * g:4 * g + 4, 0:n]
                    v.tensor_tensor(e, e, xc[:, 6 + g, t].unsqueeze(1).to_broadcast([P, 4, n]), ALU.mult)
                dve.wait_ge(sem("ssm_l"), c + 1)
                for g in range(G):
                    e = m_seg[0:n, 4 * g:4 * g + 4, 0:n]
                    i = v.tensor_tensor(e, e, m_cb[0:n, g, 0:n].unsqueeze(1).to_broadcast([n, 4, n]), ALU.mult)
                i.then_inc(sem("ssm_ops"), 1)
                if c == PT:
                    break
                dve.wait_ge(sem("ssm_post"), c + 1)
                if c == 0:
                    v.tensor_copy(m_st[:], ps[:, 5].rearrange("p (h e) -> p h e", h=SH))
                else:
                    ch(v.tensor_tensor(m_st[:], m_st[:], small[:, 16:24].unsqueeze(2).to_broadcast([P, SH, HD]), ALU.mult))
                    v.tensor_tensor(m_st[:], m_st[:], ps[:, 5].rearrange("p (h e) -> p h e", h=SH), ALU.add)
                y = m_xdt[:].rearrange("p h e -> p (h e)").rearrange("p (j t) -> p j t", j=4)
                for j in range(4):
                    i = v.scalar_tensor_tensor(out=y[:, j], in0=xc[:, j, t], scalar=d_col[:, j:j + 1],
                                               in1=ps[:, 6, j * P:(j + 1) * P], op0=ALU.mult, op1=ALU.add)
                ch(i)
                v.tensor_tensor(zT[:, :, t], zT[:, :, t], y, ALU.mult).then_inc(sem("ssm_post_out"), 1)
                if c == PT - 1:
                    dve.wait_ge(sem("ssm_fin_tr"), 1)
                    v.tensor_copy(s0t, ps[:, 5]).then_inc(sem("ssm_fin"), 1)
            t = slice(SEQ, T)
            dve.wait_ge(sem("s0t_used"), NB)
            y = m_cb[:].rearrange("p g t -> p (g t)").rearrange("p (j t) -> p j t", j=4)
            for j in range(4):
                i = v.scalar_tensor_tensor(out=y[:, j], in0=xc[:, j, t], scalar=d_col[:, j:j + 1],
                                           in1=ps[:, 6, j * TS:(j + 1) * TS], op0=ALU.mult, op1=ALU.add)
            ch(i)
            v.tensor_tensor(zT[:, :, t], zT[:, :, t], y, ALU.mult)
            for g in range(G):
                i = v.tensor_tensor(m_bd[g], m_bt[0:TS, g].unsqueeze(1).to_broadcast([TS, NB, SN]),
                                    own_seq.unsqueeze(2).to_broadcast([TS, NB, SN]), ALU.mult)
            i.then_inc(sem("bd_ready"), 1)
            for j in range(4):
                dve.wait_ge(sem("s_new_mm"), j + 1)
                for b in range(NB):
                    i = v.scalar_tensor_tensor(out=s0_in[:, b, j], in0=s0_in[:, b, j],
                                               scalar=small[:, 32 + 8 * j + b:33 + 8 * j + b],
                                               in1=ps[:, 2 * (j % 2) + b // 4, (b % 4) * SN:(b % 4 + 1) * SN],
                                               op0=ALU.mult, op1=ALU.add)
                i.then_inc(sem("s_new"), 1)

        def ssm_act(act, E):
            for c in range(NT):
                n = tile_n(c)
                act.wait_ge(sem("ssm_seg"), c + 1)
                if c == PT:
                    nc.scalar.activation(small[:, 32:64], ps[:, 1, 272:304], ACT.Exp)
                nc.scalar.copy(m_bt[0:n], ps[0:n, 1, 0:256].rearrange("p (g e) -> p g e", g=G))
                for g in range(G):
                    i = nc.scalar.activation(m_eac[:, 4 * g:4 * g + 4, 0:n],
                                             ps[:, 3 + g, 0:4 * n].rearrange("p (h t) -> p h t", h=4), ACT.Exp)
                i.then_inc(sem("ssm_act"), 1)
                nc.scalar.activation(small[0:n, 0:8], small[0:n, 0:8], ACT.Exp).then_inc(sem("ssm_de"), 1)
                act.wait_ge(sem("ssm_min"), c + 1)
                nc.scalar.activation(m_seg[0:n, :, 0:n], m_seg[0:n, :, 0:n], ACT.Exp).then_inc(sem("ssm_l"), 1)
            act.wait_ge(sem("ssm_fin_stored"), 16)
            for b in range(NB):
                act.wait_ge(sem("s0_tr"), b + 1)
                if b:
                    act.wait_ge(sem("s0t_used"), b)
                nc.scalar.copy(s0t, ps[:, 5 + 2 * (b % 2)]).then_inc(sem("s0t_ready"), 1)

        def ssm_pool(pool, E):
            pool.wait_ge(sem("ssm_fin"), 1)
            pool.dma_start(d["ssm_prompt"][0, 0].rearrange("(c h) e n -> (h e) c n", h=2),
                           s0t.rearrange("p (c n) -> p c n", c=4)).then_inc(sem("ssm_fin_stored"), 16)
            pool.wait_ge(sem("s_new"), 4)
            for b in range(NB):
                pool.dma_start(d["ssm_sample"][0, b].rearrange("(c h) e n -> (h e) c n", h=2), s0_in[:, b])\
                    .then_inc(sem("s0_stored"), 16)
            pool.wait_ge(sem("s0_stored"), 16 * NB)

        w1c = at(h0, BLK, P)
        cmp_diag = at(h0 + 8192, R0, P)
        pcT = at(free_b, PT, P)
        vbd = at(free_b + 1024, R0, P)
        sc = at(free_b + 1536, PT, 8 * PCB)
        bias_cmp = at(free_b + 2560, PT, 8 * PCB)
        loads["cmp_bias_in"] = [(bias_cmp, const["bias_cmp"].rearrange("p i h n -> p i (h n)")),
                                (cmp_diag, const["cmp_diag"].rearrange("p (r c) -> p r c", r=R0))]
        hid_p = small[:, 0:32].rearrange("p (k n) -> p k n", k=2)
        kcp, vcp = cst[:, 0:PCB], cst[:, 128:256]
        cm, cden = cst[:, 256:320], cst[:, 320:384]

        def cmp_sp(sp):
            load(sp, "cmp_bias_in", "ssm_norm")
            sp.wait_ge(sem("w1c_zero"), 1)
            for kv, w in enumerate(("cmp_w1_k", "cmp_w1_v")):
                if kv:
                    sp.wait_ge(sem("w1c_used"), 1)
                for b in range(2):
                    sp.dma_start(w1c[b * BLK:(b + 1) * BLK, :, b * HD:(b + 1) * HD], d[w][0]).then_inc(sem("w1c_in"), 16)

        def cmp_pool(pool, E):
            nc.gpsimd.memset(w1c, 0.0).then_inc(sem("w1c_zero"), 1)

        def cmp_pe(pe, E):
            for kv in range(2):
                pe.wait_ge(sem("w1c_in"), 32 * (kv + 1))
                for e in range(HD):
                    mm = nc.tensor.matmul(ps[:, kv, 0:PT * G], w1c[:, e, :], kvt[:, 0:PT, kv * P + e:(kv + 1) * P:HD],
                                          start=e == 0, stop=e == HD - 1)
                mm.then_inc(sem("w1c_used"), 1)
            pe.wait_ge(sem("hid_p"), 2)
            for kv in range(2):
                for b in range(2):
                    for g in range(G):
                        half = slice(b * HD, (b + 1) * HD)
                        mm = nc.tensor.matmul(ps[g * HD:(g + 1) * HD, 2 + b, kv * PT:(kv + 1) * PT],
                                              w2[half, kv], hid_p[half, kv, g:PT * G:G], start=True, stop=True)
            mm.then_inc(sem("cmp_mm"), 1)
            pe.wait_ge(sem("cmp_kv"), 1)
            nc.tensor.transpose(ps[:, 3, 0:P], vcp, ident[:]).then_inc(sem("cmp_mm"), 1)
            for i in range(PT):
                for r in range(R0):
                    for g in range(G):
                        o = (i * R0 + r) * PCB
                        half = slice(g * HD, (g + 1) * HD)
                        mm = nc.tensor.matmul(ps[:, 4 + g, o:o + PCB], qT[half, r, toks(i)], kcp[half],
                                              start=True, stop=True)
            mm.then_inc(sem("cmp_mm"), 1)
            pe.wait_ge(sem("cmp_p"), 1)
            for i in range(PT):
                mm = nc.tensor.transpose(ps[:, 6 + i // 4, (i % 4) * P:(i % 4 + 1) * P], sc[:, i], ident[:])
            mm.then_inc(sem("cmp_mm"), 1)

        def cmp_act(act, E):
            for kv in range(2):
                act.wait_ge(sem("w1c_used"), kv + 1)
                nc.scalar.activation(hid_p[:, kv], ps[:, kv, 0:PT * G], ACT.Gelu_apprx_tanh, bias=peb[:, kv:kv + 1])\
                    .then_inc(sem("hid_p"), 1)
            act.wait_ge(sem("cmp_s"), 1)
            nc.scalar.activation(sc, sc, ACT.Exp).then_inc(sem("cmp_e"), 1)

        def cmp_dve(dve, E):
            v, ch = nc.vector, E.chain
            dve.wait_ge(sem("cmp_mm"), 1)
            kb = ps[:, 2:4, 0:2 * PT].rearrange("p b (k n) -> p k n b", k=2)
            v.tensor_copy(kcp.rearrange("p (n b) -> p n b", b=2), kb[:, 0])
            for h in range(8):
                i = v.tensor_copy(vcp[:, h * PCB:(h + 1) * PCB].rearrange("p (n b) -> p n b", b=2), kb[:, 1])
            i.then_inc(sem("cmp_kv"), 1)
            loaded(dve, "cmp_bias_in")
            dve.wait_ge(sem("cmp_mm"), 2)
            v.tensor_tensor(vbd, ps[:, 3, 0:P].unsqueeze(1).to_broadcast([P, R0, P]), cmp_diag, ALU.mult)
            dve.wait_ge(sem("cmp_mm"), 3)
            for g in range(G):
                s5, b5 = (x.rearrange("p i (r g n) -> p i r g n", r=R0, g=G)[:, :, :, g] for x in (sc, bias_cmp))
                i = v.tensor_tensor(s5, ps[:, 4 + g].rearrange("p (i r n) -> p i r n", i=PT, r=R0), b5, ALU.add)
            ch(i)
            s3 = sc.rearrange("p i (h n) -> p (i h) n", n=PCB)
            ch(v.tensor_reduce(cm, s3, AX_X, ALU.max))
            ch(v.tensor_scalar(cm, cm, FLOOR, None, ALU.max))
            v.tensor_tensor(s3, s3, cm.unsqueeze(2).to_broadcast([P, 64, PCB]), ALU.subtract).then_inc(sem("cmp_s"), 1)
            dve.wait_ge(sem("cmp_e"), 1)
            ch(v.tensor_reduce(cden, s3, AX_X, ALU.add))
            ch(v.tensor_scalar(cden, cden, 1e-30, None, ALU.max))
            ch(v.reciprocal(cden, cden))
            for g in range(G):
                c4 = cden.rearrange("p (i r g) -> p i r g", i=PT, r=R0)[:, :, :, g]
                i = v.tensor_tensor(c4, c4, gates[:, 0:PT, g * 12:g * 12 + 12:3], ALU.mult)
            ch(i)
            v.tensor_tensor(s3, s3, cden.unsqueeze(2).to_broadcast([P, 64, PCB]), ALU.mult).then_inc(sem("cmp_p"), 1)
            dve.wait_ge(sem("cmp_mm"), 4)
            for k in range(2):
                v.tensor_copy(pcT[:, 4 * k:4 * k + 4], ps[:, 6 + k].rearrange("p (i t) -> p i t", i=4))

        kS, kW = at(h0, 1, T)[:, 0], at(h0 + T, 1, T)[:, 0]
        bias_s = at(h0 + 2 * T, G, SEQ)
        bias_w = at(h0 + 2 * T + 2048, G, WIN0 + P)
        sp3 = [at(h0 + 2 * T + 3328 + k * 1024, 1, 1024)[:, 0] for k in range(3)]
        pt2 = [at(free_b + 1536 + k * 1024, 8, P) for k in range(2)]
        ob = [at(free_b + 3584 + k * P, G, HD) for k in range(2)]
        knew = at(free_b + 3840, 2, TS)
        negm, den8, scal = small[:, 0:4], small[:, 8:16], small[:, 16:24]
        loads["bias_in"] = [(bias_s, const["bias_slc"]), (bias_w, const["bias_win"])]
        UNITS = [(r, i, g, br) for r in range(R0) for i in range(PT) for g in range(G) for br in range(2)]

        def key_tiles(u):
            _, i, _, br = UNITS[u]
            n = i + 1 if br == 0 else min(i + 1, WIN0 // P + 1)
            return i + 1 - n, n

        groups, first_group = [], []
        for u in range(len(UNITS)):
            first_group.append(len(groups))
            n = key_tiles(u)[1]
            groups += [(u, j, min(4, n - j)) for j in range(0, n, 4)]
        first_group.append(len(groups))

        def attn_pe(pe, E):
            for k, (dst0, col) in enumerate(((0, 256), (3, 512))):
                for i in range(NT):
                    n = tile_n(i)
                    mm = nc.tensor.transpose(ps[:, dst0 + i // 4, (i % 4) * P:(i % 4) * P + n],
                                             kvt[0:n, i, col:col + P], ident[0:n, 0:n])
                mm.then_inc(sem("kt_tr"), 1)
            pe.wait_ge(sem("kt_s"), 1)
            pe.wait_ge(sem("kt_w"), 1)
            n_units = len(UNITS)
            for step in range(n_units + 5):
                if step < n_units:
                    u = step
                    r, i, g, br = UNITS[u]
                    if u >= 2:
                        pe.wait_ge(sem("at_scored"), u - 1)
                    j0, n = key_tiles(u)
                    half = slice(g * HD, (g + 1) * HD)
                    keys = (kS, kW)[br]
                    for a in range(0, n * P, 512):
                        b = min(a + 512, n * P)
                        mm = nc.tensor.matmul(ps[:, 2 * (u % 2) + a // 512, 0:b - a], qT[half, r, toks(i)],
                                              keys[half, j0 * P + a:j0 * P + b], start=True, stop=True)
                    mm.then_inc(sem("at_qk"), 1)
                if 2 <= step < n_units + 2:
                    u = step - 2
                    pe.wait_ge(sem("at_exp"), u + 1)
                    for k in range(first_group[u], first_group[u + 1]):
                        _, j, n = groups[k]
                        if k >= 2:
                            pe.wait_ge(sem(f"at_copied{k % 2}"), k // 2)
                        for b in range(n):
                            mm = nc.tensor.transpose(ps[:, 4 + k % 2, b * P:(b + 1) * P],
                                                     sp3[u % 3][:, (j + b) * P:(j + b + 1) * P], ident[:])
                        mm.then_inc(sem("at_tr"), 1)
                if 3 <= step < n_units + 3:
                    u = step - 3
                    r, i, g, br = UNITS[u]
                    ri, k4 = u // 4, u % 4
                    last = first_group[u + 1] - 1
                    for k in {last, max(last - 1, 0)}:
                        pe.wait_ge(sem(f"at_copied{k % 2}"), k // 2 + 1)
                    if k4 == 0 and ri >= 2:
                        pe.wait_ge(sem("at_oT"), ri - 1)
                    j0, n = key_tiles(u)
                    c = 256 + 256 * br + P + g * HD
                    for j in range(n):
                        mm = nc.tensor.matmul(ps[:, 6 + ri % 2, k4 * HD:(k4 + 1) * HD], pt2[u % 2][:, j],
                                              kvt[:, j0 + j, c:c + HD], start=j == 0, stop=j == n - 1)
                    if k4 == 3:
                        mm = nc.tensor.matmul(ps[:, 6 + ri % 2, 256:384], pcT[:, i], vbd[:, r], start=True, stop=True)
                    mm.then_inc(sem("at_pv"), 1)
                if step >= 8 and step % 4 == 0:
                    ri = step // 4 - 2
                    pe.wait_ge(sem("at_o"), ri + 1)
                    nc.tensor.transpose(ps[:, 6 + ri % 2, 384:512], ob[ri % 2].rearrange("p g e -> p (g e)"), ident[:])\
                        .then_inc(sem("at_ot"), 1)

        def copy_groups(e, copy, u, which):
            for k in range(first_group[u], first_group[u + 1]):
                _, j, n = groups[k]
                if k % 2 == which:
                    e.wait_ge(sem("at_tr"), k + 1)
                    if u >= 2:
                        e.wait_ge(sem("at_pv"), u - 1)
                    copy(pt2[u % 2][:, j:j + n], ps[:, 4 + k % 2, 0:n * P].rearrange("p (j t) -> p j t", j=n))\
                        .then_inc(sem(f"at_copied{which}"), 1)

        def attn_dve(dve, E):
            v, ch = nc.vector, E.chain
            dve.wait_ge(sem("kt_tr"), 1)
            v.tensor_copy(kS[:], ps[:, 0:3].rearrange("p b c -> p (b c)")[:, 0:T]).then_inc(sem("kt_s"), 1)
            loaded(dve, "bias_in")
            n_units = len(UNITS)

            def finish(ri):
                r, i = UNITS[4 * ri][:2]
                dve.wait_ge(sem("at_pv"), 4 * ri + 4)
                s = (ri % 2) * 4
                ch(v.reciprocal(scal[:, s:s + 4], den8[:, s:s + 4]))
                gt = gates[:, i].rearrange("p (g r k) -> p g r k", g=G, r=R0)[:, :, r, 1:3]
                s4 = scal[:, s:s + 4].rearrange("p (g k) -> p g k", g=G)
                ch(v.tensor_tensor(s4, s4, gt, ALU.mult))
                o, bank = ob[ri % 2], ps[:, 6 + ri % 2]
                if ri >= 2:
                    dve.wait_ge(sem("at_ot"), ri - 1)
                ch(v.tensor_copy(o, bank[:, 256:384].rearrange("p (g e) -> p g e", g=G)))
                for br in range(2):
                    for g in range(G):
                        k = g * 2 + br
                        ins = v.scalar_tensor_tensor(out=o[:, g], in0=bank[:, k * HD:(k + 1) * HD],
                                                     scalar=scal[:, s + k:s + k + 1], in1=o[:, g],
                                                     op0=ALU.mult, op1=ALU.add)
                    if br == 0:
                        ch(ins)
                ins.then_inc(sem("at_o"), 1)

            for step in range(n_units + 5):
                if step < n_units:
                    u = step
                    r, i, g, br = UNITS[u]
                    if i == 0 and g == 0 and br == 0 and r:
                        v.tensor_scalar(bias_s, bias_s, 0.5, None, ALU.mult)
                        ch(v.tensor_scalar(bias_w, bias_w, 0.5, None, ALU.mult))
                    n = key_tiles(u)[1] * P
                    bias = (bias_s, bias_w)[br]
                    dve.wait_ge(sem("at_qk"), u + 1)
                    if u >= 3:
                        dve.wait_ge(sem("at_tr"), first_group[u - 2])
                    if u >= 4:
                        dve.wait_ge(sem("at_exp"), u - 3)
                    v.tensor_tensor_reduce(sp3[u % 3][:, 0:n],
                                           ps[:, 2 * (u % 2):2 * (u % 2) + 2].rearrange("p b c -> p (b c)")[:, 0:n],
                                           bias[:, g, bias.shape[2] - n:], -1.0, -NEG, ALU.add, ALU.min,
                                           negm[:, u % 4:u % 4 + 1]).then_inc(sem("at_scored"), 1)
                if 2 <= step < n_units + 2:
                    copy_groups(dve, v.tensor_copy, step - 2, 0)
                if step >= 7 and step % 4 == 3 and step // 4 - 1 < n_units // 4:
                    finish(step // 4 - 1)
            v.tensor_copy(knew[:, 0], kS[:, SEQ:])
            ch(v.tensor_copy(knew[:, 1], kW[:, SEQ:]))
            ch(v.memset(qbd[:], 0.0))
            for g in range(G):
                half = slice(g * HD, (g + 1) * HD)
                v.tensor_copy(qbd[half, :, g * 32:(g + 1) * 32].rearrange("p b (r t) -> p b r t", r=R0),
                              qT[half, :, SEQ:].rearrange("p r (b t) -> p b r t", b=NB))

        def attn_act(act, E):
            act.wait_ge(sem("kt_tr"), 2)
            nc.scalar.copy(kW, ps[:, 3:6].rearrange("p b c -> p (b c)")[:, 0:T]).then_inc(sem("kt_w"), 1)
            n_units = len(UNITS)

            def out(ri):
                r, i = UNITS[4 * ri][:2]
                act.wait_ge(sem("at_ot"), ri + 1)
                nc.scalar.copy(oN[:, r, toks(i)], ps[:, 6 + ri % 2, 384:512]).then_inc(sem("at_oT"), 1)

            for step in range(n_units + 5):
                if step < n_units:
                    u = step
                    n = key_tiles(u)[1] * P
                    act.wait_ge(sem("at_scored"), u + 1)
                    s = (u // 4 % 2) * 4 + u % 4
                    if u % 4 == 0 and u >= 8:
                        act.wait_ge(sem("at_o"), u // 4 - 1)
                    nc.scalar.activation(sp3[u % 3][:, 0:n], sp3[u % 3][:, 0:n], ACT.Exp, scale=-1.0,
                                         bias=negm[:, u % 4:u % 4 + 1], accum_out=den8[:, s:s + 1])\
                        .then_inc(sem("at_exp"), 1)
                if 2 <= step < n_units + 2:
                    copy_groups(act, nc.scalar.copy, step - 2, 1)
                if step >= 9 and step % 4 == 1:
                    out(step // 4 - 2)
            out(n_units // 4 - 1)

        rs = [at(h0 + s * 4096, NPAGE, 256) for s in range(2)]
        kts, ktw = at(kv0, NPAGE, P), at(kv0 + 2048, 4, P)
        rw = [at(kv0 + 2560 + s * 1024, 4, 256) for s in range(2)]
        dec_cmp, dec_blk = at(kv0 + 4608, 1, NCB)[:, 0], at(kv0 + 4640, 1, NCB)[:, 0]
        dec_off, dec_new = at(kv0 + 4672, 1, BLK)[:, 0], at(kv0 + 4736, NB // 2, TS)
        over, tok_rows = at(kv0 + 4992, 1, P)[:, 0], at(kv0 + 5120, NB // 2, P, parts=TS)
        pick, dec_win = at(kv0 + 5632, 1, 24)[:, 0], at(kv0 + 5656, 1, WIN0)[:, 0]
        pts, ptw, ptx = at(q0, NPAGE, P), at(q0 + 2048, 4, P), at(q0 + 2560, 3, P, parts=TS)
        earlier = at(q0 + 2944, 1, NCB * NCB)[:, 0]
        imp, selb = at(q0 + 3968, NB // 2, NCB), at(q0 + 4096, NB // 2, NCB + 1)
        grow = at(q0 + 4228, NB // 2, 3)
        ds = at(free_b, NCB + 1, BLK)
        dw = at(free_b + 2112, 1, WIN0 + TS)[:, 0]
        pc = at(free_b + 2688, NB // 2, NCB)
        ra, rb = at(free_b, NCB, NCB), at(free_b + 1024, NCB, NCB)
        loads["dec_in"] = [(dec_cmp, const["dec_cmp"]), (dec_blk, const["dec_blk"]), (dec_off, const["dec_off"]),
                           (dec_new, const["dec_new"]), (over, const["over_heads"]), (tok_rows, const["tok_rows"]),
                           (pick, const["gate_pick"]), (dec_win, const["dec_win"]),
                           (earlier, const["earlier"].rearrange("p a b -> p (a b)"))]
        NEW_S = kvt[0:TS, PT, 256:512]
        NEW_W = kvt[0:TS, PT, 512:768]

        dgroups = []
        for bp in range(NB // 2):
            for b in (2 * bp, 2 * bp + 1):
                dgroups += [("k", bp, b, j) for j in range(4)] + [("kw", bp, b, 0)]
            dgroups += [("p", bp, 0, j) for j in range(4)] + [("pw", bp, 0, 0), ("px", bp, 0, 0)]

        def dec_sp(sp):
            load(sp, "dec_in", "attn")
            for b in range(NB):
                if b >= 2:
                    sp.wait_ge(sem("dt_pv"), b // 2)
                sp.dma_start(rw[b % 2], d["state_nsa_win_kv"][0, b].rearrange("(j p) a g e -> p j (a g e)", p=P))\
                    .then_inc(sem(f"raw_in{b % 2}"), 16)
                for j in range(0, NPAGE, 8):
                    o = b * NPAGE + j
                    pages = [sp.value_load(table[0:1, o + i:o + i + 1], min_val=0, max_val=159) for i in range(8)]
                    for i, page in enumerate(pages):
                        sp.dma_start(rs[b % 2][:, j + i, :], slc_pages[bass.ds(page, 1)].rearrange("a p n -> p (a n)"))\
                            .then_inc(sem(f"raw_in{b % 2}"), 16)

        def dec_pe(pe, E):
            loaded(pe, "dec_in")
            for b in range(NB):
                part = slice(b % 2 * HD, (b % 2 + 1) * HD)
                nc.tensor.matmul(ps[part, 0, b // 2 * NCB:(b // 2 + 1) * NCB], qbd[:, b], kcT[:, b * NCB:(b + 1) * NCB],
                                 start=True, stop=True)
            for bp in range(NB // 2):
                mm = nc.tensor.matmul(ps[:, 1, bp * 24:(bp + 1) * 24], tok_rows[:, bp], gates[0:TS, PT],
                                      start=True, stop=True)
            mm.then_inc(sem("dt_c"), 1)
            pe.wait_ge(sem("dt_pc"), 1)
            nc.tensor.matmul(ps[:, 2, 0:P], over, pc.rearrange("p b n -> p (b n)"), start=True, stop=True)\
                .then_inc(sem("dt_c"), 1)
            k = 0

            def group(k):
                if k >= 2:
                    pe.wait_ge(sem(f"dt_cp{k % 2}"), k // 2)
                return ps[:, 6 + k % 2]

            def copied(k):
                for j in (k - 1, k):
                    pe.wait_ge(sem(f"dt_cp{j % 2}"), j // 2 + 1)

            for bp in range(NB // 2):
                for b2 in range(2):
                    b = 2 * bp + b2
                    pe.wait_ge(sem(f"raw_in{b2}"), 16 * (NPAGE + 1) * (bp + 1))
                    for j in range(5):
                        bank = group(k)
                        k += 1
                        for i in range(4):
                            src = rs[b2][:, 4 * j + i, 0:P] if j < 4 else rw[b2][:, i, 0:P]
                            mm = nc.tensor.transpose(bank[:, i * P:(i + 1) * P], src, ident[:])
                        mm.then_inc(sem("dt_tr"), 1)
                    copied(k - 1)
                    if b2 == 0:
                        pe.wait_ge(sem("dt_sel"), 1)
                        if bp:
                            pe.wait_ge(sem("dt_out"), bp)
                    part = slice(b2 * HD, (b2 + 1) * HD)
                    for j in range(4):
                        nc.tensor.matmul(ps[part, j], qbd[:, b], kts[:, 4 * j:4 * j + 4].rearrange("p a b -> p (a b)"),
                                         start=True, stop=True)
                    nc.tensor.matmul(ps[part, 4], qbd[:, b], ktw.rearrange("p a b -> p (a b)"), start=True, stop=True)
                    nc.tensor.matmul(ps[part, 5, 0:TS], qbd[:, b], knew[:, 0], start=True, stop=True)
                    nc.tensor.matmul(ps[part, 5, TS:2 * TS], qbd[:, b], knew[:, 1], start=True, stop=True)\
                        .then_inc(sem("dt_qk"), 1)
                pe.wait_ge(sem("dt_p"), bp + 1)
                for j in range(6):
                    bank = group(k)
                    k += 1
                    if j < 5:
                        for i in range(4):
                            src = ds[:, 8 * j + 2 * i:8 * j + 2 * i + 2].rearrange("p a b -> p (a b)") if j < 4 \
                                else dw[:, i * P:(i + 1) * P]
                            mm = nc.tensor.transpose(bank[:, i * P:(i + 1) * P], src, ident[:])
                    else:
                        nc.tensor.transpose(bank[0:TS, 0:P], ds[:, NCB], ident[:])
                        nc.tensor.transpose(bank[0:TS, P:2 * P], dw[:, WIN0:], ident[:])
                        mm = nc.tensor.transpose(bank[0:NCB, 2 * P:3 * P], pc[:, bp], ident[:])
                    mm.then_inc(sem("dt_tr"), 1)
                copied(k - 1)
                for b2 in range(2):
                    b = 2 * bp + b2
                    c = slice(b2 * HD, (b2 + 1) * HD)
                    out = ps[:, 5, P + b2 * HD:P + (b2 + 1) * HD]
                    nc.tensor.matmul(out, vc[:, b], ptx[0:NCB, 2, c], start=True, stop=False)
                    for j in range(NPAGE):
                        nc.tensor.matmul(out, rs[b2][:, j, P:], pts[:, j, c], start=False, stop=False)
                    nc.tensor.matmul(out, NEW_S[:, P:], ptx[:, 0, c], start=False, stop=False)
                    for j in range(4):
                        nc.tensor.matmul(out, rw[b2][:, j, P:], ptw[:, j, c], start=False, stop=False)
                    mm = nc.tensor.matmul(out, NEW_W[:, P:], ptx[:, 1, c], start=False, stop=True)
                mm.then_inc(sem("dt_pv"), 1)

        def dec_copies(e, copy, which, kinds, bp, b=None):
            for k, (kind, gp, gb, j) in enumerate(dgroups):
                if k % 2 != which or kind not in kinds or gp != bp or (b is not None and gb != b):
                    continue
                e.wait_ge(sem("dt_tr"), k + 1)
                if kind[0] == "k" and gb:
                    e.wait_ge(sem("dt_qk"), gb)
                if kind[0] == "p" and bp:
                    e.wait_ge(sem("dt_pv"), bp)
                bank = ps[:, 6 + k % 2]
                b4 = bank.rearrange("p (a b) -> p a b", a=4)
                if kind == "k":
                    i = copy(kts[:, 4 * j:4 * j + 4], b4)
                elif kind == "kw":
                    i = copy(ktw, b4)
                elif kind == "p":
                    i = copy(pts[:, 4 * j:4 * j + 4], b4)
                elif kind == "pw":
                    i = copy(ptw, b4)
                else:
                    copy(ptx[:, 0:2], b4[0:TS, 0:2])
                    i = copy(ptx[0:NCB, 2], bank[0:NCB, 2 * P:3 * P])
                i.then_inc(sem(f"dt_cp{which}"), 1)

        def dec_act(act, E):
            act.wait_ge(sem("dt_cs"), 1)
            nc.scalar.activation(pc, pc, ACT.Exp).then_inc(sem("dt_ce"), 1)
            for bp in range(NB // 2):
                dec_copies(act, nc.scalar.copy, 1, ("k", "kw"), bp)
                act.wait_ge(sem("dt_ms"), bp + 1)
                nc.scalar.activation(ds, ds, ACT.Exp, scale=-1.0, bias=small[:, 0:1], accum_out=small[:, 2:3])
                act.wait_ge(sem("dt_mw"), bp + 1)
                nc.scalar.activation(dw, dw, ACT.Exp, bias=small[:, 1:2], accum_out=small[:, 3:4])\
                    .then_inc(sem("dt_e"), 1)
                dec_copies(act, nc.scalar.copy, 1, ("p", "pw", "px"), bp)

        def dec_dve(dve, E):
            v, ch = nc.vector, E.chain
            loaded(dve, "dec_in")
            dve.wait_ge(sem("dt_c"), 1)
            m4, d4 = small[:, 8:12], small[:, 12:16]
            gp = ra.rearrange("p a b -> p (a b)")[:, 0:96].rearrange("p (b n) -> p b n", b=4)
            ch(v.tensor_tensor(gp, ps[:, 1, 0:96].rearrange("p (b n) -> p b n", b=4),
                               pick.unsqueeze(1).to_broadcast([P, 4, 24]), ALU.mult))
            ch(v.tensor_reduce(grow, gp.rearrange("p b (h k) -> p b k h", k=3), AX_X, ALU.add))
            ch(v.tensor_tensor(pc, ps[:, 0, 0:P].rearrange("p (b n) -> p b n", b=4),
                               dec_cmp.unsqueeze(1).to_broadcast([P, 4, NCB]), ALU.add))
            ch(v.tensor_reduce(m4, pc, AX_X, ALU.max))
            v.tensor_tensor(pc, pc, m4.unsqueeze(2).to_broadcast([P, 4, NCB]), ALU.subtract).then_inc(sem("dt_cs"), 1)
            dve.wait_ge(sem("dt_ce"), 1)
            ch(v.tensor_reduce(d4, pc, AX_X, ALU.add))
            ch(v.reciprocal(d4, d4))
            v.tensor_tensor(pc, pc, d4.unsqueeze(2).to_broadcast([P, 4, NCB]), ALU.mult).then_inc(sem("dt_pc"), 1)
            dve.wait_ge(sem("dt_c"), 2)
            ch(v.tensor_copy(imp, ps[:, 2, 0:P].rearrange("p (b n) -> p b n", b=4)))
            for bp in range(NB // 2):
                other = imp[:, bp].unsqueeze(1).to_broadcast([P, NCB, NCB])
                this = imp[:, bp].unsqueeze(2).to_broadcast([P, NCB, NCB])
                v.tensor_tensor(ra, other, this, ALU.is_gt)
                ch(v.tensor_tensor(rb, other, this, ALU.is_equal))
                ch(v.tensor_tensor(rb, rb, earlier.rearrange("p (a b) -> p a b", a=NCB), ALU.mult))
                ch(v.tensor_tensor(ra, ra, rb, ALU.add))
                ch(v.tensor_reduce(selb[:, bp, 0:NCB], ra, AX_X, ALU.add))
            s = selb[:, :, 0:NCB]
            ch(v.tensor_scalar(s, s, TOPK - 1.5, -NEG, ALU.is_lt, ALU.mult))
            ch(v.tensor_scalar(s, s, NEG, None, ALU.add))
            v.tensor_tensor(s, s, dec_blk.unsqueeze(1).to_broadcast([P, 4, NCB]), ALU.add)
            v.memset(selb[:, :, NCB:], 0.0)
            ch(v.tensor_tensor(pc, pc, grow[:, :, 0:1].to_broadcast([P, 4, NCB]), ALU.mult))
            v.tensor_copy(small[:, 16:17], small[:, 8:9]).then_inc(sem("dt_sel"), 1)
            for bp in range(NB // 2):
                dec_copies(dve, v.tensor_copy, 0, ("k", "kw"), bp)
                dve.wait_ge(sem("dt_qk"), 2 * bp + 2)
                v.tensor_tensor(ds[:, 0:NCB], ps[:, 0:4].rearrange("p a (b c) -> p (a b) c", c=BLK),
                                dec_off.unsqueeze(1).to_broadcast([P, NCB, BLK]), ALU.add)
                v.tensor_tensor(ds[:, NCB], ps[:, 5, 0:TS], dec_new[:, bp], ALU.add)
                v.tensor_tensor(dw[:, 0:WIN0], ps[:, 4], dec_win, ALU.add)
                ch(v.tensor_tensor(dw[:, WIN0:], ps[:, 5, TS:2 * TS], dec_new[:, bp], ALU.add))
                v.tensor_tensor_reduce(ds, ds, selb[:, bp].unsqueeze(2).to_broadcast([P, NCB + 1, BLK]), -1.0, -NEG,
                                       ALU.add, ALU.min, small[:, 0:1]).then_inc(sem("dt_ms"), 1)
                ch(v.tensor_reduce(small[:, 1:2], dw, AX_X, ALU.max))
                v.tensor_scalar(small[:, 1:2], small[:, 1:2], -1.0, None, ALU.mult).then_inc(sem("dt_mw"), 1)
                dve.wait_ge(sem("dt_e"), bp + 1)
                ch(v.reciprocal(small[:, 4:6], small[:, 2:4]))
                ch(v.tensor_tensor(small[:, 4:6], small[:, 4:6], grow[:, bp, 1:3], ALU.mult))
                v.tensor_scalar(ds, ds, small[:, 4:5], None, ALU.mult)
                v.tensor_scalar(dw, dw, small[:, 5:6], None, ALU.mult).then_inc(sem("dt_p"), 1)
                dec_copies(dve, v.tensor_copy, 0, ("p", "pw", "px"), bp)
                dve.wait_ge(sem("dt_pv"), bp + 1)
                for b2 in range(2):
                    for g in range(G):
                        half = slice(g * HD, (g + 1) * HD)
                        c = P + b2 * HD + g * 32
                        t0 = SEQ + (2 * bp + b2) * DL
                        i = v.tensor_copy(oN[half, :, t0:t0 + DL],
                                          ps[half, 5, c:c + 32].rearrange("p (r t) -> p r t", r=R0))
                i.then_inc(sem("dt_out"), 1)

        def residual_pe(pe, E, rhs):
            for m in range(4):
                w = E.next_panel()
                for s in range(2):
                    mm = dense_unit(pe, E, s, range(KC), lambda n: w[:, n, s * P:(s + 1) * P], rhs)
                    mm.then_inc(unit_ready[s], 1)
                E.free_panel(unit_ready[1], E.seen[1])

        def residual_dve(dve, E):
            for u in range(KC):
                E.unit_wait(u % 2)
                for j, (a, b) in enumerate(SPLIT):
                    i = nc.vector.tensor_tensor(xT[:, u, a:b], xT[:, u, a:b], ps[:, 3 * (u % 2) + j, 0:b - a], ALU.add)
                i.then_inc(unit_free[u % 2], 1)

        def skip_units(E, n):
            for s in range(2):
                E.pass_unit(s, n)

        def up_pe(pe, E):
            for m in range(FFN // WCOL):
                w = [E.next_panel(), E.next_panel()]
                for f in range(2):
                    for s in range(2):
                        mm = dense_unit(pe, E, s, range(KC), lambda n: w[s][:, n, f * P:(f + 1) * P], lambda k: hT[:, k])
                        mm.then_inc(unit_ready[s], 1)
                for s in range(2):
                    E.free_panel(unit_ready[s], E.seen[s])

        def up_act(act, E):
            for f in range(FC):
                E.unit_wait(0)
                for j, (a, b) in enumerate(SPLIT):
                    i = nc.scalar.activation(act_h[:, f, a:b], ps[:, j, 0:b - a], ACT.Silu)
                i.then_inc(unit_free[0], 1)
                E.pass_unit(1)

        def up_dve(dve, E):
            for f in range(FC):
                E.unit_wait(1)
                E.pass_unit(0)
                dve.wait_ge(unit_free[0], E.seen[0])
                for j, (a, b) in enumerate(SPLIT):
                    i = nc.vector.tensor_tensor(act_h[:, f, a:b], act_h[:, f, a:b], ps[:, 3 + j, 0:b - a], ALU.mult)
                i.then_inc(unit_free[1], 1)

        def down_pe(pe, E):
            for m in range(4):
                for k in range(0, FC, 8):
                    e = min(k + 8, FC)
                    w = E.next_panel()
                    for s in range(2):
                        mm = dense_unit(pe, E, s, range(k, e), lambda n: w[:, n, s * P:(s + 1) * P],
                                        lambda k: act_h[:, k], first=k == 0, last=e == FC, wait=k == 0)
                        if e == FC:
                            mm.then_inc(unit_ready[s], 1)
                    if e == FC:
                        E.free_panel(unit_ready[1], E.seen[1])
                    else:
                        mm.then_inc(sem("down_mid"), 1)
                        E.free_panel(sem("down_mid"), E.after("down_mid") + 1)

        oT1 = xc

        def proj1_pe(pe, E):
            token_major_pe(pe, E, [256])
            for rp in range(4):
                w = E.next_panel()
                for s in range(2):
                    mm = dense_unit(pe, E, s, range(KC), lambda n: w[:, n, s * P:(s + 1) * P], lambda k: hT[:, k])
                    mm.then_inc(unit_ready[s], 1)
                E.free_panel(unit_ready[1], E.seen[1])

        def proj1_out(E, ns, which, scaled, copy):
            token_major_out(E, ns, copy, which, [256], kvt1)
            for r in range(R1):
                if r % 2 != which:
                    E.pass_unit(r % 2)
                    continue
                E.unit_wait(which)
                for j, (a, b) in enumerate(SPLIT):
                    i = scaled(qT1[:, r, a:b], ps[:, 3 * which + j, 0:b - a], HD ** -0.5)
                i.then_inc(unit_free[which], 1)

        bias1 = at(z0, R1 * G, 2 * P)
        s1 = [at(kv0 + 2304 + k * 1024, 4, 2 * P) for k in range(2)]
        pt1 = [at(kv0 + 4352 + k * 1024, 8, P) for k in range(2)]
        o1 = [at(kv0 + 6400 + k * 256, 4, HD) for k in range(2)]
        loads["bias1_in"] = [(bias1, const["bias_swa"])]
        U1 = [(r, i2) for r in range(R1) for i2 in range(PT // 2)]
        neg1 = [small[:, 16 * k:16 * k + 4] for k in range(2)]
        sink1 = [small[:, 16 * k + 4:16 * k + 8] for k in range(2)]
        den1 = [small[:, 16 * k + 8:16 * k + 12] for k in range(2)]

        def swa_pe(pe, E):
            for i in range(NT):
                n = tile_n(i)
                mm = nc.tensor.transpose(ps[:, i // 4, (i % 4) * P:(i % 4) * P + n], kvt1[0:n, i, 0:P], ident[0:n, 0:n])
            mm.then_inc(sem("kt1_tr"), 1)
            pe.wait_ge(sem("kt1"), 1)
            n_units = len(U1)
            for step in range(n_units + 4):
                if step < n_units:
                    r, i2 = U1[step]
                    if step >= 2:
                        pe.wait_ge(sem("sw_scored"), step - 1)
                    for k in range(4):
                        i, g = 2 * i2 + k // 2, k % 2
                        half = slice(g * HD, (g + 1) * HD)
                        o = P if i == 0 else 0
                        c = (k // 2) * 2 * P
                        mm = nc.tensor.matmul(ps[:, 2 * (step % 2) + g, c + o:c + 2 * P],
                                              qT1[half, r, toks(i)], kT1[half, (i - 1) * P + o:(i + 1) * P],
                                              start=True, stop=True)
                    mm.then_inc(sem("sw_qk"), 1)
                if 1 <= step < n_units + 1:
                    u = step - 1
                    r, i2 = U1[u]
                    pe.wait_ge(sem("sw_exp"), u + 1)
                    for ii in range(2):
                        if u:
                            pe.wait_ge(sem(f"sw_copied{ii}"), u)
                        for k in range(4):
                            g, j = k // 2, k % 2
                            if i2 == 0 and ii == 0 and j == 0:
                                continue
                            mm = nc.tensor.transpose(ps[:, 4 + ii, k * P:(k + 1) * P],
                                                     s1[u % 2][:, 2 * g + ii, j * P:(j + 1) * P], ident[:])
                        mm.then_inc(sem("sw_tr"), 1)
                if 2 <= step < n_units + 2:
                    u = step - 2
                    r, i2 = U1[u]
                    for ii in range(2):
                        pe.wait_ge(sem(f"sw_copied{ii}"), u + 1)
                    if u >= 2:
                        pe.wait_ge(sem("sw_oT"), u - 1)
                    for k in range(4):
                        i, g = 2 * i2 + k // 2, k % 2
                        js = (1,) if i == 0 else (0, 1)
                        for j in js:
                            mm = nc.tensor.matmul(ps[:, 6 + u % 2, k * HD:(k + 1) * HD], pt1[u % 2][:, (k // 2) * 4 + g * 2 + j],
                                                  kvt1[:, i - 1 + j, P + g * HD:P + (g + 1) * HD],
                                                  start=j == js[0], stop=j == 1)
                    mm.then_inc(sem("sw_pv"), 1)
                if 3 <= step < n_units + 3:
                    u = step - 3
                    pe.wait_ge(sem("sw_o"), u + 1)
                    for ii in range(2):
                        mm = nc.tensor.transpose(ps[:, 6 + u % 2, 256 + ii * P:256 + (ii + 1) * P],
                                                 o1[u % 2][:, 2 * ii:2 * ii + 2].rearrange("p g e -> p (g e)"), ident[:])
                    mm.then_inc(sem("sw_ot"), 1)

        def swa_copy(e, copy, u, ii):
            e.wait_ge(sem("sw_tr"), 2 * u + ii + 1)
            if u >= 2:
                e.wait_ge(sem("sw_pv"), u - 1)
            src = ps[:, 4 + ii].rearrange("p (k t) -> p k t", k=4)
            dst = pt1[u % 2][:, 4 * ii:4 * ii + 4]
            if U1[u][1] == 0 and ii == 0:
                src, dst = src[:, 1::2], dst[:, 1::2]
            copy(dst, src).then_inc(sem(f"sw_copied{ii}"), 1)

        def swa_dve(dve, E):
            v, ch = nc.vector, E.chain
            dve.wait_ge(sem("kt1_tr"), 1)
            v.tensor_copy(kT1, ps[:, 0:3].rearrange("p b c -> p (b c)")[:, 0:T]).then_inc(sem("kt1"), 1)
            loaded(dve, "bias1_in")
            n_units = len(U1)
            for step in range(n_units + 3):
                if step < n_units:
                    u = step
                    r, i2 = U1[u]
                    s, bk = s1[u % 2], ps[:, 2 * (u % 2):2 * (u % 2) + 2]
                    dve.wait_ge(sem("sw_qk"), u + 1)
                    if u >= 2:
                        dve.wait_ge(sem("sw_tr"), 2 * u - 2)
                    bias = bias1[:, 2 * r:2 * r + 2]
                    s4 = s.rearrange("p (g i) c -> p g i c", g=2)
                    b4 = bk.rearrange("p g (i c) -> p g i c", i=2)
                    if i2:
                        i = v.tensor_tensor(s4, b4, bias.unsqueeze(2).to_broadcast([P, 2, 2, 2 * P]), ALU.add)
                    else:
                        v.memset(s4[:, :, 0, 0:P], NEG)
                        v.tensor_tensor(s4[:, :, 1], b4[:, :, 1], bias, ALU.add)
                        i = v.tensor_tensor(s4[:, :, 0, P:], b4[:, :, 0, P:], bias[:, :, P:], ALU.add)
                    i.then_inc(sem("sw_scored"), 1)
                    dve.wait_ge(sem("sw_scored"), u + 1)
                    ng, sk = neg1[u % 2], sink1[u % 2]
                    ch(v.tensor_reduce(ng, s, AX_X, ALU.max))
                    sr = sinks[:, r].unsqueeze(2).to_broadcast([P, 2, 2])
                    g4 = ng.rearrange("p (g i) -> p g i", g=2)
                    ch(v.tensor_tensor(g4, g4, sr, ALU.max))
                    v.tensor_tensor(sk.rearrange("p (g i) -> p g i", g=2), sr, g4, ALU.subtract)
                    v.tensor_scalar(ng, ng, -1.0, None, ALU.mult).then_inc(sem("sw_m"), 1)
                if 1 <= step < n_units + 1:
                    swa_copy(dve, v.tensor_copy, step - 1, 0)
                if 3 <= step < n_units + 3:
                    u = step - 3
                    dve.wait_ge(sem("sw_pv"), u + 1)
                    dve.wait_ge(sem("sw_den"), u + 1)
                    dn = den3[u % 3]
                    ch(v.tensor_tensor(dn[:, 0:4], dn[:, 0:4], dn[:, 4:8], ALU.add))
                    ch(v.reciprocal(dn[:, 0:4], dn[:, 0:4]))
                    if u >= 2:
                        dve.wait_ge(sem("sw_ot"), u - 1)
                    v.tensor_tensor(o1[u % 2].rearrange("p (i g) e -> p i g e", i=2),
                                    ps[:, 6 + u % 2, 0:256].rearrange("p (i g e) -> p i g e", i=2, g=G),
                                    dn[:, 0:4].rearrange("p (g i) -> p i g", g=G).unsqueeze(3)
                                    .to_broadcast([P, 2, 2, HD]), ALU.mult).then_inc(sem("sw_o"), 1)

        den3 = [cst[:, 8 * k:8 * k + 8] for k in range(3)]

        def swa_act(act, E):
            n_units = len(U1)
            for step in range(n_units + 4):
                if step < n_units:
                    u = step
                    act.wait_ge(sem("sw_m"), u + 1)
                    if u >= 3:
                        act.wait_ge(sem("sw_o"), u - 2)
                    dn = den3[u % 3]
                    nc.scalar.activation(dn[:, 4:8], sink1[u % 2], ACT.Exp).then_inc(sem("sw_den"), 1)
                    for k in range(4):
                        i = nc.scalar.activation(s1[u % 2][:, k], s1[u % 2][:, k], ACT.Exp,
                                                 bias=neg1[u % 2][:, k:k + 1], accum_out=dn[:, k:k + 1])
                    i.then_inc(sem("sw_exp"), 1)
                if 1 <= step < n_units + 1:
                    swa_copy(act, nc.scalar.copy, step - 1, 1)
                if 4 <= step:
                    u = step - 4
                    r, i2 = U1[u]
                    act.wait_ge(sem("sw_ot"), u + 1)
                    nc.scalar.copy(oT1[:, r, 256 * i2:256 * (i2 + 1)], ps[:, 6 + u % 2, 256:512])\
                        .then_inc(sem("sw_oT"), 1)

        raw1 = at(q0 + T, NB, 256)
        buf1 = at(q0 + T + 2048, 1, WIN1)[:, 0]
        qbd1, kb1 = at(kv0 + 2304, NB, P), at(kv0 + 3328, NB, P)
        sd1 = at(kv0 + 4352, NB, WIN1 + TS)
        pd1, pn1 = at(z0, NB, P), at(z0 + 1024, NB, P, parts=TS)
        new1 = at(z0 + 2048, NB, TS)
        loads["dec1_in"] = [(raw1, d["state_swa_kv"][0].rearrange("b p a g e -> p b (a g e)")), (buf1, const["swa_buf"])]
        loads["new1_in"] = [(new1, const["swa_new"])]

        def swa_dec_pe(pe, E):
            loaded(pe, "dec1_in")
            for b in range(NB):
                mm = nc.tensor.transpose(ps[:, b // 4, (b % 4) * P:(b % 4 + 1) * P], raw1[:, b, 0:P], ident[:])
            mm.then_inc(sem("sd_mm"), 1)
            pe.wait_ge(sem("sd_k"), 1)
            for b in range(NB):
                nc.tensor.matmul(ps[:, 2 + b // 4, (b % 4) * P:(b % 4 + 1) * P], qbd1[:, b], kb1[:, b], start=True, stop=True)
                mm = nc.tensor.matmul(ps[:, 4, b * TS:(b + 1) * TS], qbd1[:, b], kT1[:, SEQ:], start=True, stop=True)
            mm.then_inc(sem("sd_mm"), 1)
            pe.wait_ge(sem("sd_p"), 1)
            for b in range(NB):
                nc.tensor.transpose(ps[:, 5 + b // 4, (b % 4) * P:(b % 4 + 1) * P], sd1[:, b, 0:P], ident[:])
                mm = nc.tensor.transpose(ps[0:TS, 7 * (1 - b // 4), (b % 4) * P:(b % 4 + 1) * P], sd1[:, b, P:], ident[:])
            mm.then_inc(sem("sd_mm"), 1)
            pe.wait_ge(sem("sd_pt"), 1)
            pe.wait_ge(sem("sd_pn"), 1)
            for b in range(NB):
                out = ps[:, 2 + b // 4, (b % 4) * P:(b % 4 + 1) * P]
                nc.tensor.matmul(out, raw1[:, b, P:], pd1[:, b], start=True, stop=False)
                mm = nc.tensor.matmul(out, kvt1[0:TS, PT, P:], pn1[:, b], start=False, stop=True)
            mm.then_inc(sem("sd_mm"), 1)

        def swa_dec_act(act, E):
            act.wait_ge(sem("sd_s"), 1)
            nc.scalar.activation(sd1, sd1, ACT.Exp)
            nc.scalar.activation(small[:, 8:16], small[:, 8:16], ACT.Exp).then_inc(sem("sd_e"), 1)
            act.wait_ge(sem("sd_mm"), 3)
            for k in range(2):
                i = nc.scalar.copy(pn1[:, 4 * k:4 * k + 4], ps[0:TS, 7 * (1 - k)].rearrange("p (b t) -> p b t", b=4))
            i.then_inc(sem("sd_pn"), 1)

        def swa_dec_dve(dve, E):
            v, ch = nc.vector, E.chain
            ch(v.memset(qbd1, 0.0))
            for g in range(G):
                half = slice(g * HD, (g + 1) * HD)
                v.tensor_copy(qbd1[half, :, g * HD:(g + 1) * HD].rearrange("p b (r t) -> p b r t", r=R1),
                              qT1[half, :, SEQ:].rearrange("p r (b t) -> p b r t", b=NB))
            dve.wait_ge(sem("sd_mm"), 1)
            for k in range(2):
                i = v.tensor_copy(kb1[:, 4 * k:4 * k + 4], ps[:, k].rearrange("p (b t) -> p b t", b=4))
            i.then_inc(sem("sd_k"), 1)
            loaded(dve, "dec1_in")
            loaded(dve, "new1_in")
            dve.wait_ge(sem("sd_mm"), 2)
            for k in range(2):
                v.tensor_tensor(sd1[:, 4 * k:4 * k + 4, 0:P], ps[:, 2 + k].rearrange("p (b t) -> p b t", b=4),
                                buf1.unsqueeze(1).to_broadcast([P, 4, P]), ALU.add)
            ch(v.tensor_tensor(sd1[:, :, P:], ps[:, 4].rearrange("p (b t) -> p b t", b=NB), new1, ALU.add))
            m, es, dn = small[:, 0:8], small[:, 8:16], small[:, 16:24]
            ch(v.tensor_reduce(m, sd1, AX_X, ALU.max))
            ch(v.tensor_scalar(m, m, sink_col[:], None, ALU.max))
            v.tensor_scalar(es, m, -1.0, sink_col[:], ALU.mult, ALU.add)
            v.tensor_tensor(sd1, sd1, m.unsqueeze(2).to_broadcast([P, NB, WIN1 + TS]), ALU.subtract)\
                .then_inc(sem("sd_s"), 1)
            dve.wait_ge(sem("sd_e"), 1)
            ch(v.tensor_reduce(dn, sd1, AX_X, ALU.add))
            ch(v.tensor_tensor(dn, dn, es, ALU.add))
            ch(v.reciprocal(dn, dn))
            v.tensor_tensor(sd1, sd1, dn.unsqueeze(2).to_broadcast([P, NB, WIN1 + TS]), ALU.mult).then_inc(sem("sd_p"), 1)
            dve.wait_ge(sem("sd_mm"), 3)
            for k in range(2):
                i = v.tensor_copy(pd1[:, 4 * k:4 * k + 4], ps[:, 5 + k].rearrange("p (b t) -> p b t", b=4))
            i.then_inc(sem("sd_pt"), 1)
            dve.wait_ge(sem("sd_mm"), 4)
            for k in range(2):
                for g in range(G):
                    half = slice(g * HD, (g + 1) * HD)
                    src = ps[half, 2 + k].rearrange("p (b g r t) -> p b g r t", b=4, g=G, r=R1)[:, :, g]
                    dst = oT1[half, :, SEQ + 32 * k:SEQ + 32 * (k + 1)].rearrange("p r (b t) -> p b r t", b=4)
                    v.tensor_copy(dst, src)

        def swa_pool(pool, E):
            store(pool, rows(d["swa_prompt"][0, 0]), kvt1[:, PT - 1])
            for b in range(NB):
                store(pool, rows(d["swa_sample"][0, b])[WIN1 - DL:], kvt1[b * DL:(b + 1) * DL, PT])

        yo = [at(kv0 + s * D_MODEL, D_MODEL, 1)[:, :, 0] for s in range(2)]

        def store_pe(pe, E):
            for i in range(NT):
                n = tile_n(i)
                if i >= 2:
                    pe.wait_ge(sem("y_half0"), i - 1)
                    pe.wait_ge(sem("y_half1"), i - 1)
                for c in range(KC):
                    mm = nc.tensor.transpose(ps[0:n, 2 * (i % 2) + c // 4, (c % 4) * P:(c % 4 + 1) * P],
                                             hT[:, c, toks(i)], ident[:])
                mm.then_inc(sem("y_tr"), 1)

        def store_copy(e, copy, which):
            for i in range(NT):
                n = tile_n(i)
                e.wait_ge(sem("y_tr"), i + 1)
                if i >= 2:
                    e.wait_ge(sem(f"y_stored{i % 2}"), 16 * (i // 2))
                copy(yo[i % 2][0:n, which * 512:(which + 1) * 512], ps[0:n, 2 * (i % 2) + which])\
                    .then_inc(sem(f"y_half{which}"), 1)

        def store_sp(sp):
            for i in range(NT):
                sp.wait_ge(sem("y_half0"), i + 1)
                sp.wait_ge(sem("y_half1"), i + 1)
                dst = d["y_prompt"][0, toks(i)] if i < PT else d["y_sample"].rearrange("b t n -> (b t) n")
                sp.dma_start(dst, yo[i % 2][0:tile_n(i)]).then_inc(sem(f"y_stored{i % 2}"), 16)

        def x_of(c):
            return xT[:, c]

        def h_of(c):
            return hT[:, c]

        def z_of(c):
            return zT[:, c]

        NORMS = {"norm_mix0": (KC, x_of, h_of, gain("mix", 0), D_MODEL), "ssm_norm": (4, z_of, z_of, gain("ssm"), SX),
                 "norm_ffn0": (KC, x_of, h_of, gain("ffn", 0), D_MODEL), "norm_mix1": (KC, x_of, h_of, gain("mix", 1), D_MODEL),
                 "norm_ffn1": (KC, x_of, h_of, gain("ffn", 1), D_MODEL), "norm_fin": (KC, x_of, h_of, gain("final"), D_MODEL)}

        @block.tensor
        def _(pe):
            E = Engine(pe, nc.tensor, "pe")
            residual = {"out0": lambda k: oN[:, k] if k < R0 else zT[:, k - R0], "out1": lambda k: oT1[:, k]}
            body = {"setup": setup_pe, "cache": cache_pe, "load": load_pe, "proj0": proj0_pe, "prep": prep_pe,
                    "ssm": ssm_pe, "cmp": cmp_pe, "attn": attn_pe, "dec": dec_pe, "up0": up_pe, "down0": down_pe,
                    "proj1": proj1_pe, "swa": swa_pe, "swa_dec": swa_dec_pe, "up1": up_pe, "down1": down_pe,
                    "store": store_pe}
            for name in STAGES:
                if name in NORMS:
                    norm_pe(pe, E, NORMS[name][0])
                elif name in residual:
                    residual_pe(pe, E, residual[name])
                elif name in body:
                    body[name](pe, E)
                E.end_stage(name)

        @block.scalar
        def _(act):
            E = Engine(act, nc.scalar, "act")
            body = {"setup": setup_act, "cache": cache_act, "load": load_act, "proj0": proj0_act, "prep": prep_act,
                    "conv": conv_act, "ssm": ssm_act, "cmp": cmp_act, "attn": attn_act, "dec": dec_act,
                    "up0": up_act, "up1": up_act, "swa": swa_act, "swa_dec": swa_dec_act,
                    "proj1": lambda e, E: proj1_out(E, nc.scalar, 0, nc.scalar.mul, nc.scalar.copy),
                    "store": lambda e, E: store_copy(e, nc.scalar.copy, 1)}
            for name in STAGES:
                if name in NORMS:
                    n, src, _, _, width = NORMS[name]
                    norm_act(act, E, n, src, width)
                elif name in ("out0", "out1", "down0", "down1"):
                    skip_units(E, 4)
                elif name in body:
                    body[name](act, E)
                E.end_stage(name)

        @block.vector
        def _(dve):
            E = Engine(dve, nc.vector, "dve")
            body = {"setup": setup_dve, "cache": cache_dve, "load": load_dve, "proj0": proj0_dve, "prep": prep_dve,
                    "conv": conv_dve, "ssm": ssm_dve, "cmp": cmp_dve, "attn": attn_dve, "dec": dec_dve,
                    "up0": up_dve, "up1": up_dve, "swa": swa_dve, "swa_dec": swa_dec_dve,
                    "proj1": lambda e, E: proj1_out(E, nc.vector, 1, nc.vector.tensor_scalar_mul, nc.vector.tensor_copy),
                    "store": lambda e, E: store_copy(e, nc.vector.tensor_copy, 0)}
            for name in STAGES:
                if name in NORMS:
                    n, src, dst, g0, _ = NORMS[name]
                    norm_dve(dve, E, n, src, dst, g0)
                elif name in ("out0", "out1", "down0", "down1"):
                    residual_dve(dve, E)
                elif name in body:
                    body[name](dve, E)
                E.end_stage(name)

        @block.gpsimd
        def _(pool):
            E = Engine(pool, nc.gpsimd, "pool")
            body = {"cache": cache_pool, "prep": prep_pool, "ssm": ssm_pool, "cmp": cmp_pool, "swa": swa_pool}
            for name in STAGES:
                if name in body:
                    body[name](pool, E)
                if name == "attn":
                    pool.wait_ge(stored, 16 * stores[0])
                E.end_stage(name)
            pool.wait_ge(stored, 16 * stores[0])

        @block.sync
        def _(sp):
            sent = [0]

            def weights(upto):
                while sent[0] < upto:
                    n = sent[0]
                    if n >= SLOTS:
                        sp.wait_ge(*panel_done[n - SLOTS])
                    for dst, src in panels[n](wp[n % SLOTS]):
                        sp.dma_start(dst, src).then_inc(w_ready[n % SLOTS], 16)
                    sent[0] += 1

            load(sp, "setup_in")
            load(sp, "table_in")
            loaded(sp, "table_in")
            cache_sp(sp)
            weights(SLOTS)
            load_sp(sp)
            weights(13)
            load(sp, "prep_in", "proj0")
            weights(13 + SLOTS)
            load(sp, "ssm_in", "prep")
            load(sp, "ssm_state_in", "conv")
            cmp_sp(sp)
            load(sp, "bias_in", "cmp")
            dec_sp(sp)
            n = 13 + 4 + 22 + 12
            weights(n)
            weights(n + 5)
            load(sp, "bias1_in", "norm_mix1")
            weights(n + 5 + SLOTS)
            load(sp, "dec1_in", "proj1")
            load(sp, "new1_in", "swa")
            weights(len(panels))
            store_sp(sp)
            sp.wait_ge(sem("y_stored0"), 16 * (PT // 2 + 1))
            sp.wait_ge(sem("y_stored1"), 16 * (PT // 2))
            sp.wait_ge(sem("conv_stored"), 32)
            sp.wait_ge(sem("ssm_fin_stored"), 16)
            sp.wait_ge(sem("s0_stored"), 16 * NB)


def kernel(**inputs):
    import concourse.bacc as bacc
    from concourse.bass_utils import run_bass_kernel_spmd as run

    nc = bacc.Bacc("TRN2", target_bir_lowering=False, num_devices=1)
    arrays, d, const = {}, {}, {}
    for name in INPUTS:
        a = np.ascontiguousarray(inputs[name])
        arrays[f"in_{name}"] = a
        d[name] = nc.dram_tensor(f"in_{name}", a.shape, mybir.dt.from_np(a.dtype), kind="ExternalInput").ap()
    for name, a in constants().items():
        arrays[f"const_{name}"] = a
        const[name] = nc.dram_tensor(f"const_{name}", a.shape, mybir.dt.from_np(a.dtype), kind="ExternalInput").ap()
    for name, shape in OUTPUTS:
        d[name] = nc.dram_tensor(f"out_{name}", shape, F32, kind="ExternalOutput").ap()
    build(nc, d, const)
    got = run(nc, [arrays], core_ids=[0]).results[0]
    return tuple(got[f"out_{name}"] for name, _ in OUTPUTS)
```

```python
from contextlib import ExitStack

import numpy as np

import concourse.bass as bass
from concourse import mybir

F32 = mybir.dt.float32
F32R = mybir.dt.float32r
I32 = mybir.dt.int32
ALU = mybir.AluOpType
ACT = mybir.ActivationFunctionType
AX_X = mybir.AxisListType.X

P = 128
HALF = 64
D_MODEL = 1024
KC = D_MODEL // P
SEQ = 1024
NB = 8
DL = 8
TS = NB * DL
T = SEQ + TS
PT = SEQ // P
NT = PT + 1
PAST = 2048
PAGE = 128
NPAGE = PAST // PAGE
ALLPAGES = NB * NPAGE
HD = 64
G = 2
R0 = 4
R1 = 8
BLK = 64
NCB = PAST // BLK
PCB = SEQ // BLK
TOPK = 16
WIN0 = 512
WIN1 = 128
SH = 8
SN = 128
SX = 512
XC = 8
CONV = 4
FFN = 2816
FC = FFN // P
FG = 4
FGROUPS = [(f, min(f + FG, FC)) for f in range(0, FC, FG)]
EPS = 1e-6
NEG = -1.0e30
FLOOR = -1.0e25
SPLIT = ((0, 368), (368, 736), (736, T))
WCOL = 256
SLOTS = 3
KVW = 3 * 256
KVG = KVW + 24
COL_KV = 512
COL_Z = COL_KV + KVG
COL_X = COL_Z + SX
COL_DT = COL_X + 1024
XPAD = CONV - 1
XS0 = XPAD + SEQ
XW = XS0 + NB * (XPAD + DL)
ARENA = 48304
LD = 8

STAGES = ["setup", "cache", "load", "proj0", "prep", "conv", "ssm", "cmp", "attn", "dec", "out0", "ffn0",
          "proj1", "swa", "swa_dec", "out1", "ffn1", "store"]
END = {name: 4 * (n + 1) for n, name in enumerate(STAGES)}


def slopes(n):
    return 2.0 ** (-8.0 * np.arange(1, n + 1) / n)


def constants():
    f = np.float32
    c = {}
    p = np.arange(P)
    c["ident"] = np.eye(P)
    s0, s1 = slopes(G * R0), slopes(G * R1)
    rel = np.arange(SEQ) - (SEQ - P)
    dist = p[:, None] - rel[None, :]
    c["bias_slc"] = np.stack([np.where(dist >= 0, -s0[g * R0] * dist, NEG) for g in range(G)], 1)
    dw = dist[:, SEQ - WIN0 - P:]
    c["bias_win"] = np.stack([np.where((dw >= 0) & (dw <= WIN0), -s0[g * R0] * dw, NEG) for g in range(G)], 1)
    d1 = dist[:, SEQ - 2 * P:]
    c["bias_swa"] = np.stack([np.where((d1 >= 0) & (d1 <= WIN1), -s1[g * R1 + r] * d1, NEG)
                              for r in range(R1) for g in range(G)], 1)
    tc = np.arange(PT)[None, :, None] * P + p[:, None, None] - ((np.arange(PCB) + 1) * BLK - 1)[None, None]
    c["bias_cmp"] = np.stack([np.where(tc >= 0, -s0[g * R0 + r] * tc, NEG)
                              for r in range(R0) for g in range(G)], 2)
    hh = p // PCB
    c["cmp_diag"] = (hh[:, None] == np.arange(SX)[None, :] // HD) * 1.0
    b2, g, r, t = p // 64, p // 32 % 2, p // 8 % 4, p % 8
    sl = s0[g * R0 + r]
    c["dec_off"] = sl[:, None] * np.arange(BLK)[None]
    c["dec_blk"] = -sl[:, None] * (PAST + t[:, None] - BLK * np.arange(NCB)[None])
    dw = WIN0 + t[:, None] - np.arange(WIN0)[None]
    c["dec_win"] = np.where(dw <= WIN0, -sl[:, None] * dw, NEG)
    c["dec_cmp"] = -sl[:, None] * (PAST + t[:, None] - ((np.arange(NCB) + 1) * BLK - 1)[None])
    j = np.arange(TS)
    bp = np.arange(NB // 2)
    own = (j // DL)[None, None] == (2 * bp[None, :, None] + b2[:, None, None])
    dn = t[:, None, None] - (j % DL)[None, None]
    c["dec_new"] = np.where(own & (dn >= 0), -sl[:, None, None] * dn, NEG)
    q = 64 * b2 + 32 * g + t
    c["over_heads"] = (q[:, None] == q[None, :]) * 1.0
    c["earlier"] = np.broadcast_to(np.arange(NCB)[None, :] < np.arange(NCB)[:, None], (P, NCB, NCB)) * 1.0
    c["tok_rows"] = ((j[:, None, None]) == (DL * (2 * bp[None, :, None] + b2[None, None]) + t[None, None])) * 1.0
    c["gate_pick"] = ((np.arange(G * R0)[None, :] == (g * R0 + r)[:, None])[:, :, None] * np.ones(3)).reshape(P, 24)
    g1, r1 = p // 64, p // 8 % 8
    sl1 = s1[g1 * R1 + r1]
    dw = WIN1 + t[:, None] - np.arange(WIN1)[None]
    c["swa_buf"] = np.where(dw <= WIN1, -sl1[:, None] * dw, NEG)
    own = (j // DL)[None, None] == np.arange(NB)[None, :, None]
    dn = t[:, None, None] - (j % DL)[None, None]
    c["swa_new"] = np.where(own & (dn >= 0), -sl1[:, None, None] * dn, NEG)
    c["causal"] = (p[:, None] <= p[None, :]) * 1.0
    c["causal8"] = ((j[:, None] <= j[None, :]) & (j[:, None] // DL == j[None, :] // DL)) * 1.0
    c["own_seq"] = (j[:, None] // DL == np.arange(NB)[None, :]) * 1.0
    h = np.arange(SH)
    c["head_rows"] = ((h[:, None, None] == h[None, :, None]) * np.ones(P)).reshape(SH, SH * P)
    c["pair_rows"] = ((h[:, None, None] == 2 * np.arange(SH // 2)[None, :, None] + (p // HALF)[None, None]) * 1.0)
    c["last_tok"] = (j[:, None] == (j[None, :] // DL) * DL + DL - 1) * 1.0
    tt = np.arange(T)
    keep = np.where(tt < SEQ, tt % P != 0, tt % DL != 0)
    c["keep"] = np.broadcast_to(keep, (SH, T)) * 1.0
    return {k: np.ascontiguousarray(v.astype(f)) for k, v in c.items()}


INPUTS = ["x_prompt", "x_sample", "cache_nsa_cmp_kv", "cache_nsa_slc_kv", "state_nsa_win_kv", "state_ssm",
          "state_ssm_conv", "state_swa_kv", "page_table", "norm_mix", "norm_ffn", "norm_final", "w_in_even",
          "w_out_even", "cmp_pe_k", "cmp_w1_k", "cmp_w2_k", "cmp_pe_v", "cmp_w1_v", "cmp_w2_v", "ssm_conv_w",
          "ssm_conv_b", "ssm_dt_bias", "ssm_a_log", "ssm_d", "ssm_norm", "w_in_odd", "w_out_odd", "swa_sinks",
          "w_gate_up", "w_down"]
KV = (2, G, HD)
OUTPUTS = [("y_prompt", (1, SEQ, D_MODEL)), ("y_sample", (NB, DL, D_MODEL)),
           ("cmp_prompt", (1, 1, SEQ) + KV), ("slc_prompt", (1, 1, SEQ) + KV), ("win_prompt", (1, 1, WIN0) + KV),
           ("ssm_prompt", (1, 1, SH, HD, SN)), ("conv_prompt", (1, 1, XPAD, 1024)),
           ("swa_prompt", (1, 1, WIN1) + KV),
           ("cmp_sample", (1, NB, DL) + KV), ("slc_sample", (1, NB, DL) + KV), ("win_sample", (1, NB, WIN0) + KV),
           ("ssm_sample", (1, NB, SH, HD, SN)), ("conv_sample", (1, NB, XPAD, 1024)),
           ("swa_sample", (1, NB, WIN1) + KV)]


class Chain:

    def __init__(self, engine, sem):
        self.engine, self.sem, self.n = engine, sem, 0

    def __call__(self, instruction):
        self.n += 1
        instruction.then_inc(self.sem, 1)
        self.engine.wait_ge(self.sem, self.n)


def build(nc, d, const):
    ctx = ExitStack()
    with ctx:
        def sb(name, shape, dt=F32):
            return ctx.enter_context(nc.sbuf_tensor(name, shape, dt))

        sems = {}

        def sem(name):
            if name not in sems:
                sems[name] = ctx.enter_context(nc.semaphore(name))
            return sems[name]

        x0, h0, kv0, q0, z0, b0, w0 = 0, 8704, 17408, 24536, 28888, 33240, 42160
        f0 = h0 + 2 * KC * T
        wh0 = f0 + 2 * FG * T
        with ExitStack() as alias:
            def part(name, n):
                return alias.enter_context(nc.sbuf_tensor(name, [P, n], F32R))

            part("below_h", h0)
            h_hi = [part(f"h_hi{k}", T) for k in range(KC)]
            h_lo = [part(f"h_lo{k}", T) for k in range(KC)]
            a_hi = [part(f"a_hi{k}", T) for k in range(FG)]
            a_lo = [part(f"a_lo{k}", T) for k in range(FG)]
            w_hi = [part(f"w_hi{s}", KC * WCOL) for s in range(SLOTS)]
            part("below_w", w0 - wh0 - SLOTS * KC * WCOL)
            w_lo = [part(f"w_lo{s}", KC * WCOL) for s in range(SLOTS)]

        arena = sb("arena", [P, ARENA])

        def at(start, *shape, parts=P):
            size = int(np.prod(shape))
            v = arena[0:parts, start:start + size]
            if len(shape) == 2:
                v = v.rearrange("p (a b) -> p a b", a=shape[0])
            if len(shape) == 3:
                v = v.rearrange("p (a b c) -> p a b c", a=shape[0], b=shape[1])
            if len(shape) == 4:
                v = v.rearrange("p (a b c e) -> p a b c e", a=shape[0], b=shape[1], c=shape[2])
            return v

        xT = at(x0, KC, T)
        hT = at(h0, KC, T)
        kvt = at(kv0, NT, KVG)
        qT = at(q0, R0, T)
        zT = at(z0, R0, T)
        xbc = at(b0, XC, XW)
        xc = at(h0, XC, T)
        oN = at(b0, R0, T)
        wp = [at(w0 + s * KC * WCOL, KC, WCOL) for s in range(SLOTS)]
        h_raw = at(h0 + KC * T, KC, T)
        a_raw = at(f0 + FG * T, FG, T)
        qT1 = at(b0, R1, T)
        kvt1 = at(kv0, NT, 256)
        kT1 = at(q0, 1, T)[:, 0]

        ident = sb("ident", [P, P])
        ones = sb("ones", [P, P])
        cols = sb("cols", [P, 84])
        row24 = sb("row24", [1, 24])
        eps_c = sb("eps_c", [P, 1])
        kcT = sb("kcT", [P, NB * NCB])
        vc = sb("vc", [NCB, NB, P])
        w2 = sb("w2", [P, 2, HD])
        peb = sb("peb", [P, 2])
        cst = sb("cst", [P, 2 * 368])
        rstd = sb("rstd", [P, 3, 368])
        gates = sb("gates", [P, NT, 24])
        sinks = sb("sinks", [P, R1, G])
        sink_col = sb("sink_col", [P, 1])
        qbd = sb("qbd", [P, NB, 64])
        head_c = sb("head_c", [SH, 4])
        d_col = sb("d_col", [P, 4])
        table = sb("table", [1, ALLPAGES], I32)
        dtok = sb("dtok", [P, NT, 16])
        small = sb("small", [P, 64])
        ps = ctx.enter_context(nc.psum_tensor("ps", [P, 8, 512], F32))

        stage_end = sem("stage_end")
        w_split = sem("w_split")
        w_ready = [sem(f"w_ready{s}") for s in range(SLOTS)]
        panel_done = []
        unit_ready = [sem("unit_ready0"), sem("unit_ready1")]
        unit_free = [sem("unit_free0"), sem("unit_free1")]
        stored = sem("stored")
        consts_in = sem("consts_in")

        w_in0 = d["w_in_even"][0].rearrange("(c p) n -> p c n", p=P)
        w_in1 = d["w_in_odd"][0].rearrange("(c p) n -> p c n", p=P)
        w_gu = [d["w_gate_up"][l].rearrange("(c p) n -> p c n", p=P) for l in range(2)]
        w_dn = [d["w_down"][l].rearrange("(c p) n -> p c n", p=P) for l in range(2)]
        cmp_pages = d["cache_nsa_cmp_kv"][0].rearrange("n p a g e -> n p (a g e)")
        slc_pages = d["cache_nsa_slc_kv"][0].rearrange("n p a g e -> n p (a g e)")

        panels = []
        for m in range(4):
            n = min(WCOL, KVG - m * WCOL)
            panels.append(lambda w, m=m, n=n: [(w[:, :, 0:n], w_in0[:, :, COL_KV + m * WCOL:COL_KV + m * WCOL + n])])

        def query_panel(src, heads, rp):
            def pieces(w):
                out = []
                for r in range(2):
                    for g in range(G):
                        c = (g * heads + 2 * rp + r) * HD
                        out.append((w[:, :, r * P + g * HD:r * P + g * HD + HD], src[:, :, c:c + HD]))
                return out
            return pieces

        for rp in range(2):
            panels.append(query_panel(w_in0, R0, rp))
        for m in range(6):
            c = (COL_Z + m * WCOL)
            panels.append(lambda w, c=c: [(w[:, :, :], w_in0[:, :, c:c + WCOL])])
        panels.append(lambda w: [(w[:, :, 0:SH], w_in0[:, :, COL_DT:COL_DT + SH])])

        PROJ0 = len(panels)

        def out_panel0(m):
            src = d["w_out_even"][0]
            def pieces(w):
                n = slice(m * WCOL, (m + 1) * WCOL)
                out = [(w[g * HD:(g + 1) * HD, 0:R0, :],
                        src[g * 256:(g + 1) * 256, n].rearrange("(r e) n -> e r n", e=HD)) for g in range(G)]
                return out + [(w[:, R0:, :], src[512:1024, n].rearrange("(c p) n -> p c n", p=P))]
            return pieces

        def out_panel1(m):
            src = d["w_out_odd"][0]
            def pieces(w):
                n = slice(m * WCOL, (m + 1) * WCOL)
                return [(w[g * HD:(g + 1) * HD, :, :],
                         src[g * 512:(g + 1) * 512, n].rearrange("(r e) n -> e r n", e=HD)) for g in range(G)]
            return pieces

        def down_cols(f, e):
            return KC * WCOL // (e - f)

        def ffn_panels(l):
            for f, e in FGROUPS:
                for k in range(f, e):
                    panels.append(lambda w, k=k: [(w[:, :, s * P:(s + 1) * P],
                                                   w_gu[l][:, :, s * FFN + k * P:s * FFN + (k + 1) * P]) for s in range(2)])
                n = down_cols(f, e)
                for c in range(0, D_MODEL, n):
                    panels.append(lambda w, f=f, e=e, c=c, n=n: [
                        (w.rearrange("p a b -> p (a b)").rearrange("p (k n) -> p k n", n=n), w_dn[l][:, f:e, c:c + n])])

        for m in range(4):
            panels.append(out_panel0(m))
        ffn_panels(0)
        panels.append(lambda w: [(w[:, :, :], w_in1[:, :, 1024:1280])])
        for rp in range(4):
            panels.append(query_panel(w_in1, R1, rp))
        for m in range(4):
            panels.append(out_panel1(m))
        ffn_panels(1)
        w_count = []
        total = [0] * SLOTS
        for n, p in enumerate(panels):
            total[n % SLOTS] += 16 * len(p(wp[0]))
            w_count.append(total[n % SLOTS])

        class Engine:

            def __init__(self, e, ns, chain):
                self.e, self.ns, self.stage, self.panel, self.seen = e, ns, 0, 0, [0, 0]
                self.chain = Chain(e, sem(f"chain_{chain}"))
                self.count = {}

            def end_stage(self, name):
                assert STAGES[self.stage] == name, name
                self.stage += 1
                self.ns.drain().then_inc(stage_end, 1)
                self.e.wait_ge(stage_end, 4 * self.stage)

            def after(self, name, n=1):
                v = self.count.get(name, 0)
                self.count[name] = v + n
                return v

            def next_panel(self):
                n = self.panel
                self.panel += 1
                self.e.wait_ge(w_ready[n % SLOTS], w_count[n])
                return wp[n % SLOTS]

            def free_panel(self, semaphore, value):
                panel_done.append((semaphore, value))

            def unit_start(self, s):
                if self.seen[s]:
                    self.e.wait_ge(unit_free[s], self.seen[s])
                self.seen[s] += 1

            def pass_unit(self, s, n=1):
                self.seen[s] += n

            def unit_wait(self, s):
                self.seen[s] += 1
                self.e.wait_ge(unit_ready[s], self.seen[s])

        def f32(x):
            return x.bitcast(F32)

        def gain(kind, l=0):
            return {"mix": KC * l, "ffn": 2 * KC + KC * l, "final": 4 * KC, "ssm": 5 * KC}[kind]

        CONV_W, CONV_B = 44, 76

        CP = ALLPAGES + 1
        EH = BLK // 2
        xg = at(0, CP, 256)
        w1b = [at(CP * 256 + s * EH * P, EH, P) for s in range(2)]
        hid = at(CP * 256 + 2 * EH * P, 2, ALLPAGES * G)
        vcT = at(CP * 256 + 2 * EH * P + 2 * ALLPAGES * G, 1, NB * NCB)[:, 0]
        xin = [at(kv0 + s * D_MODEL, D_MODEL, 1)[:, :, 0] for s in range(2)]
        dtraw = rstd[0:SH].rearrange("p a b -> p (a b)")[:, 0:T]
        acum = dtraw
        hv = [at(h0 + i * T, 1, T, parts=SH)[:, 0] for i in range(6)]
        conv_in = at(h0 + 6 * T, 1, 1024, parts=NB * XPAD)[:, 0]
        conv_out = at(h0 + 7 * T, 1, 1024, parts=(NB + 1) * XPAD)[:, 0]
        rows84 = at(w0, 1, P, parts=84)[:, 0]
        sinkx = at(w0 + P, 1, P, parts=1)[:, 0]
        causal, causal8 = cst[:, 0:128], cst[0:TS, 128:192]
        own_seq, last_tok = cst[0:TS, 192:200], cst[0:TS, 200:264]
        m_st = at(b0 + 3584, SH, HD)
        m_seg, m_eac, m_cb, m_xdt, m_xw, m_bt = ([at(s + o, *shape) for s in (b0, w0)] for o, shape in (
            (0, (SH, P)), (1024, (SH, P)), (2048, (G, P)), (2304, (SH, HD)), (2816, (SH, HD)), (3328, (G, P))))
        m_de = [small[:, 8 * k:8 * k + 8] for k in range(2)]
        m_all = [small[:, 16 + 8 * k:24 + 8 * k] for k in range(2)]
        s0_in = at(b0 + 4096, NB, 4, SN)
        s0t = at(b0 + 8192, 1, 512)[:, 0]
        m_bd = [at(b0 + g * 1024, NB, SN, parts=TS) for g in range(G)]
        conv_pack = cst[:, 264:264 + XC * 27].rearrange("p (c k) -> p c k", c=XC)
        free_b = b0 + R0 * T

        loads = {
            "setup_in": [(ident[:], const["ident"]),
                         (rows84[0:16], d["norm_mix"].rearrange("l (c p) -> (l c) p", p=P)),
                         (rows84[16:32], d["norm_ffn"].rearrange("l (c p) -> (l c) p", p=P)),
                         (rows84[32:40], d["norm_final"].rearrange("(c p) -> c p", p=P)),
                         (rows84[40:44], d["ssm_norm"][0].rearrange("(c p) -> c p", p=P)),
                         (rows84[44:76], d["ssm_conv_w"][0].rearrange("k (c p) -> (k c) p", p=P)),
                         (rows84[76:84], d["ssm_conv_b"][0].rearrange("(c p) -> c p", p=P)),
                         (row24[0:1, 0:16], d["swa_sinks"]), (row24[0:1, 16:24], d["ssm_d"]),
                         (head_c[:, 0:1], d["ssm_dt_bias"][0].rearrange("(h a) -> h a", a=1)),
                         (head_c[:, 1:2], d["ssm_a_log"][0].rearrange("(h a) -> h a", a=1)),
                         (w2[0:HD, 0], d["cmp_w2_k"][0]), (w2[HD:, 0], d["cmp_w2_k"][0]),
                         (w2[0:HD, 1], d["cmp_w2_v"][0]), (w2[HD:, 1], d["cmp_w2_v"][0])],
            "table_in": [(table[:], d["page_table"].rearrange("b n -> (b n)").rearrange("(a n) -> a n", a=1))],
        }
        block = ctx.enter_context(nc.Block())

        def load(e, name, after=None):
            if after:
                e.wait_ge(stage_end, END[after])
            for dst, src in loads[name]:
                e.dma_start(dst, src).then_inc(sem(name), 16)

        def loaded(e, name):
            e.wait_ge(sem(name), 16 * len(loads[name]))

        def setup_pe(pe, E):
            loaded(pe, "setup_in")
            pe.wait_ge(sem("ones_set"), 1)
            nc.tensor.transpose(ps[:, 0, 0:84], rows84, ident[0:84, 0:84])
            nc.tensor.matmul(ps[:, 0, 128:152], ones[0:1, :], row24[0:1, :], start=True, stop=True)\
                .then_inc(sem("setup_mm"), 1)
            pe.wait_ge(sem("sinkx_set"), 1)
            nc.tensor.matmul(ps[:, 1, 0:1], sinkx, ones[0:1, 0:1], start=True, stop=True)\
                .then_inc(sem("setup_mm"), 1)

        def setup_dve(dve, E):
            nc.vector.memset(ones[:], 1.0).then_inc(sem("ones_set"), 1)
            nc.vector.memset(eps_c[:], EPS)
            loaded(dve, "setup_in")
            nc.vector.tensor_copy(sinkx.rearrange("p (h t) -> p h t", t=DL),
                                  row24[0:1, 0:16].unsqueeze(2).to_broadcast([1, 16, DL])).then_inc(sem("sinkx_set"), 1)
            dve.wait_ge(sem("setup_mm"), 2)
            nc.vector.tensor_copy(cols[:], ps[:, 0, 0:84])
            nc.vector.tensor_copy(sinks[:], ps[:, 0, 128:144].rearrange("p (g r) -> p r g", g=G))
            for h2 in range(2):
                half = slice(h2 * HD, (h2 + 1) * HD)
                nc.vector.tensor_copy(d_col[half, :], ps[half, 0, 144 + h2:152:2])
            nc.vector.tensor_copy(sink_col[:], ps[:, 1, 0:1])

        def setup_act(act, E):
            loaded(act, "setup_in")
            E.chain(nc.scalar.activation(head_c[:, 2:3], head_c[:, 1:2], ACT.Exp))
            nc.scalar.mul(head_c[:, 2:3], head_c[:, 2:3], -1.0)

        def page_loads(e, pool_view, slot, first, semaphore):
            pages = [e.value_load(table[0:1, first + i:first + i + 1], min_val=0, max_val=159) for i in range(LD)]
            for i, page in enumerate(pages):
                e.dma_start(slot(i), pool_view[bass.ds(page, 1)].rearrange("a p n -> p (a n)")).then_inc(semaphore, 16)

        def cache_pages(e, which):
            for first in range(which * LD, ALLPAGES, 2 * LD):
                page_loads(e, cmp_pages, lambda i: xg[:, first + i], first, sem(f"pages_in{which}"))

        def cache_sp(sp):
            sp.wait_ge(sem("w1_zero"), 2)
            for kv, pe_ in enumerate(("cmp_pe_k", "cmp_pe_v")):
                for b in range(2):
                    for g in range(G):
                        sp.dma_start(xg[b * BLK:(b + 1) * BLK, ALLPAGES, kv * P + g * HD:kv * P + (g + 1) * HD], d[pe_][0])\
                            .then_inc(sem("pe_in"), 16)
            cache_pages(sp, 0)
            for q in range(4):
                if q >= 2:
                    sp.wait_ge(sem("w1_used"), q - 1)
                w = d[("cmp_w1_k", "cmp_w1_v")[q // 2]][0][:, (q % 2) * EH:(q % 2 + 1) * EH]
                for b in range(2):
                    sp.dma_start(w1b[q % 2][b * BLK:(b + 1) * BLK, :, b * HD:(b + 1) * HD], w)\
                        .then_inc(sem(f"w1_in{q % 2}"), 16)

        def cache_pool(pool, E):
            for w in w1b:
                nc.gpsimd.memset(w, 0.0).then_inc(sem("w1_zero"), 1)

        def cache_pe(pe, E):
            pe.wait_ge(sem("pe_in"), 16 * 8)
            for which in range(2):
                pe.wait_ge(sem(f"pages_in{which}"), 16 * ALLPAGES // 2)
            for q in range(4):
                pe.wait_ge(sem(f"w1_in{q % 2}"), 32 * (q // 2 + 1))
                for e in range(EH):
                    c = q // 2 * P + q % 2 * EH + e
                    mm = nc.tensor.matmul(ps[:, q // 2, 0:CP * G], w1b[q % 2][:, e, :], xg[:, :, c:c // P * P + P:HD],
                                          start=q % 2 == 0 and e == 0, stop=q % 2 == 1 and e == EH - 1)
                mm.then_inc(sem("w1_used"), 1)
            pe.wait_ge(sem("hid_out"), 2)
            for kv in range(2):
                for b in range(2):
                    for g in range(G):
                        half = slice(b * HD, (b + 1) * HD)
                        rhs = hid[half, kv].rearrange("p (n g) -> p n g", g=G)[:, :, g]
                        mm = nc.tensor.matmul(ps[g * HD:(g + 1) * HD, 4 + 2 * kv + b, 0:ALLPAGES], w2[half, kv], rhs,
                                              start=True, stop=True)
            mm.then_inc(sem("blocks_mm"), 1)
            pe.wait_ge(sem("blocks_out"), 1)
            for b in range(NB):
                mm = nc.tensor.transpose(ps[0:NCB, b // 4, (b % 4) * P:(b % 4 + 1) * P], vcT[:, b * NCB:(b + 1) * NCB],
                                         ident[:])
            mm.then_inc(sem("blocks_mm"), 1)

        def cache_act(act, E):
            loaded(act, "table_in")
            cache_pages(act, 1)
            for kv in range(2):
                act.wait_ge(sem("w1_used"), 2 * kv + 2)
                E.chain(nc.scalar.copy(peb[:, kv:kv + 1], ps[:, kv, ALLPAGES * G:ALLPAGES * G + 1]))
                nc.scalar.activation(hid[:, kv], ps[:, kv, 0:ALLPAGES * G], ACT.Gelu_apprx_tanh, bias=peb[:, kv:kv + 1])\
                    .then_inc(sem("hid_out"), 1)

        def cache_dve(dve, E):
            dve.wait_ge(sem("blocks_mm"), 1)
            for b in range(2):
                nc.vector.tensor_copy(kcT[:].rearrange("p (n b) -> p n b", b=2)[:, :, b], ps[:, 4 + b, 0:ALLPAGES])
                mm = nc.vector.tensor_copy(vcT.rearrange("p (n b) -> p n b", b=2)[:, :, b], ps[:, 6 + b, 0:ALLPAGES])
            mm.then_inc(sem("blocks_out"), 1)
            dve.wait_ge(sem("blocks_mm"), 2)
            for h in range(2):
                nc.vector.tensor_copy(vc[:, 4 * h:4 * h + 4, :], ps[0:NCB, h].rearrange("p (b c) -> p b c", b=4))

        def tile_n(i):
            return P if i < PT else TS

        def load_sp(sp):
            sp.wait_ge(stage_end, END["cache"])
            for i in range(NT):
                if i >= 2:
                    sp.wait_ge(sem("x_used"), i - 1)
                src = d["x_prompt"][0, i * P:(i + 1) * P] if i < PT else d["x_sample"].rearrange("b t n -> (b t) n")
                sp.dma_start(xin[i % 2][0:tile_n(i)], src).then_inc(sem(f"x_in{i % 2}"), 16)

        def load_pe(pe, E):
            for i in range(NT):
                n = tile_n(i)
                pe.wait_ge(sem(f"x_in{i % 2}"), 16 * (i // 2 + 1))
                if i >= 2:
                    pe.wait_ge(sem("x_copied"), i - 1)
                    pe.wait_ge(sem("x_copied_a"), i - 1)
                for c in range(KC):
                    mm = nc.tensor.transpose(ps[:, 2 * (i % 2) + c // 4, (c % 4) * n:(c % 4 + 1) * n],
                                             xin[i % 2][0:n, c * P:(c + 1) * P], ident[0:n, 0:n])
                mm.then_inc(sem("x_used"), 1)

        def load_dve(dve, E):
            for i in range(NT):
                n = tile_n(i)
                dve.wait_ge(sem("x_used"), i + 1)
                nc.vector.tensor_copy(xT[:, 0:4, i * P:i * P + n],
                                      ps[:, 2 * (i % 2), 0:4 * n].rearrange("p (c t) -> p c t", c=4))\
                    .then_inc(sem("x_copied"), 1)

        def load_act(act, E):
            for i in range(NT):
                n = tile_n(i)
                act.wait_ge(sem("x_used"), i + 1)
                nc.scalar.copy(xT[:, 4:8, i * P:i * P + n],
                               ps[:, 2 * (i % 2) + 1, 0:4 * n].rearrange("p (c t) -> p c t", c=4))\
                    .then_inc(sem("x_copied_a"), 1)

        rs_flat = rstd[:].rearrange("p a b -> p (a b)")[:, 0:T]

        def norm_pe(pe, E, N):
            for c in range(0, N["n"], 2):
                pe.wait_ge(sem("norm_pair"), E.after("norm_pair") + 1)
                for s, (a, b) in enumerate(SPLIT):
                    mm = nc.tensor.matmul(ps[:, s, 0:b - a], ones[:], N["sq"](c + 1)[:, a:b],
                                          start=c == 0, stop=c == N["n"] - 2)
            mm.then_inc(sem("norm_mm"), 1)
            E.normed = E.after("norm_done", N["n"])

        def norm_act(act, E, N):
            for c in range(N["n"]):
                nc.scalar.activation(N["sq"](c), N["src"](c), ACT.Square).then_inc(sem("norm_sq"), 1)
            act.wait_ge(sem("norm_mm"), E.after("norm_mm") + 1)
            for s, (a, b) in enumerate(SPLIT):
                i = nc.scalar.activation(rs_flat[:, a:b], ps[:, s, 0:b - a], ACT.Ln, scale=1.0 / N["width"], bias=eps_c[:])
            E.chain(i)
            nc.scalar.activation(rs_flat, rs_flat, ACT.Exp, scale=-0.5).then_inc(sem("norm_rstd"), 1)
            if N["split"]:
                for c in range(N["n"]):
                    act.wait_ge(sem("norm_raw"), E.after("norm_raw") + 1)
                    nc.scalar.copy(h_hi[c][:], h_raw[:, c]).then_inc(sem("norm_hi"), 1)

        def norm_dve(dve, E, N):
            v = nc.vector
            for c in range(1, N["n"], 2):
                dve.wait_ge(sem("norm_sq"), E.after("norm_sq", 2) + 2)
                v.tensor_tensor(N["sq"](c), N["sq"](c), N["sq"](c - 1), ALU.add).then_inc(sem("norm_pair"), 1)
            dve.wait_ge(sem("norm_rstd"), E.after("norm_rstd") + 1)
            for c in range(N["n"] + 1):
                if c < N["n"]:
                    v.scalar_tensor_tensor(out=N["dst"](c), in0=N["src"](c), in1=rs_flat,
                                           scalar=cols[:, N["gain"] + c:N["gain"] + c + 1], op0=ALU.mult, op1=ALU.mult)\
                        .then_inc(sem("norm_raw" if N["split"] else "norm_done"), 1)
                if c and N["split"]:
                    dve.wait_ge(sem("norm_hi"), E.after("norm_hi") + 1)
                    v.tensor_tensor(h_lo[c - 1][:], h_raw[:, c - 1], f32(h_hi[c - 1][:]), ALU.subtract)\
                        .then_inc(sem("norm_done"), 1)

        def normed(pe, E, k):
            pe.wait_ge(sem("norm_done"), E.normed + k + 1)

        def dense_unit(pe, E, s, chunks, weight, rhs):
            E.unit_start(s)
            for n, k in enumerate(chunks):
                for j, (a, b) in enumerate(SPLIT):
                    w = weight(n)
                    mm = nc.tensor.matmul(ps[0:w.shape[-1], 3 * s + j, 0:b - a], w, rhs(k)[:, a:b],
                                          start=n == 0, stop=n == len(chunks) - 1)
            return mm

        def token_major_pe(pe, E, widths):
            unit = 0
            for n in widths:
                w = E.next_panel()
                for i in range(NT):
                    s = unit % 2
                    unit += 1
                    E.unit_start(s)
                    for k in range(KC):
                        if unit == 1:
                            normed(pe, E, k)
                        mm = nc.tensor.matmul(ps[0:tile_n(i), 3 * s, 0:n], hT[:, k, i * P:i * P + tile_n(i)],
                                              w[:, k, 0:n], start=k == 0, stop=k == KC - 1)
                    mm.then_inc(unit_ready[s], 1)
                E.free_panel(unit_ready[s], E.seen[s])

        def token_major_out(E, ns, copy, which, widths, dst):
            unit = 0
            for m, n in enumerate(widths):
                for i in range(NT):
                    s = unit % 2
                    unit += 1
                    if s != which:
                        E.pass_unit(s)
                    else:
                        E.unit_wait(s)
                        copy(dst[0:tile_n(i), i, m * 256:m * 256 + n], ps[0:tile_n(i), 3 * s, 0:n])\
                            .then_inc(unit_free[s], 1)

        KV_WIDTHS = [min(WCOL, KVG - m * WCOL) for m in range(4)]
        EVEN = [("q", r) for r in range(4)] + [("z", c) for c in range(4)] + [("x", c) for c in range(XC)] + [("dt", 0)]

        def proj0_pe(pe, E):
            token_major_pe(pe, E, KV_WIDTHS)
            for u, (kind, c) in enumerate(EVEN):
                if u % 2 == 0:
                    w = E.next_panel()
                m = SH if kind == "dt" else P
                mm = dense_unit(pe, E, u % 2, range(KC), lambda n: w[:, n, (u % 2) * P:(u % 2) * P + m], lambda k: hT[:, k])
                mm.then_inc(unit_ready[u % 2], 1)
                if u % 2 == 1 or kind == "dt":
                    E.free_panel(unit_ready[u % 2], E.seen[u % 2])

        def proj0_out(E, which, scaled, copy):
            for u, (kind, c) in enumerate(EVEN):
                if u % 2 != which:
                    E.pass_unit(u % 2)
                    continue
                E.unit_wait(which)
                for j, (a, b) in enumerate(SPLIT):
                    src = ps[0:SH if kind == "dt" else P, 3 * which + j, 0:b - a]
                    if kind == "q":
                        i = scaled(qT[:, c, a:b], src, HD ** -0.5)
                    elif kind == "z":
                        i = copy(zT[:, c, a:b], src)
                    elif kind == "dt":
                        i = copy(dtraw[:, a:b], src)
                    else:
                        e = min(b, SEQ)
                        i = copy(xbc[:, c, XPAD + a:XPAD + e], src[:, 0:e - a])
                        if b > SEQ:
                            dst = xbc[:, c, XS0:].rearrange("p (b t) -> p b t", b=NB)[:, :, XPAD:]
                            i = copy(dst, src[:, SEQ - a:].rearrange("p (b t) -> p b t", b=NB))
                i.then_inc(unit_free[which], 1)

        def proj0_act(act, E):
            token_major_out(E, nc.scalar, nc.scalar.copy, 0, KV_WIDTHS, kvt)
            proj0_out(E, 0, nc.scalar.mul, nc.scalar.copy)

        def proj0_dve(dve, E):
            token_major_out(E, nc.vector, nc.vector.tensor_copy, 1, KV_WIDTHS, kvt)
            proj0_out(E, 1, nc.vector.tensor_scalar_mul, nc.vector.tensor_copy)

        loads["prep_in"] = [(conv_in, d["state_ssm_conv"][0].rearrange("b k n -> (b k) n")),
                            (hv[5], const["keep"])]
        tail = xbc[:, :, XS0:].rearrange("p c (b t) -> p c b t", b=NB)

        QE = 16
        w1c = [at(w0 + s * QE * P, QE, P) for s in range(SLOTS)]
        hid_p = qbd[:, 0, 0:2 * PT * G].rearrange("p (k n) -> p k n", k=2)

        def hidden_sp(sp):
            sp.wait_ge(sem("w1c_zero"), 1)
            for q in range(2 * BLK // QE):
                if q >= SLOTS:
                    sp.wait_ge(sem("w1c_used"), q - SLOTS + 1)
                e = q * QE % BLK
                for b in range(2):
                    sp.dma_start(w1c[q % SLOTS][b * BLK:(b + 1) * BLK, :, b * HD:(b + 1) * HD],
                                 d[("cmp_w1_k", "cmp_w1_v")[q * QE // BLK]][0][:, e:e + QE]).then_inc(sem(f"w1c_in{q % SLOTS}"), 16)

        def hidden_pe(pe, kv):
            for q in range(kv * BLK // QE, (kv + 1) * BLK // QE):
                pe.wait_ge(sem(f"w1c_in{q % SLOTS}"), 32 * (q // SLOTS + 1))
                for j in range(QE):
                    e = q * QE % BLK + j
                    mm = nc.tensor.matmul(ps[:, 6 + kv, 0:PT * G], w1c[q % SLOTS][:, j, :],
                                          kvt[:, 0:PT, kv * P + e:(kv + 1) * P:HD], start=e == 0, stop=e == BLK - 1)
                mm.then_inc(sem("w1c_used"), 1)

        def hidden_act(act):
            for kv in range(2):
                act.wait_ge(sem("w1c_used"), (kv + 1) * BLK // QE)
                nc.scalar.activation(hid_p[:, kv], ps[:, 6 + kv, 0:PT * G], ACT.Gelu_apprx_tanh, bias=peb[:, kv:kv + 1])

        def prep_pe(pe, E):
            loaded(pe, "prep_in")
            for c in range(XC):
                mm = nc.tensor.transpose(ps[:, 0, c * 24:(c + 1) * 24], conv_in[:, c * P:(c + 1) * P], ident[0:24, 0:24])
            mm.then_inc(sem("conv_tr"), 1)
            pe.wait_ge(sem("conv_packed"), 1)
            for c in range(XC):
                mm = nc.tensor.transpose(ps[0:27, 1 + c // 4, (c % 4) * P:(c % 4 + 1) * P], conv_pack[:, c], ident[:])
            mm.then_inc(sem("conv_tr"), 1)
            hidden_pe(pe, 0)
            pe.wait_ge(sem("dt_done"), 1)
            for i in range(NT):
                n = tile_n(i)
                nc.tensor.transpose(ps[0:n, 3, i * 16:i * 16 + 8], hv[4][:, i * P:i * P + n], ident[0:SH, 0:SH])
                mm = nc.tensor.transpose(ps[0:n, 3, i * 16 + 8:i * 16 + 16], acum[:, i * P:i * P + n], ident[0:SH, 0:SH])
            mm.then_inc(sem("dtok_tr"), 1)

        def prep_act(act, E):
            nc.scalar.activation(gates[:, 0:PT], kvt[:, 0:PT, KVW:KVG], ACT.Sigmoid)
            nc.scalar.activation(gates[0:TS, PT], kvt[0:TS, PT, KVW:KVG], ACT.Sigmoid)
            for c in range(R0):
                nc.scalar.activation(zT[:, c], zT[:, c], ACT.Silu)
            act.wait_ge(sem("abs_dt"), 1)
            nc.scalar.activation(hv[1], hv[1], ACT.Exp, scale=-1.0).then_inc(sem("exp_dt"), 1)

        def prep_dve(dve, E):
            v, ch = nc.vector, E.chain
            v.memset(at(w0, SLOTS * QE * P, 1)[:, :, 0], 0.0).then_inc(sem("w1c_zero"), 1)
            ch(v.tensor_scalar(hv[0], dtraw, head_c[:, 0:1], None, ALU.add))
            ch(v.tensor_scalar(hv[1], hv[0], -1.0, None, ALU.mult))
            v.tensor_tensor(hv[1], hv[1], hv[0], ALU.max).then_inc(sem("abs_dt"), 1)
            v.tensor_scalar(hv[4], hv[0], 0.0, None, ALU.max)
            dve.wait_ge(sem("conv_tr"), 1)
            v.tensor_copy(tail[:, :, :, 0:XPAD], ps[:, 0, 0:192].rearrange("p (c b k) -> p c b k", c=XC, b=NB))
            v.memset(xbc[:, :, 0:XPAD], 0.0)
            v.tensor_copy(conv_pack[:, :, 0:XPAD], xbc[:, :, SEQ:SEQ + XPAD])
            for k in range(XPAD):
                i = v.tensor_copy(conv_pack[:, :, XPAD + k:27:XPAD], tail[:, :, :, DL + k])
            i.then_inc(sem("conv_packed"), 1)
            dve.wait_ge(sem("exp_dt"), 1)
            ch(v.tensor_scalar(hv[2], hv[1], 2.0, None, ALU.add))
            ch(v.reciprocal(hv[2], hv[2]))
            ch(v.tensor_tensor(hv[1], hv[1], hv[2], ALU.mult))
            ch(v.tensor_tensor(hv[2], hv[1], hv[1], ALU.mult))
            ch(v.tensor_scalar(hv[3], hv[2], 1.0 / 15, None, ALU.mult))
            for k in (13, 11, 9, 7, 5, 3):
                ch(v.scalar_tensor_tensor(out=hv[3], in0=hv[3], scalar=1.0 / k, in1=hv[2], op0=ALU.add, op1=ALU.mult))
            ch(v.scalar_tensor_tensor(out=hv[3], in0=hv[3], scalar=1.0, in1=hv[1], op0=ALU.add, op1=ALU.mult))
            ch(v.scalar_tensor_tensor(out=hv[4], in0=hv[3], scalar=2.0, in1=hv[4], op0=ALU.mult, op1=ALU.add))
            ch(v.tensor_scalar(hv[0], hv[4], head_c[:, 2:3], None, ALU.mult))
            loaded(dve, "prep_in")
            v.tensor_tensor_scan(acum, hv[5], hv[0], 0.0, ALU.mult, ALU.add).then_inc(sem("dt_done"), 1)
            dve.wait_ge(sem("conv_tr"), 2)
            for h in range(2):
                i = v.tensor_copy(conv_out[:, h * 512:(h + 1) * 512], ps[0:27, 1 + h])
            i.then_inc(sem("conv_rows"), 1)
            dve.wait_ge(sem("dtok_tr"), 1)
            v.tensor_copy(dtok[:, 0:PT], ps[:, 3, 0:PT * 16].rearrange("p (i h) -> p i h", h=16))
            v.tensor_copy(dtok[0:TS, PT], ps[0:TS, 3, PT * 16:NT * 16])

        stores = [0]

        def store(e, dst, src):
            stores[0] += 1
            e.dma_start(dst, src).then_inc(stored, 16)

        def rows(x):
            return x.rearrange("t a g e -> t (a g e)")

        def prep_pool(pool, E):
            names = (("cmp_prompt", "cmp_sample"), ("slc_prompt", "slc_sample"))
            for n, (pr, sa) in enumerate(names):
                c = slice(n * 256, (n + 1) * 256)
                store(pool, rows(d[pr][0, 0]).rearrange("(i p) n -> p i n", p=P), kvt[:, 0:PT, c])
                store(pool, d[sa][0].rearrange("b t a g e -> (b t) (a g e)"), kvt[0:TS, PT, c])
            store(pool, rows(d["win_prompt"][0, 0]).rearrange("(i p) n -> p i n", p=P), kvt[:, 4:PT, 512:768])
            for b in range(NB):
                store(pool, rows(d["win_sample"][0, b])[WIN0 - DL:], kvt[b * DL:(b + 1) * DL, PT, 512:768])
            store(pool, d["win_sample"][0, :, 0:WIN0 - DL].rearrange("b t a g e -> b (t a g e)"),
                  d["state_nsa_win_kv"][0, :, DL:].rearrange("b t a g e -> b (t a g e)"))
            store(pool, d["swa_sample"][0, :, 0:WIN1 - DL].rearrange("b t a g e -> b (t a g e)"),
                  d["state_swa_kv"][0, :, DL:].rearrange("b t a g e -> b (t a g e)"))
            pool.wait_ge(sem("conv_rows"), 1)
            pool.dma_start(d["conv_prompt"][0, 0], conv_out[0:XPAD]).then_inc(sem("conv_stored"), 16)
            pool.dma_start(d["conv_sample"][0].rearrange("b k n -> (b k) n"), conv_out[XPAD:27])\
                .then_inc(sem("conv_stored"), 16)

        def conv_taps(c):
            for part in range(2):
                out = xc[:, c, 0:SEQ] if part == 0 else xc[:, c, SEQ:].rearrange("p (b t) -> p b t", b=NB)
                taps = [xbc[:, c, k:k + SEQ] if part == 0 else tail[:, c, :, k:k + DL] for k in range(CONV)]
                yield out, taps

        def conv_act(act, E):
            act.wait_ge(sem("conv_stored"), 32)
            for c in range(XC):
                for out, taps in conv_taps(c):
                    i = nc.scalar.activation(out, taps[0], ACT.Identity, scale=cols[:, CONV_W + c:CONV_W + c + 1],
                                             bias=cols[:, CONV_B + c:CONV_B + c + 1])
                i.then_inc(sem("conv_first"), 1)
            for c in range(XC):
                act.wait_ge(sem("conv_sum"), c + 1)
                nc.scalar.activation(xc[:, c], xc[:, c], ACT.Silu)
            hidden_act(act)

        def conv_dve(dve, E):
            for c in range(XC):
                dve.wait_ge(sem("conv_first"), c + 1)
                for k in range(1, CONV):
                    w = cols[:, CONV_W + k * XC + c:CONV_W + k * XC + c + 1]
                    for out, taps in conv_taps(c):
                        i = nc.vector.scalar_tensor_tensor(out=out, in0=taps[k], scalar=w, in1=out,
                                                           op0=ALU.mult, op1=ALU.add)
                    if k < CONV - 1:
                        E.chain(i)
                i.then_inc(sem("conv_sum"), 1)

        loads["ssm_in"] = [(causal, const["causal"]), (causal8, const["causal8"]), (own_seq, const["own_seq"]),
                           (last_tok, const["last_tok"])]
        loads["ssm_state_in"] = [(s0_in[:, b], d["state_ssm"][0, b].rearrange("(c h) e n -> (h e) c n", h=2))
                                 for b in range(NB)]

        def toks(i):
            return slice(i * P, i * P + tile_n(i))

        def ssm_pe(pe, E):
            loaded(pe, "ssm_in")
            def before(c):
                n, t = tile_n(c), toks(c)
                if c:
                    pe.wait_ge(sem("ssm_seg"), c)
                    pe.wait_ge(sem("ssm_act"), c)
                for j in range(4):
                    nc.tensor.transpose(ps[0:n, 0, j * P:(j + 1) * P], xc[:, j, t], ident[:])
                for g in range(G):
                    nc.tensor.transpose(ps[0:n, 1, g * P:(g + 1) * P], xc[:, 4 + g, t], ident[:])
                    nc.tensor.matmul(ps[0:n, 2, g * P:g * P + n], xc[:, 4 + g, t], xc[:, 6 + g, t], start=True, stop=True)
                if c == PT:
                    nc.tensor.matmul(ps[0:TS, 1, 256:264], last_tok, dtok[0:TS, PT, 8:16], start=True, stop=True)
                    for h in range(SH):
                        j = h // 2
                        nc.tensor.matmul(ps[h % 2 * HD:(h % 2 + 1) * HD, 1, 272 + 8 * j:280 + 8 * j],
                                         ident[0:SH, h:h + 1].to_broadcast([SH, HD]),
                                         acum[:, SEQ + DL - 1:T:DL], start=True, stop=True)
                for h in range(SH):
                    mm = nc.tensor.matmul(ps[:, 3 + h // 4, (h % 4) * n:(h % 4 + 1) * n],
                                          ident[0:SH, h:h + 1].to_broadcast([SH, P]), acum[:, t], start=True, stop=True)
                mm.then_inc(sem("ssm_pre"), 1)

            before(0)
            for c in range(NT):
                n, t = tile_n(c), toks(c)
                if c < PT:
                    before(c + 1)
                pe.wait_ge(sem("ssm_ops"), c + 1)
                if c:
                    pe.wait_ge(sem("ssm_post_out"), min(c, PT))
                if c < PT:
                    for g in range(G):
                        nc.tensor.matmul(ps[:, 5, g * 256:(g + 1) * 256], m_bt[c % 2][0:n, g], m_xw[c % 2][0:n, 4 * g:4 * g + 4],
                                         start=True, stop=True)
                    for h in range(SH):
                        out = ps[h % 2 * HD:(h % 2 + 1) * HD, 6, h // 2 * P:h // 2 * P + n]
                        if c:
                            nc.tensor.matmul(out, m_st[:, h], m_eac[c % 2][:, h, 0:n], start=True, stop=False)
                        mm = nc.tensor.matmul(out, m_xdt[c % 2][0:n, h], m_seg[c % 2][0:n, h, 0:n], start=c == 0, stop=True)
                    mm.then_inc(sem("ssm_post"), 1)
                if c == PT - 1:
                    pe.wait_ge(sem("ssm_post_out"), PT)
                    for j in range(4):
                        mm = nc.tensor.transpose(ps[:, 5, j * P:(j + 1) * P], m_st[:, 2 * j:2 * j + 2], ident[:])
                    mm.then_inc(sem("ssm_fin_tr"), 1)
            loaded(pe, "ssm_state_in")
            pe.wait_ge(sem("ssm_fin"), 1)
            for h in range(SH):
                nc.tensor.matmul(ps[h % 2 * HD:(h % 2 + 1) * HD, 6, h // 2 * TS:(h // 2 + 1) * TS], m_xdt[0][0:TS, h],
                                 m_seg[0][0:TS, h, 0:TS], start=h < 2, stop=False, skip_group_check=True)
            for b in range(NB + 1):
                if b < NB:
                    for j in range(4):
                        mm = nc.tensor.transpose(ps[:, 5 + 2 * (b % 2), j * P:(j + 1) * P], s0_in[:, b, j], ident[:])
                    mm.then_inc(sem("s0_tr"), 1)
                if b:
                    pe.wait_ge(sem("s0t_ready"), b)
                    for h in range(SH):
                        o = h // 2 * TS + (b - 1) * DL
                        mm = nc.tensor.matmul(ps[h % 2 * HD:(h % 2 + 1) * HD, 6, o:o + DL], s0t[:, h * HD:(h + 1) * HD],
                                              m_eac[0][:, h, (b - 1) * DL:b * DL], start=False, stop=b == NB,
                                              skip_group_check=True)
                    mm.then_inc(sem("s0t_used"), 1)
            pe.wait_ge(sem("bd_ready"), 1)
            for j in range(4):
                if j >= 2:
                    pe.wait_ge(sem("s_new"), j - 1)
                for k in range(2):
                    mm = nc.tensor.matmul(ps[:, 2 * (j % 2) + k], m_xw[0][0:TS, 2 * j:2 * j + 2],
                                          m_bd[j // 2][:, 4 * k:4 * k + 4], start=True, stop=True)
                mm.then_inc(sem("s_new_mm"), 1)

        def ssm_dve(dve, E):
            v, ch = nc.vector, E.chain
            loaded(dve, "ssm_in")

            def operands(c):
                n, t = tile_n(c), toks(c)
                dve.wait_ge(sem("ssm_pre"), c + 1)
                if c >= 2:
                    dve.wait_ge(sem("ssm_post_out"), c - 1)
                v.tensor_tensor(m_xdt[c % 2][0:n], ps[0:n, 0].rearrange("p (h e) -> p h e", h=SH),
                                dtok[0:n, c, 0:8].unsqueeze(2).to_broadcast([n, SH, HD]), ALU.mult)
                if c == PT:
                    v.tensor_tensor(m_de[c % 2][0:n], ps[0:n, 1, 256:264], dtok[0:n, c, 8:16], ALU.subtract)
                v.tensor_tensor(m_cb[c % 2][0:n, :, 0:n], ps[0:n, 2, 0:256].rearrange("p (g t) -> p g t", g=G)[:, :, 0:n],
                                (causal if c < PT else causal8).unsqueeze(1).to_broadcast([n, G, n]), ALU.mult)
                for g in range(G):
                    ac = ps[0:n, 3 + g, 0:4 * n].rearrange("p (h t) -> p h t", h=4)
                    dt = dtok[0:n, c, 8 + 4 * g:12 + 4 * g]
                    if c < PT:
                        v.tensor_tensor(m_de[c % 2][0:n, 4 * g:4 * g + 4], ac[:, :, n - 1], dt, ALU.subtract)
                    i = v.tensor_tensor(m_seg[c % 2][0:n, 4 * g:4 * g + 4, 0:n], ac, dt.unsqueeze(2).to_broadcast([n, 4, n]),
                                        ALU.subtract)
                i.then_inc(sem("ssm_seg"), 1)
                dve.wait_ge(sem("ssm_seg"), c + 1)
                v.tensor_scalar(m_seg[c % 2][0:n, :, 0:n], m_seg[c % 2][0:n, :, 0:n], 0.0, None, ALU.min).then_inc(sem("ssm_min"), 1)
                dve.wait_ge(sem("ssm_de"), c + 1)
                v.tensor_tensor(m_xw[c % 2][0:n], m_xdt[c % 2][0:n], m_de[c % 2][0:n].unsqueeze(2).to_broadcast([n, SH, HD]), ALU.mult)
                if c < PT:
                    ch(v.tensor_copy(m_all[c % 2], m_eac[c % 2][:, :, n - 1]))
                for g in range(G):
                    e = m_eac[c % 2][:, 4 * g:4 * g + 4, 0:n]
                    v.tensor_tensor(e, e, xc[:, 6 + g, t].unsqueeze(1).to_broadcast([P, 4, n]), ALU.mult)
                dve.wait_ge(sem("ssm_l"), c + 1)
                for g in range(G):
                    e = m_seg[c % 2][0:n, 4 * g:4 * g + 4, 0:n]
                    i = v.tensor_tensor(e, e, m_cb[c % 2][0:n, g, 0:n].unsqueeze(1).to_broadcast([n, 4, n]), ALU.mult)
                i.then_inc(sem("ssm_ops"), 1)

            def state_and_output(c):
                n, t = tile_n(c), toks(c)
                dve.wait_ge(sem("ssm_post"), c + 1)
                if c == 0:
                    v.tensor_copy(m_st[:], ps[:, 5].rearrange("p (h e) -> p h e", h=SH))
                else:
                    ch(v.tensor_tensor(m_st[:], m_st[:], m_all[c % 2].unsqueeze(2).to_broadcast([P, SH, HD]), ALU.mult))
                    v.tensor_tensor(m_st[:], m_st[:], ps[:, 5].rearrange("p (h e) -> p h e", h=SH), ALU.add)
                y = m_xdt[c % 2][:].rearrange("p h e -> p (h e)").rearrange("p (j t) -> p j t", j=4)
                for j in range(4):
                    i = v.scalar_tensor_tensor(out=y[:, j], in0=xc[:, j, t], scalar=d_col[:, j:j + 1],
                                               in1=ps[:, 6, j * P:(j + 1) * P], op0=ALU.mult, op1=ALU.add)
                ch(i)
                v.tensor_tensor(zT[:, :, t], zT[:, :, t], y, ALU.mult).then_inc(sem("ssm_post_out"), 1)
                if c == PT - 1:
                    dve.wait_ge(sem("ssm_fin_tr"), 1)
                    v.tensor_copy(s0t, ps[:, 5]).then_inc(sem("ssm_fin"), 1)

            for c in range(NT):
                operands(c)
                if c:
                    state_and_output(c - 1)
            t = slice(SEQ, T)
            dve.wait_ge(sem("s0t_used"), NB)
            y = m_cb[0][:].rearrange("p g t -> p (g t)").rearrange("p (j t) -> p j t", j=4)
            for j in range(4):
                i = v.scalar_tensor_tensor(out=y[:, j], in0=xc[:, j, t], scalar=d_col[:, j:j + 1],
                                           in1=ps[:, 6, j * TS:(j + 1) * TS], op0=ALU.mult, op1=ALU.add)
            ch(i)
            v.tensor_tensor(zT[:, :, t], zT[:, :, t], y, ALU.mult)
            for g in range(G):
                i = v.tensor_tensor(m_bd[g], m_bt[0][0:TS, g].unsqueeze(1).to_broadcast([TS, NB, SN]),
                                    own_seq.unsqueeze(2).to_broadcast([TS, NB, SN]), ALU.mult)
            i.then_inc(sem("bd_ready"), 1)
            for j in range(4):
                dve.wait_ge(sem("s_new_mm"), j + 1)
                for b in range(NB):
                    i = v.scalar_tensor_tensor(out=s0_in[:, b, j], in0=s0_in[:, b, j],
                                               scalar=small[:, 32 + 8 * j + b:33 + 8 * j + b],
                                               in1=ps[:, 2 * (j % 2) + b // 4, (b % 4) * SN:(b % 4 + 1) * SN],
                                               op0=ALU.mult, op1=ALU.add)
                i.then_inc(sem("s_new"), 1)

        def ssm_act(act, E):
            for c in range(NT):
                n = tile_n(c)
                act.wait_ge(sem("ssm_seg"), c + 1)
                if c == PT:
                    nc.scalar.activation(small[:, 32:64], ps[:, 1, 272:304], ACT.Exp)
                nc.scalar.copy(m_bt[c % 2][0:n], ps[0:n, 1, 0:256].rearrange("p (g e) -> p g e", g=G))
                for g in range(G):
                    i = nc.scalar.activation(m_eac[c % 2][:, 4 * g:4 * g + 4, 0:n],
                                             ps[:, 3 + g, 0:4 * n].rearrange("p (h t) -> p h t", h=4), ACT.Exp)
                i.then_inc(sem("ssm_act"), 1)
                nc.scalar.activation(m_de[c % 2][0:n], m_de[c % 2][0:n], ACT.Exp).then_inc(sem("ssm_de"), 1)
                act.wait_ge(sem("ssm_min"), c + 1)
                nc.scalar.activation(m_seg[c % 2][0:n, :, 0:n], m_seg[c % 2][0:n, :, 0:n], ACT.Exp).then_inc(sem("ssm_l"), 1)
            act.wait_ge(sem("ssm_fin_stored"), 16)
            for b in range(NB):
                act.wait_ge(sem("s0_tr"), b + 1)
                if b:
                    act.wait_ge(sem("s0t_used"), b)
                nc.scalar.copy(s0t, ps[:, 5 + 2 * (b % 2)]).then_inc(sem("s0t_ready"), 1)

        def ssm_pool(pool, E):
            pool.wait_ge(sem("ssm_fin"), 1)
            pool.dma_start(d["ssm_prompt"][0, 0].rearrange("(c h) e n -> (h e) c n", h=2),
                           s0t.rearrange("p (c n) -> p c n", c=4)).then_inc(sem("ssm_fin_stored"), 16)
            pool.wait_ge(sem("s_new"), 4)
            for b in range(NB):
                pool.dma_start(d["ssm_sample"][0, b].rearrange("(c h) e n -> (h e) c n", h=2), s0_in[:, b])\
                    .then_inc(sem("s0_stored"), 16)

        cmp_diag = at(h0 + 8192, R0, P)
        pcT = at(free_b, PT, P)
        vbd = at(free_b + 1024, R0, P)
        sc = at(free_b + 1536, PT, 8 * PCB)
        bias_cmp = at(free_b + 2560, PT, 8 * PCB)
        loads["cmp_bias_in"] = [(bias_cmp, const["bias_cmp"].rearrange("p i h n -> p i (h n)")),
                                (cmp_diag, const["cmp_diag"].rearrange("p (r c) -> p r c", r=R0))]
        kcp, vcp = cst[:, 0:PCB], cst[:, 128:256]
        cm, cden = cst[:, 256:320], cst[:, 320:384]

        def cmp_sp(sp):
            sp.wait_ge(stage_end, END["ssm"])
            sp.wait_ge(sem("s0_stored"), 16 * NB)
            load(sp, "cmp_bias_in")

        def cmp_pe(pe, E):
            for kv in range(2):
                for b in range(2):
                    for g in range(G):
                        half = slice(b * HD, (b + 1) * HD)
                        mm = nc.tensor.matmul(ps[g * HD:(g + 1) * HD, 3 + b, kv * PT:(kv + 1) * PT],
                                              w2[half, kv], hid_p[half, kv, g:PT * G:G], start=True, stop=True)
            mm.then_inc(sem("cmp_mm"), 1)
            pe.wait_ge(sem("cmp_kv"), 1)
            nc.tensor.transpose(ps[:, 5, 0:P], vcp, ident[:]).then_inc(sem("cmp_mm"), 1)
            for i in range(PT):
                for r in range(R0):
                    for g in range(G):
                        o = (i * R0 + r) * PCB
                        half = slice(g * HD, (g + 1) * HD)
                        mm = nc.tensor.matmul(ps[:, 6 + g, o:o + PCB], qT[half, r, toks(i)], kcp[half],
                                              start=True, stop=True)
            mm.then_inc(sem("cmp_mm"), 1)
            pe.wait_ge(sem("cmp_p"), 1)
            for i in range(PT):
                mm = nc.tensor.transpose(ps[:, 6 + i // 4, (i % 4) * P:(i % 4 + 1) * P], sc[:, i], ident[:])
            mm.then_inc(sem("cmp_mm"), 1)

        def cmp_act(act, E):
            act.wait_ge(sem("cmp_s"), 1)
            nc.scalar.activation(sc, sc, ACT.Exp).then_inc(sem("cmp_e"), 1)

        def cmp_dve(dve, E):
            v, ch = nc.vector, E.chain
            dve.wait_ge(sem("cmp_mm"), 1)
            kb = ps[:, 3:5, 0:2 * PT].rearrange("p b (k n) -> p k n b", k=2)
            v.tensor_copy(kcp.rearrange("p (n b) -> p n b", b=2), kb[:, 0])
            for h in range(8):
                i = v.tensor_copy(vcp[:, h * PCB:(h + 1) * PCB].rearrange("p (n b) -> p n b", b=2), kb[:, 1])
            i.then_inc(sem("cmp_kv"), 1)
            loaded(dve, "cmp_bias_in")
            dve.wait_ge(sem("cmp_mm"), 2)
            v.tensor_tensor(vbd, ps[:, 5, 0:P].unsqueeze(1).to_broadcast([P, R0, P]), cmp_diag, ALU.mult)
            dve.wait_ge(sem("cmp_mm"), 3)
            for g in range(G):
                s5, b5 = (x.rearrange("p i (r g n) -> p i r g n", r=R0, g=G)[:, :, :, g] for x in (sc, bias_cmp))
                i = v.tensor_tensor(s5, ps[:, 6 + g].rearrange("p (i r n) -> p i r n", i=PT, r=R0), b5, ALU.add)
            ch(i)
            s3 = sc.rearrange("p i (h n) -> p (i h) n", n=PCB)
            ch(v.tensor_reduce(cm, s3, AX_X, ALU.max))
            ch(v.tensor_scalar(cm, cm, FLOOR, None, ALU.max))
            v.tensor_tensor(s3, s3, cm.unsqueeze(2).to_broadcast([P, 64, PCB]), ALU.subtract).then_inc(sem("cmp_s"), 1)
            dve.wait_ge(sem("cmp_e"), 1)
            ch(v.tensor_reduce(cden, s3, AX_X, ALU.add))
            ch(v.tensor_scalar(cden, cden, 1e-30, None, ALU.max))
            ch(v.reciprocal(cden, cden))
            for g in range(G):
                c4 = cden.rearrange("p (i r g) -> p i r g", i=PT, r=R0)[:, :, :, g]
                i = v.tensor_tensor(c4, c4, gates[:, 0:PT, g * 12:g * 12 + 12:3], ALU.mult)
            ch(i)
            v.tensor_tensor(s3, s3, cden.unsqueeze(2).to_broadcast([P, 64, PCB]), ALU.mult).then_inc(sem("cmp_p"), 1)
            dve.wait_ge(sem("cmp_mm"), 4)
            for k in range(2):
                v.tensor_copy(pcT[:, 4 * k:4 * k + 4], ps[:, 6 + k].rearrange("p (i t) -> p i t", i=4))

        kS, kW = at(h0, 1, T)[:, 0], at(h0 + T, 1, T)[:, 0]
        bias_s = at(h0 + 2 * T, G, SEQ)
        bias_w = at(h0 + 2 * T + 2048, G, WIN0 + P)
        sp3 = [at(h0 + 2 * T + 3328 + k * 1024, 1, 1024)[:, 0] for k in range(3)]
        pt2 = [at(free_b + 1536 + k * 1024, 8, P) for k in range(2)]
        ob = [at(free_b + 3584 + k * P, G, HD) for k in range(2)]
        after_s = free_b + 6208 + NPAGE * 256
        knew = at(after_s + 144, 2, TS)
        negm, den8, scal = small[:, 0:4], small[:, 8:16], small[:, 16:24]
        loads["bias_in"] = [(bias_s, const["bias_slc"]), (bias_w, const["bias_win"])]
        UNITS = [(r, i, g, br) for r in range(R0) for i in range(PT) for g in range(G) for br in range(2)]

        def key_tiles(u):
            _, i, _, br = UNITS[u]
            n = i + 1 if br == 0 else min(i + 1, WIN0 // P + 1)
            return i + 1 - n, n

        groups, first_group = [], []
        for u in range(len(UNITS)):
            first_group.append(len(groups))
            n = key_tiles(u)[1]
            groups += [(u, j, min(4, n - j)) for j in range(0, n, 4)]
        first_group.append(len(groups))

        def attn_pe(pe, E):
            for k, (dst0, col) in enumerate(((0, 256), (3, 512))):
                for i in range(NT):
                    n = tile_n(i)
                    mm = nc.tensor.transpose(ps[:, dst0 + i // 4, (i % 4) * P:(i % 4) * P + n],
                                             kvt[0:n, i, col:col + P], ident[0:n, 0:n])
                mm.then_inc(sem("kt_tr"), 1)
            pe.wait_ge(sem("kt_s"), 1)
            pe.wait_ge(sem("kt_w"), 1)
            n_units = len(UNITS)
            for step in range(n_units + 5):
                if step < n_units:
                    u = step
                    r, i, g, br = UNITS[u]
                    if u >= 2:
                        pe.wait_ge(sem("at_scored"), u - 1)
                    j0, n = key_tiles(u)
                    half = slice(g * HD, (g + 1) * HD)
                    keys = (kS, kW)[br]
                    for a in range(0, n * P, 512):
                        b = min(a + 512, n * P)
                        mm = nc.tensor.matmul(ps[:, 2 * (u % 2) + a // 512, 0:b - a], qT[half, r, toks(i)],
                                              keys[half, j0 * P + a:j0 * P + b], start=True, stop=True)
                    mm.then_inc(sem("at_qk"), 1)
                if 2 <= step < n_units + 2:
                    u = step - 2
                    pe.wait_ge(sem("at_exp"), u + 1)
                    for k in range(first_group[u], first_group[u + 1]):
                        _, j, n = groups[k]
                        if k >= 2:
                            pe.wait_ge(sem(f"at_copied{k % 2}"), k // 2)
                        for b in range(n):
                            mm = nc.tensor.transpose(ps[:, 4 + k % 2, b * P:(b + 1) * P],
                                                     sp3[u % 3][:, (j + b) * P:(j + b + 1) * P], ident[:])
                        mm.then_inc(sem("at_tr"), 1)
                if 3 <= step < n_units + 3:
                    u = step - 3
                    r, i, g, br = UNITS[u]
                    ri, k4 = u // 4, u % 4
                    last = first_group[u + 1] - 1
                    for k in {last, max(last - 1, 0)}:
                        pe.wait_ge(sem(f"at_copied{k % 2}"), k // 2 + 1)
                    if k4 == 0 and ri >= 2:
                        pe.wait_ge(sem("at_oT"), ri - 1)
                    j0, n = key_tiles(u)
                    c = 256 + 256 * br + P + g * HD
                    for j in range(n):
                        mm = nc.tensor.matmul(ps[:, 6 + ri % 2, k4 * HD:(k4 + 1) * HD], pt2[u % 2][:, j],
                                              kvt[:, j0 + j, c:c + HD], start=j == 0, stop=j == n - 1)
                    if k4 == 3:
                        mm = nc.tensor.matmul(ps[:, 6 + ri % 2, 256:384], pcT[:, i], vbd[:, r], start=True, stop=True)
                    mm.then_inc(sem("at_pv"), 1)
                if step >= 8 and step % 4 == 0:
                    ri = step // 4 - 2
                    pe.wait_ge(sem("at_o"), ri + 1)
                    nc.tensor.transpose(ps[:, 6 + ri % 2, 384:512], ob[ri % 2].rearrange("p g e -> p (g e)"), ident[:])\
                        .then_inc(sem("at_ot"), 1)

        def copy_groups(e, copy, u, which):
            for k in range(first_group[u], first_group[u + 1]):
                _, j, n = groups[k]
                if k % 2 == which:
                    e.wait_ge(sem("at_tr"), k + 1)
                    if u >= 2:
                        e.wait_ge(sem("at_pv"), u - 1)
                    copy(pt2[u % 2][:, j:j + n], ps[:, 4 + k % 2, 0:n * P].rearrange("p (j t) -> p j t", j=n))\
                        .then_inc(sem(f"at_copied{which}"), 1)

        def attn_dve(dve, E):
            v, ch = nc.vector, E.chain
            dve.wait_ge(sem("kt_tr"), 1)
            v.tensor_copy(kS[:], ps[:, 0:3].rearrange("p b c -> p (b c)")[:, 0:T]).then_inc(sem("kt_s"), 1)
            loaded(dve, "bias_in")
            n_units = len(UNITS)

            def finish(ri):
                r, i = UNITS[4 * ri][:2]
                dve.wait_ge(sem("at_pv"), 4 * ri + 4)
                s = (ri % 2) * 4
                ch(v.reciprocal(scal[:, s:s + 4], den8[:, s:s + 4]))
                gt = gates[:, i].rearrange("p (g r k) -> p g r k", g=G, r=R0)[:, :, r, 1:3]
                s4 = scal[:, s:s + 4].rearrange("p (g k) -> p g k", g=G)
                ch(v.tensor_tensor(s4, s4, gt, ALU.mult))
                o, bank = ob[ri % 2], ps[:, 6 + ri % 2]
                if ri >= 2:
                    dve.wait_ge(sem("at_ot"), ri - 1)
                ch(v.tensor_copy(o, bank[:, 256:384].rearrange("p (g e) -> p g e", g=G)))
                for br in range(2):
                    for g in range(G):
                        k = g * 2 + br
                        ins = v.scalar_tensor_tensor(out=o[:, g], in0=bank[:, k * HD:(k + 1) * HD],
                                                     scalar=scal[:, s + k:s + k + 1], in1=o[:, g],
                                                     op0=ALU.mult, op1=ALU.add)
                    if br == 0:
                        ch(ins)
                ins.then_inc(sem("at_o"), 1)

            for step in range(n_units + 5):
                if step >= 7 and step % 4 == 3 and step // 4 - 1 < n_units // 4:
                    finish(step // 4 - 1)
                if 2 <= step < n_units + 2:
                    copy_groups(dve, v.tensor_copy, step - 2, 0)
                if step < n_units:
                    u = step
                    r, i, g, br = UNITS[u]
                    if i == 0 and g == 0 and br == 0 and r:
                        dve.wait_ge(sem("at_scored"), u)
                        v.tensor_scalar(bias_s, bias_s, 0.5, None, ALU.mult)
                        ch(v.tensor_scalar(bias_w, bias_w, 0.5, None, ALU.mult))
                    n = key_tiles(u)[1] * P
                    bias = (bias_s, bias_w)[br]
                    dve.wait_ge(sem("at_qk"), u + 1)
                    if u >= 3:
                        dve.wait_ge(sem("at_tr"), first_group[u - 2])
                    if u >= 4:
                        dve.wait_ge(sem("at_exp"), u - 3)
                    v.tensor_tensor_reduce(sp3[u % 3][:, 0:n],
                                           ps[:, 2 * (u % 2):2 * (u % 2) + 2].rearrange("p b c -> p (b c)")[:, 0:n],
                                           bias[:, g, bias.shape[2] - n:], -1.0, -NEG, ALU.add, ALU.min,
                                           negm[:, u % 4:u % 4 + 1]).then_inc(sem("at_scored"), 1)
            v.tensor_copy(knew[:, 0], kS[:, SEQ:])
            ch(v.tensor_copy(knew[:, 1], kW[:, SEQ:]))
            ch(v.memset(qbd[:], 0.0))
            for g in range(G):
                half = slice(g * HD, (g + 1) * HD)
                v.tensor_copy(qbd[half, :, g * 32:(g + 1) * 32].rearrange("p b (r t) -> p b r t", r=R0),
                              qT[half, :, SEQ:].rearrange("p r (b t) -> p b r t", b=NB))

        def attn_act(act, E):
            act.wait_ge(sem("kt_tr"), 2)
            nc.scalar.copy(kW, ps[:, 3:6].rearrange("p b c -> p (b c)")[:, 0:T]).then_inc(sem("kt_w"), 1)
            n_units = len(UNITS)

            def out(ri):
                r, i = UNITS[4 * ri][:2]
                act.wait_ge(sem("at_ot"), ri + 1)
                nc.scalar.copy(oN[:, r, toks(i)], ps[:, 6 + ri % 2, 384:512]).then_inc(sem("at_oT"), 1)

            for step in range(n_units + 5):
                if step >= 9 and step % 4 == 1:
                    out(step // 4 - 2)
                if 2 <= step < n_units + 2:
                    copy_groups(act, nc.scalar.copy, step - 2, 1)
                if step < n_units:
                    u = step
                    n = key_tiles(u)[1] * P
                    act.wait_ge(sem("at_scored"), u + 1)
                    s = (u // 4 % 2) * 4 + u % 4
                    if u % 4 == 0 and u >= 8:
                        act.wait_ge(sem("at_o"), u // 4 - 1)
                    nc.scalar.activation(sp3[u % 3][:, 0:n], sp3[u % 3][:, 0:n], ACT.Exp, scale=-1.0,
                                         bias=negm[:, u % 4:u % 4 + 1], accum_out=den8[:, s:s + 1])\
                        .then_inc(sem("at_exp"), 1)
            out(n_units // 4 - 1)

        rs_places = [at(h0, NPAGE, 256), at(h0 + 4096, NPAGE, 256), at(free_b + 2112, NPAGE, 256), at(free_b + 6208, NPAGE, 256)]
        rs = [rs_places[(b + 3) % 4] for b in range(NB)]
        ptx, pc = at(h0 + 8192, 3, P, parts=TS), at(h0 + 8576, NB // 2, NCB)
        kts, ktw = at(kv0, NPAGE, P), at(kv0 + 2048, 4, P)
        rw = [at(kv0 + 2560 + s * 1024, 4, 256) for s in range(2)]
        dec_cmp, dec_blk = at(kv0 + 4608, 1, NCB)[:, 0], at(kv0 + 4640, 1, NCB)[:, 0]
        dec_off, dec_new = at(kv0 + 4672, 1, BLK)[:, 0], at(kv0 + 4736, NB // 2, TS)
        over, tok_rows = at(kv0 + 4992, 1, P)[:, 0], at(kv0 + 5120, NB // 2, P, parts=TS)
        pick, dec_win = at(kv0 + 5632, 1, 24)[:, 0], at(kv0 + 5656, 1, WIN0)[:, 0]
        pts, ptw = at(q0, NPAGE, P), at(q0 + 2048, 4, P)
        dw = at(q0 + 2560, 1, WIN0 + TS)[:, 0]
        earlier = at(q0 + 3136, 1, NCB * NCB)[:, 0]
        imp, selb = at(q0 + 4160, NB // 2, NCB), at(after_s, NB // 2, NCB + 1)
        grow = at(after_s + 132, NB // 2, 3)
        ds = at(free_b, NCB + 1, BLK)
        ra, rb = at(free_b, NCB, NCB), at(free_b + 1024, NCB, NCB)
        loads["dec_in"] = [(dec_cmp, const["dec_cmp"]), (dec_blk, const["dec_blk"]), (dec_off, const["dec_off"]),
                           (dec_new, const["dec_new"]), (over, const["over_heads"]), (tok_rows, const["tok_rows"]),
                           (pick, const["gate_pick"]), (dec_win, const["dec_win"]),
                           (earlier, const["earlier"].rearrange("p a b -> p (a b)"))]
        NEW_S = kvt[0:TS, PT, 256:512]
        NEW_W = kvt[0:TS, PT, 512:768]

        dgroups = []
        for bp in range(NB // 2):
            for b in (2 * bp, 2 * bp + 1):
                dgroups += [("k", bp, b, j) for j in range(4)] + [("kw", bp, b, 0)]
            dgroups += [("p", bp, 0, j) for j in range(4)] + [("pw", bp, 0, 0), ("px", bp, 0, 0)]

        def dec_sp(sp):
            load(sp, "dec_in", "attn")
            for bp in range(NB // 2):
                if bp >= 2:
                    sp.wait_ge(sem("dt_pv"), bp - 1)
                for b in (2 * bp, 2 * bp + 1):
                    if b:
                        dec_pages(sp, b)
                if bp:
                    sp.wait_ge(sem("dt_pv"), bp)
                for b in (2 * bp, 2 * bp + 1):
                    sp.dma_start(rw[b % 2], d["state_nsa_win_kv"][0, b].rearrange("(j p) a g e -> p j (a g e)", p=P))\
                        .then_inc(sem(f"win_in{b % 2}"), 16)

        def dec_pages(sp, b):
            for j in range(0, NPAGE, LD):
                page_loads(sp, slc_pages, lambda i: rs[b][:, j + i, :], b * NPAGE + j, sem(f"seq_in{b % 4}"))

        def dec_pe(pe, E):
            loaded(pe, "dec_in")
            for b in range(NB):
                part = slice(b % 2 * HD, (b % 2 + 1) * HD)
                nc.tensor.matmul(ps[part, 0, b // 2 * NCB:(b // 2 + 1) * NCB], qbd[:, b], kcT[:, b * NCB:(b + 1) * NCB],
                                 start=True, stop=True)
            for bp in range(NB // 2):
                mm = nc.tensor.matmul(ps[:, 1, bp * 24:(bp + 1) * 24], tok_rows[:, bp], gates[0:TS, PT],
                                      start=True, stop=True)
            mm.then_inc(sem("dt_c"), 1)
            pe.wait_ge(sem("dt_pc"), 1)
            nc.tensor.matmul(ps[:, 2, 0:P], over, pc.rearrange("p b n -> p (b n)"), start=True, stop=True)\
                .then_inc(sem("dt_c"), 1)
            k = 0

            def group(k):
                if k >= 2:
                    pe.wait_ge(sem(f"dt_cp{k % 2}"), k // 2)
                return ps[:, 6 + k % 2]

            def copied(k):
                for j in (k - 1, k):
                    pe.wait_ge(sem(f"dt_cp{j % 2}"), j // 2 + 1)

            for bp in range(NB // 2):
                for b2 in range(2):
                    b = 2 * bp + b2
                    pe.wait_ge(sem(f"seq_in{b % 4}"), 16 * NPAGE * (b // 4 + 1))
                    pe.wait_ge(sem(f"win_in{b2}"), 16 * (bp + 1))
                    for j in range(5):
                        bank = group(k)
                        k += 1
                        for i in range(4):
                            src = rs[b][:, 4 * j + i, 0:P] if j < 4 else rw[b2][:, i, 0:P]
                            mm = nc.tensor.transpose(bank[:, i * P:(i + 1) * P], src, ident[:])
                        mm.then_inc(sem("dt_tr"), 1)
                    copied(k - 1)
                    if b2 == 0:
                        pe.wait_ge(sem("dt_sel"), 1)
                        if bp:
                            pe.wait_ge(sem("dt_out"), bp)
                    part = slice(b2 * HD, (b2 + 1) * HD)
                    for j in range(4):
                        nc.tensor.matmul(ps[part, j], qbd[:, b], kts[:, 4 * j:4 * j + 4].rearrange("p a b -> p (a b)"),
                                         start=True, stop=True)
                    nc.tensor.matmul(ps[part, 4], qbd[:, b], ktw.rearrange("p a b -> p (a b)"), start=True, stop=True)
                    nc.tensor.matmul(ps[part, 5, 0:TS], qbd[:, b], knew[:, 0], start=True, stop=True)
                    nc.tensor.matmul(ps[part, 5, TS:2 * TS], qbd[:, b], knew[:, 1], start=True, stop=True)\
                        .then_inc(sem("dt_qk"), 1)
                pe.wait_ge(sem("dt_p"), bp + 1)
                for j in range(6):
                    bank = group(k)
                    k += 1
                    if j < 5:
                        for i in range(4):
                            src = ds[:, 8 * j + 2 * i:8 * j + 2 * i + 2].rearrange("p a b -> p (a b)") if j < 4 \
                                else dw[:, i * P:(i + 1) * P]
                            mm = nc.tensor.transpose(bank[:, i * P:(i + 1) * P], src, ident[:])
                    else:
                        nc.tensor.transpose(bank[0:TS, 0:P], ds[:, NCB], ident[:])
                        nc.tensor.transpose(bank[0:TS, P:2 * P], dw[:, WIN0:], ident[:])
                        mm = nc.tensor.transpose(bank[0:NCB, 2 * P:3 * P], pc[:, bp], ident[:])
                    mm.then_inc(sem("dt_tr"), 1)
                copied(k - 1)
                for b2 in range(2):
                    b = 2 * bp + b2
                    c = slice(b2 * HD, (b2 + 1) * HD)
                    out = ps[:, 5, P + b2 * HD:P + (b2 + 1) * HD]
                    nc.tensor.matmul(out, vc[:, b], ptx[0:NCB, 2, c], start=True, stop=False)
                    for j in range(NPAGE):
                        nc.tensor.matmul(out, rs[b][:, j, P:], pts[:, j, c], start=False, stop=False)
                    nc.tensor.matmul(out, NEW_S[:, P:], ptx[:, 0, c], start=False, stop=False)
                    for j in range(4):
                        nc.tensor.matmul(out, rw[b2][:, j, P:], ptw[:, j, c], start=False, stop=False)
                    mm = nc.tensor.matmul(out, NEW_W[:, P:], ptx[:, 1, c], start=False, stop=True)
                mm.then_inc(sem("dt_pv"), 1)

        def dec_copies(e, copy, which, kinds, bp, b=None):
            for k, (kind, gp, gb, j) in enumerate(dgroups):
                if k % 2 != which or kind not in kinds or gp != bp or (b is not None and gb != b):
                    continue
                e.wait_ge(sem("dt_tr"), k + 1)
                if kind[0] == "k" and gb:
                    e.wait_ge(sem("dt_qk"), gb)
                if kind[0] == "p" and bp:
                    e.wait_ge(sem("dt_pv"), bp)
                bank = ps[:, 6 + k % 2]
                b4 = bank.rearrange("p (a b) -> p a b", a=4)
                if kind == "k":
                    i = copy(kts[:, 4 * j:4 * j + 4], b4)
                elif kind == "kw":
                    i = copy(ktw, b4)
                elif kind == "p":
                    i = copy(pts[:, 4 * j:4 * j + 4], b4)
                elif kind == "pw":
                    i = copy(ptw, b4)
                else:
                    copy(ptx[:, 0:2], b4[0:TS, 0:2])
                    i = copy(ptx[0:NCB, 2], bank[0:NCB, 2 * P:3 * P])
                i.then_inc(sem(f"dt_cp{which}"), 1)

        def dec_act(act, E):
            act.wait_ge(sem("dt_cs"), 1)
            nc.scalar.activation(pc, pc, ACT.Exp).then_inc(sem("dt_ce"), 1)
            for bp in range(NB // 2):
                dec_copies(act, nc.scalar.copy, 1, ("k", "kw"), bp)
                act.wait_ge(sem("dt_ms"), bp + 1)
                nc.scalar.activation(ds, ds, ACT.Exp, scale=-1.0, bias=small[:, 0:1], accum_out=small[:, 2:3])
                act.wait_ge(sem("dt_mw"), bp + 1)
                nc.scalar.activation(dw, dw, ACT.Exp, bias=small[:, 1:2], accum_out=small[:, 3:4])\
                    .then_inc(sem("dt_e"), 1)
                dec_copies(act, nc.scalar.copy, 1, ("p", "pw", "px"), bp)

        def dec_dve(dve, E):
            v, ch = nc.vector, E.chain
            loaded(dve, "dec_in")
            dve.wait_ge(sem("dt_c"), 1)
            m4, d4 = small[:, 8:12], small[:, 12:16]
            gp = ra.rearrange("p a b -> p (a b)")[:, 0:96].rearrange("p (b n) -> p b n", b=4)
            ch(v.tensor_tensor(gp, ps[:, 1, 0:96].rearrange("p (b n) -> p b n", b=4),
                               pick.unsqueeze(1).to_broadcast([P, 4, 24]), ALU.mult))
            ch(v.tensor_reduce(grow, gp.rearrange("p b (h k) -> p b k h", k=3), AX_X, ALU.add))
            ch(v.tensor_tensor(pc, ps[:, 0, 0:P].rearrange("p (b n) -> p b n", b=4),
                               dec_cmp.unsqueeze(1).to_broadcast([P, 4, NCB]), ALU.add))
            ch(v.tensor_reduce(m4, pc, AX_X, ALU.max))
            v.tensor_tensor(pc, pc, m4.unsqueeze(2).to_broadcast([P, 4, NCB]), ALU.subtract).then_inc(sem("dt_cs"), 1)
            dve.wait_ge(sem("dt_ce"), 1)
            ch(v.tensor_reduce(d4, pc, AX_X, ALU.add))
            ch(v.reciprocal(d4, d4))
            v.tensor_tensor(pc, pc, d4.unsqueeze(2).to_broadcast([P, 4, NCB]), ALU.mult).then_inc(sem("dt_pc"), 1)
            dve.wait_ge(sem("dt_c"), 2)
            ch(v.tensor_copy(imp, ps[:, 2, 0:P].rearrange("p (b n) -> p b n", b=4)))
            v.memset(selb[:, :, NCB:], 0.0)
            v.tensor_tensor(pc, pc, grow[:, :, 0:1].to_broadcast([P, 4, NCB]), ALU.mult).then_inc(sem("dt_sel"), 1)
            dve.wait_ge(sem("dt_sel"), 1)

            def select(bp):
                other = imp[:, bp].unsqueeze(1).to_broadcast([P, NCB, NCB])
                this = imp[:, bp].unsqueeze(2).to_broadcast([P, NCB, NCB])
                s = selb[:, bp, 0:NCB]
                v.tensor_tensor(ra, other, this, ALU.is_gt)
                ch(v.tensor_tensor(rb, other, this, ALU.is_equal))
                ch(v.tensor_tensor(rb, rb, earlier.rearrange("p (a b) -> p a b", a=NCB), ALU.mult))
                ch(v.tensor_tensor(ra, ra, rb, ALU.add))
                ch(v.tensor_reduce(s, ra, AX_X, ALU.add))
                ch(v.tensor_scalar(s, s, TOPK - 1.5, -NEG, ALU.is_lt, ALU.mult))
                ch(v.tensor_scalar(s, s, NEG, None, ALU.add))
                ch(v.tensor_tensor(s, s, dec_blk, ALU.add))

            for bp in range(NB // 2):
                dec_copies(dve, v.tensor_copy, 0, ("k", "kw"), bp)
                if bp == 0:
                    select(0)
                dve.wait_ge(sem("dt_qk"), 2 * bp + 2)
                v.tensor_tensor(ds[:, 0:NCB], ps[:, 0:4].rearrange("p a (b c) -> p (a b) c", c=BLK),
                                dec_off.unsqueeze(1).to_broadcast([P, NCB, BLK]), ALU.add)
                v.tensor_tensor(ds[:, NCB], ps[:, 5, 0:TS], dec_new[:, bp], ALU.add)
                v.tensor_tensor(dw[:, 0:WIN0], ps[:, 4], dec_win, ALU.add)
                ch(v.tensor_tensor(dw[:, WIN0:], ps[:, 5, TS:2 * TS], dec_new[:, bp], ALU.add))
                v.tensor_tensor_reduce(ds, ds, selb[:, bp].unsqueeze(2).to_broadcast([P, NCB + 1, BLK]), -1.0, -NEG,
                                       ALU.add, ALU.min, small[:, 0:1]).then_inc(sem("dt_ms"), 1)
                ch(v.tensor_reduce(small[:, 1:2], dw, AX_X, ALU.max))
                v.tensor_scalar(small[:, 1:2], small[:, 1:2], -1.0, None, ALU.mult).then_inc(sem("dt_mw"), 1)
                dve.wait_ge(sem("dt_e"), bp + 1)
                ch(v.reciprocal(small[:, 4:6], small[:, 2:4]))
                ch(v.tensor_tensor(small[:, 4:6], small[:, 4:6], grow[:, bp, 1:3], ALU.mult))
                v.tensor_scalar(ds, ds, small[:, 4:5], None, ALU.mult)
                v.tensor_scalar(dw, dw, small[:, 5:6], None, ALU.mult).then_inc(sem("dt_p"), 1)
                dec_copies(dve, v.tensor_copy, 0, ("p", "pw", "px"), bp)
                if bp + 1 < NB // 2:
                    for which in range(2):
                        dve.wait_ge(sem(f"dt_cp{which}"), 8 * (bp + 1))
                    select(bp + 1)
                dve.wait_ge(sem("dt_pv"), bp + 1)
                for b2 in range(2):
                    for g in range(G):
                        half = slice(g * HD, (g + 1) * HD)
                        c = P + b2 * HD + g * 32
                        t0 = SEQ + (2 * bp + b2) * DL
                        i = v.tensor_copy(oN[half, :, t0:t0 + DL],
                                          ps[half, 5, c:c + 32].rearrange("p (r t) -> p r t", r=R0))
                i.then_inc(sem("dt_out"), 1)

        def residual_pe(pe, E, rhs):
            for m in range(4):
                w = E.next_panel()
                for s in range(2):
                    mm = dense_unit(pe, E, s, range(KC), lambda n: w[:, n, s * P:(s + 1) * P], rhs)
                    mm.then_inc(unit_ready[s], 1)
                E.free_panel(unit_ready[1], E.seen[1])

        def residual_dve(dve, E):
            for u in range(KC):
                E.unit_wait(u % 2)
                for j, (a, b) in enumerate(SPLIT):
                    i = nc.vector.tensor_tensor(xT[:, u, a:b], xT[:, u, a:b], ps[:, 3 * (u % 2) + j, 0:b - a], ALU.add)
                i.then_inc(unit_free[u % 2], 1)

        def skip_units(E, n):
            for s in range(2):
                E.pass_unit(s, n)

        def split_unit(pe, E, s, chunks, w_of, rhs_of, made=None):
            E.unit_start(s)
            for n, k in enumerate(chunks):
                if made:
                    pe.wait_ge(made[0], made[1] + k + 1)
                (wh, wl), (xh, xl) = w_of(n), rhs_of(k)
                for w, x, first, last in ((wh, xh, n == 0, False), (wh, xl, False, False),
                                          (wl, xh, False, n == len(chunks) - 1)):
                    for j, (a, b) in enumerate(SPLIT):
                        mm = nc.tensor.matmul(ps[:, 3 * s + j, 0:b - a], w, x[:, a:b], start=first, stop=last)
            return mm

        def split_panel(E, cols):
            n = E.panel
            E.panel += 1
            E.e.wait_ge(w_split, E.after("w_split") + 1)
            return [x[n % SLOTS][:].rearrange("p (k n) -> p k n", n=cols) for x in (w_hi, w_lo)]

        def pool_split(pool, E, count):
            for _ in range(count):
                n = E.panel
                w = E.next_panel().rearrange("p a b -> p (a b)")
                E.chain(nc.gpsimd.tensor_copy(w_hi[n % SLOTS][:], w))
                nc.gpsimd.tensor_tensor(w_lo[n % SLOTS][:], w, f32(w_hi[n % SLOTS][:]), ALU.subtract).then_inc(w_split, 1)

        N_FFN = sum(e - f + D_MODEL // down_cols(f, e) for f, e in FGROUPS)

        def ffn_pe(pe, E):
            for f, e in FGROUPS:
                for k in range(f, e):
                    hi, lo = split_panel(E, WCOL)
                    for s in range(2):
                        c = slice(s * P, (s + 1) * P)
                        mm = split_unit(pe, E, s, range(KC), lambda n: (hi[:, n, c], lo[:, n, c]),
                                        lambda k: (h_hi[k], h_lo[k]), (sem("norm_done"), E.normed) if k == 0 and s == 0 else None)
                        mm.then_inc(unit_ready[s], 1)
                    E.free_panel(unit_ready[1], E.seen[1])
                n = down_cols(f, e)
                hidden = E.after("hidden", e - f)
                for c in range(0, D_MODEL, n):
                    hi, lo = split_panel(E, n)
                    for u in range(n // P):
                        s = u % 2
                        cc = slice(u * P, (u + 1) * P)
                        mm = split_unit(pe, E, s, range(e - f), lambda n: (hi[:, n, cc], lo[:, n, cc]),
                                        lambda k: (a_hi[k], a_lo[k]),
                                        (sem("hidden_split"), hidden) if c == 0 and u == 0 else None)
                        mm.then_inc(unit_ready[s], 1)
                    E.free_panel(unit_ready[1], E.seen[1])

        def ffn_act(act, E):
            for f, e in FGROUPS:
                for k in range(f, e):
                    E.unit_wait(0)
                    E.pass_unit(1)
                    for j, (a, b) in enumerate(SPLIT):
                        i = nc.scalar.activation(a_raw[:, k - f, a:b], ps[:, j, 0:b - a], ACT.Silu)
                    i.then_inc(unit_free[0], 1)
                    act.wait_ge(unit_free[1], E.seen[1])
                    nc.scalar.copy(a_hi[k - f][:], a_raw[:, k - f]).then_inc(sem("hidden_hi"), 1)
                skip_units(E, KC // 2)

        def ffn_dve(dve, E):
            v = nc.vector
            for f, e in FGROUPS:
                for k in range(f, e):
                    E.unit_wait(1)
                    E.pass_unit(0)
                    dve.wait_ge(unit_free[0], E.seen[0])
                    h = a_raw[:, k - f]
                    for j, (a, b) in enumerate(SPLIT):
                        i = v.tensor_tensor(h[:, a:b], h[:, a:b], ps[:, 3 + j, 0:b - a], ALU.mult)
                    i.then_inc(unit_free[1], 1)
                    dve.wait_ge(sem("hidden_hi"), E.after("hidden") + 1)
                    v.tensor_tensor(a_lo[k - f][:], h, f32(a_hi[k - f][:]), ALU.subtract).then_inc(sem("hidden_split"), 1)
                residual_dve(dve, E)

        oT1 = xc

        def proj1_pe(pe, E):
            token_major_pe(pe, E, [256])
            for rp in range(4):
                w = E.next_panel()
                for s in range(2):
                    mm = dense_unit(pe, E, s, range(KC), lambda n: w[:, n, s * P:(s + 1) * P], lambda k: hT[:, k])
                    mm.then_inc(unit_ready[s], 1)
                E.free_panel(unit_ready[1], E.seen[1])

        def proj1_out(E, ns, which, scaled, copy):
            token_major_out(E, ns, copy, which, [256], kvt1)
            for r in range(R1):
                if r % 2 != which:
                    E.pass_unit(r % 2)
                    continue
                E.unit_wait(which)
                for j, (a, b) in enumerate(SPLIT):
                    i = scaled(qT1[:, r, a:b], ps[:, 3 * which + j, 0:b - a], HD ** -0.5)
                i.then_inc(unit_free[which], 1)

        bias1 = at(z0, R1 * G, 2 * P)
        s1 = [at(s, 4, 2 * P) for s in (kv0 + 2304, kv0 + 3328, q0 + T + 2176)]
        pt1 = [at(kv0 + 4352 + k * 1024, 8, P) for k in range(2)]
        o1 = [at(kv0 + 6400 + k * 256, 4, HD) for k in range(2)]
        loads["bias1_in"] = [(bias1, const["bias_swa"])]
        U1 = [(r, i2) for r in range(R1) for i2 in range(PT // 2)]
        neg1 = [small[:, 16 * k:16 * k + 4] for k in range(3)]
        sink1 = [small[:, 16 * k + 4:16 * k + 8] for k in range(3)]

        def swa_pe(pe, E):
            for i in range(NT):
                n = tile_n(i)
                mm = nc.tensor.transpose(ps[:, i // 4, (i % 4) * P:(i % 4) * P + n], kvt1[0:n, i, 0:P], ident[0:n, 0:n])
            mm.then_inc(sem("kt1_tr"), 1)
            pe.wait_ge(sem("kt1"), 1)
            n_units = len(U1)
            for step in range(n_units + 4):
                if step < n_units:
                    r, i2 = U1[step]
                    if step >= 2:
                        pe.wait_ge(sem("sw_scored"), step - 1)
                    for k in range(4):
                        i, g = 2 * i2 + k // 2, k % 2
                        half = slice(g * HD, (g + 1) * HD)
                        o = P if i == 0 else 0
                        c = (k // 2) * 2 * P
                        mm = nc.tensor.matmul(ps[:, 2 * (step % 2) + g, c + o:c + 2 * P],
                                              qT1[half, r, toks(i)], kT1[half, (i - 1) * P + o:(i + 1) * P],
                                              start=True, stop=True)
                    mm.then_inc(sem("sw_qk"), 1)
                if 2 <= step < n_units + 2:
                    u = step - 2
                    r, i2 = U1[u]
                    pe.wait_ge(sem("sw_exp"), u + 1)
                    for ii in range(2):
                        if u:
                            pe.wait_ge(sem(f"sw_copied{ii}"), u)
                        for k in range(4):
                            g, j = k // 2, k % 2
                            if i2 == 0 and ii == 0 and j == 0:
                                continue
                            mm = nc.tensor.transpose(ps[:, 4 + ii, k * P:(k + 1) * P],
                                                     s1[u % 3][:, 2 * g + ii, j * P:(j + 1) * P], ident[:])
                        mm.then_inc(sem("sw_tr"), 1)
                if 3 <= step < n_units + 3:
                    u = step - 3
                    r, i2 = U1[u]
                    for ii in range(2):
                        pe.wait_ge(sem(f"sw_copied{ii}"), u + 1)
                    if u >= 2:
                        pe.wait_ge(sem("sw_oT"), u - 1)
                    for k in range(4):
                        i, g = 2 * i2 + k // 2, k % 2
                        js = (1,) if i == 0 else (0, 1)
                        for j in js:
                            mm = nc.tensor.matmul(ps[:, 6 + u % 2, k * HD:(k + 1) * HD], pt1[u % 2][:, (k // 2) * 4 + g * 2 + j],
                                                  kvt1[:, i - 1 + j, P + g * HD:P + (g + 1) * HD],
                                                  start=j == js[0], stop=j == 1)
                    mm.then_inc(sem("sw_pv"), 1)
                if 4 <= step:
                    u = step - 4
                    pe.wait_ge(sem("sw_o"), u + 1)
                    for ii in range(2):
                        mm = nc.tensor.transpose(ps[:, 6 + u % 2, 256 + ii * P:256 + (ii + 1) * P],
                                                 o1[u % 2][:, 2 * ii:2 * ii + 2].rearrange("p g e -> p (g e)"), ident[:])
                    mm.then_inc(sem("sw_ot"), 1)

        def swa_copy(e, copy, u, ii):
            e.wait_ge(sem("sw_tr"), 2 * u + ii + 1)
            if u >= 2:
                e.wait_ge(sem("sw_pv"), u - 1)
            src = ps[:, 4 + ii].rearrange("p (k t) -> p k t", k=4)
            dst = pt1[u % 2][:, 4 * ii:4 * ii + 4]
            if U1[u][1] == 0 and ii == 0:
                src, dst = src[:, 1::2], dst[:, 1::2]
            copy(dst, src).then_inc(sem(f"sw_copied{ii}"), 1)

        def swa_dve(dve, E):
            v, ch = nc.vector, E.chain
            dve.wait_ge(sem("kt1_tr"), 1)
            v.tensor_copy(kT1, ps[:, 0:3].rearrange("p b c -> p (b c)")[:, 0:T]).then_inc(sem("kt1"), 1)
            loaded(dve, "bias1_in")
            n_units = len(U1)
            for step in range(n_units + 4):
                if 4 <= step:
                    u = step - 4
                    dve.wait_ge(sem("sw_pv"), u + 1)
                    dve.wait_ge(sem("sw_den"), u + 1)
                    dn = den6[u % 6]
                    ch(v.tensor_tensor(dn[:, 0:4], dn[:, 0:4], dn[:, 4:8], ALU.add))
                    ch(v.reciprocal(dn[:, 0:4], dn[:, 0:4]))
                    if u >= 2:
                        dve.wait_ge(sem("sw_ot"), u - 1)
                    v.tensor_tensor(o1[u % 2].rearrange("p (i g) e -> p i g e", i=2),
                                    ps[:, 6 + u % 2, 0:256].rearrange("p (i g e) -> p i g e", i=2, g=G),
                                    dn[:, 0:4].rearrange("p (g i) -> p i g", g=G).unsqueeze(3)
                                    .to_broadcast([P, 2, 2, HD]), ALU.mult).then_inc(sem("sw_o"), 1)
                if 3 <= step < n_units + 3:
                    swa_copy(dve, v.tensor_copy, step - 3, 0)
                if step < n_units:
                    u = step
                    r, i2 = U1[u]
                    s, bk = s1[u % 3], ps[:, 2 * (u % 2):2 * (u % 2) + 2]
                    dve.wait_ge(sem("sw_qk"), u + 1)
                    if u >= 3:
                        dve.wait_ge(sem("sw_tr"), 2 * u - 4)
                    bias = bias1[:, 2 * r:2 * r + 2]
                    s4 = s.rearrange("p (g i) c -> p g i c", g=2)
                    b4 = bk.rearrange("p g (i c) -> p g i c", i=2)
                    if i2:
                        i = v.tensor_tensor(s4, b4, bias.unsqueeze(2).to_broadcast([P, 2, 2, 2 * P]), ALU.add)
                    else:
                        v.memset(s4[:, :, 0, 0:P], NEG)
                        v.tensor_tensor(s4[:, :, 1], b4[:, :, 1], bias, ALU.add)
                        i = v.tensor_tensor(s4[:, :, 0, P:], b4[:, :, 0, P:], bias[:, :, P:], ALU.add)
                    i.then_inc(sem("sw_scored"), 1)
                    dve.wait_ge(sem("sw_scored"), u + 1)
                    ng, sk = neg1[u % 3], sink1[u % 3]
                    ch(v.tensor_reduce(ng, s, AX_X, ALU.max))
                    sr = sinks[:, r].unsqueeze(2).to_broadcast([P, 2, 2])
                    g4 = ng.rearrange("p (g i) -> p g i", g=2)
                    ch(v.tensor_tensor(g4, g4, sr, ALU.max))
                    v.tensor_tensor(sk.rearrange("p (g i) -> p g i", g=2), sr, g4, ALU.subtract)
                    v.tensor_scalar(ng, ng, -1.0, None, ALU.mult).then_inc(sem("sw_m"), 1)

        den6 = [cst[:, 8 * k:8 * k + 8] for k in range(6)]

        def swa_act(act, E):
            n_units = len(U1)
            for step in range(n_units + 5):
                if 3 <= step < n_units + 3:
                    swa_copy(act, nc.scalar.copy, step - 3, 1)
                if 5 <= step:
                    u = step - 5
                    r, i2 = U1[u]
                    act.wait_ge(sem("sw_ot"), u + 1)
                    nc.scalar.copy(oT1[:, r, 256 * i2:256 * (i2 + 1)], ps[:, 6 + u % 2, 256:512])\
                        .then_inc(sem("sw_oT"), 1)
                if step < n_units:
                    u = step
                    act.wait_ge(sem("sw_m"), u + 1)
                    if u >= 6:
                        act.wait_ge(sem("sw_o"), u - 5)
                    dn = den6[u % 6]
                    nc.scalar.activation(dn[:, 4:8], sink1[u % 3], ACT.Exp).then_inc(sem("sw_den"), 1)
                    for k in range(4):
                        i = nc.scalar.activation(s1[u % 3][:, k], s1[u % 3][:, k], ACT.Exp,
                                                 bias=neg1[u % 3][:, k:k + 1], accum_out=dn[:, k:k + 1])
                    i.then_inc(sem("sw_exp"), 1)

        raw1 = at(q0 + T, NB, 256)
        buf1 = at(q0 + T + 2048, 1, WIN1)[:, 0]
        qbd1, kb1 = at(kv0 + 2304, NB, P), at(kv0 + 3328, NB, P)
        sd1 = at(kv0 + 4352, NB, WIN1 + TS)
        pd1, pn1 = at(z0, NB, P), at(z0 + 1024, NB, P, parts=TS)
        new1 = at(z0 + 2048, NB, TS)
        loads["dec1_in"] = [(raw1, d["state_swa_kv"][0].rearrange("b p a g e -> p b (a g e)")), (buf1, const["swa_buf"])]
        loads["new1_in"] = [(new1, const["swa_new"])]

        def swa_dec_pe(pe, E):
            loaded(pe, "dec1_in")
            for b in range(NB):
                mm = nc.tensor.transpose(ps[:, b // 4, (b % 4) * P:(b % 4 + 1) * P], raw1[:, b, 0:P], ident[:])
            mm.then_inc(sem("sd_mm"), 1)
            pe.wait_ge(sem("sd_k"), 1)
            for b in range(NB):
                nc.tensor.matmul(ps[:, 2 + b // 4, (b % 4) * P:(b % 4 + 1) * P], qbd1[:, b], kb1[:, b], start=True, stop=True)
                mm = nc.tensor.matmul(ps[:, 4, b * TS:(b + 1) * TS], qbd1[:, b], kT1[:, SEQ:], start=True, stop=True)
            mm.then_inc(sem("sd_mm"), 1)
            pe.wait_ge(sem("sd_p"), 1)
            for b in range(NB):
                nc.tensor.transpose(ps[:, 5 + b // 4, (b % 4) * P:(b % 4 + 1) * P], sd1[:, b, 0:P], ident[:])
                mm = nc.tensor.transpose(ps[0:TS, 7 * (1 - b // 4), (b % 4) * P:(b % 4 + 1) * P], sd1[:, b, P:], ident[:])
            mm.then_inc(sem("sd_mm"), 1)
            pe.wait_ge(sem("sd_pt"), 1)
            pe.wait_ge(sem("sd_pn"), 1)
            for b in range(NB):
                out = ps[:, 2 + b // 4, (b % 4) * P:(b % 4 + 1) * P]
                nc.tensor.matmul(out, raw1[:, b, P:], pd1[:, b], start=True, stop=False)
                mm = nc.tensor.matmul(out, kvt1[0:TS, PT, P:], pn1[:, b], start=False, stop=True)
            mm.then_inc(sem("sd_mm"), 1)

        def swa_dec_act(act, E):
            act.wait_ge(sem("sd_s"), 1)
            nc.scalar.activation(sd1, sd1, ACT.Exp)
            nc.scalar.activation(small[:, 8:16], small[:, 8:16], ACT.Exp).then_inc(sem("sd_e"), 1)
            act.wait_ge(sem("sd_mm"), 3)
            for k in range(2):
                i = nc.scalar.copy(pn1[:, 4 * k:4 * k + 4], ps[0:TS, 7 * (1 - k)].rearrange("p (b t) -> p b t", b=4))
            i.then_inc(sem("sd_pn"), 1)

        def swa_dec_dve(dve, E):
            v, ch = nc.vector, E.chain
            ch(v.memset(qbd1, 0.0))
            for g in range(G):
                half = slice(g * HD, (g + 1) * HD)
                v.tensor_copy(qbd1[half, :, g * HD:(g + 1) * HD].rearrange("p b (r t) -> p b r t", r=R1),
                              qT1[half, :, SEQ:].rearrange("p r (b t) -> p b r t", b=NB))
            dve.wait_ge(sem("sd_mm"), 1)
            for k in range(2):
                i = v.tensor_copy(kb1[:, 4 * k:4 * k + 4], ps[:, k].rearrange("p (b t) -> p b t", b=4))
            i.then_inc(sem("sd_k"), 1)
            loaded(dve, "dec1_in")
            loaded(dve, "new1_in")
            dve.wait_ge(sem("sd_mm"), 2)
            for k in range(2):
                v.tensor_tensor(sd1[:, 4 * k:4 * k + 4, 0:P], ps[:, 2 + k].rearrange("p (b t) -> p b t", b=4),
                                buf1.unsqueeze(1).to_broadcast([P, 4, P]), ALU.add)
            ch(v.tensor_tensor(sd1[:, :, P:], ps[:, 4].rearrange("p (b t) -> p b t", b=NB), new1, ALU.add))
            m, es, dn = small[:, 0:8], small[:, 8:16], small[:, 16:24]
            ch(v.tensor_reduce(m, sd1, AX_X, ALU.max))
            ch(v.tensor_scalar(m, m, sink_col[:], None, ALU.max))
            v.tensor_scalar(es, m, -1.0, sink_col[:], ALU.mult, ALU.add)
            v.tensor_tensor(sd1, sd1, m.unsqueeze(2).to_broadcast([P, NB, WIN1 + TS]), ALU.subtract)\
                .then_inc(sem("sd_s"), 1)
            dve.wait_ge(sem("sd_e"), 1)
            ch(v.tensor_reduce(dn, sd1, AX_X, ALU.add))
            ch(v.tensor_tensor(dn, dn, es, ALU.add))
            ch(v.reciprocal(dn, dn))
            v.tensor_tensor(sd1, sd1, dn.unsqueeze(2).to_broadcast([P, NB, WIN1 + TS]), ALU.mult).then_inc(sem("sd_p"), 1)
            dve.wait_ge(sem("sd_mm"), 3)
            for k in range(2):
                i = v.tensor_copy(pd1[:, 4 * k:4 * k + 4], ps[:, 5 + k].rearrange("p (b t) -> p b t", b=4))
            i.then_inc(sem("sd_pt"), 1)
            dve.wait_ge(sem("sd_mm"), 4)
            for k in range(2):
                for g in range(G):
                    half = slice(g * HD, (g + 1) * HD)
                    src = ps[half, 2 + k].rearrange("p (b g r t) -> p b g r t", b=4, g=G, r=R1)[:, :, g]
                    dst = oT1[half, :, SEQ + 32 * k:SEQ + 32 * (k + 1)].rearrange("p r (b t) -> p b r t", b=4)
                    v.tensor_copy(dst, src)

        def swa_pool(pool, E):
            store(pool, rows(d["swa_prompt"][0, 0]), kvt1[:, PT - 1])
            for b in range(NB):
                store(pool, rows(d["swa_sample"][0, b])[WIN1 - DL:], kvt1[b * DL:(b + 1) * DL, PT])

        yo = [at(kv0 + s * D_MODEL, D_MODEL, 1)[:, :, 0] for s in range(2)]

        def store_pe(pe, E):
            for i in range(NT):
                n = tile_n(i)
                if i >= 2:
                    pe.wait_ge(sem("y_half0"), i - 1)
                    pe.wait_ge(sem("y_half1"), i - 1)
                for c in range(KC):
                    if i == 0:
                        normed(pe, E, c)
                    mm = nc.tensor.transpose(ps[0:n, 2 * (i % 2) + c // 4, (c % 4) * P:(c % 4 + 1) * P],
                                             hT[:, c, toks(i)], ident[:])
                mm.then_inc(sem("y_tr"), 1)

        def store_copy(e, copy, which):
            for i in range(NT):
                n = tile_n(i)
                e.wait_ge(sem("y_tr"), i + 1)
                if i >= 2:
                    e.wait_ge(sem(f"y_stored{i % 2}"), 16 * (i // 2))
                copy(yo[i % 2][0:n, which * 512:(which + 1) * 512], ps[0:n, 2 * (i % 2) + which])\
                    .then_inc(sem(f"y_half{which}"), 1)

        def store_sp(sp):
            for i in range(NT):
                sp.wait_ge(sem("y_half0"), i + 1)
                sp.wait_ge(sem("y_half1"), i + 1)
                dst = d["y_prompt"][0, toks(i)] if i < PT else d["y_sample"].rearrange("b t n -> (b t) n")
                sp.dma_start(dst, yo[i % 2][0:tile_n(i)]).then_inc(sem(f"y_stored{i % 2}"), 16)

        def x_of(c):
            return xT[:, c]

        def h_of(c):
            return hT[:, c]

        def z_of(c):
            return zT[:, c]

        def raw_of(c):
            return h_raw[:, c]

        def norm(n, src, dst, g0, width, sq=None, split=False):
            return {"n": n, "src": src, "dst": dst, "gain": g0, "width": width, "sq": sq or dst, "split": split}

        NORMS = {"proj0": norm(KC, x_of, h_of, gain("mix", 0), D_MODEL),
                 "cmp": norm(4, z_of, z_of, gain("ssm"), SX, sq=lambda c: at(w0, R0, T)[:, c]),
                 "ffn0": norm(KC, x_of, raw_of, gain("ffn", 0), D_MODEL, split=True),
                 "proj1": norm(KC, x_of, h_of, gain("mix", 1), D_MODEL),
                 "ffn1": norm(KC, x_of, raw_of, gain("ffn", 1), D_MODEL, split=True),
                 "store": norm(KC, x_of, h_of, gain("final"), D_MODEL)}

        @block.tensor
        def _(pe):
            E = Engine(pe, nc.tensor, "pe")
            residual = {"out0": lambda k: oN[:, k] if k < R0 else zT[:, k - R0], "out1": lambda k: oT1[:, k]}
            body = {"setup": setup_pe, "cache": cache_pe, "load": load_pe, "proj0": proj0_pe, "prep": prep_pe, "conv": lambda pe, E: hidden_pe(pe, 1),
                    "ssm": ssm_pe, "cmp": cmp_pe, "attn": attn_pe, "dec": dec_pe, "ffn0": ffn_pe, "ffn1": ffn_pe,
                    "proj1": proj1_pe, "swa": swa_pe, "swa_dec": swa_dec_pe,
                    "store": store_pe}
            for name in STAGES:
                if name in NORMS:
                    norm_pe(pe, E, NORMS[name])
                if name in residual:
                    residual_pe(pe, E, residual[name])
                elif name in body:
                    body[name](pe, E)
                E.end_stage(name)

        @block.scalar
        def _(act):
            E = Engine(act, nc.scalar, "act")
            body = {"setup": setup_act, "cache": cache_act, "load": load_act, "proj0": proj0_act, "prep": prep_act,
                    "conv": conv_act, "ssm": ssm_act, "cmp": cmp_act, "attn": attn_act, "dec": dec_act,
                    "ffn0": ffn_act, "ffn1": ffn_act, "swa": swa_act, "swa_dec": swa_dec_act,
                    "proj1": lambda e, E: proj1_out(E, nc.scalar, 0, nc.scalar.mul, nc.scalar.copy),
                    "store": lambda e, E: store_copy(e, nc.scalar.copy, 1)}
            for name in STAGES:
                if name in NORMS:
                    norm_act(act, E, NORMS[name])
                if name in ("out0", "out1"):
                    skip_units(E, 4)
                elif name in body:
                    body[name](act, E)
                E.end_stage(name)

        @block.vector
        def _(dve):
            E = Engine(dve, nc.vector, "dve")
            body = {"setup": setup_dve, "cache": cache_dve, "load": load_dve, "proj0": proj0_dve, "prep": prep_dve,
                    "conv": conv_dve, "ssm": ssm_dve, "cmp": cmp_dve, "attn": attn_dve, "dec": dec_dve,
                    "ffn0": ffn_dve, "ffn1": ffn_dve, "swa": swa_dve, "swa_dec": swa_dec_dve,
                    "proj1": lambda e, E: proj1_out(E, nc.vector, 1, nc.vector.tensor_scalar_mul, nc.vector.tensor_copy),
                    "store": lambda e, E: store_copy(e, nc.vector.tensor_copy, 0)}
            for name in STAGES:
                if name in NORMS:
                    norm_dve(dve, E, NORMS[name])
                if name in ("out0", "out1"):
                    residual_dve(dve, E)
                elif name in body:
                    body[name](dve, E)
                E.end_stage(name)

        @block.gpsimd
        def _(pool):
            E = Engine(pool, nc.gpsimd, "pool")
            body = {"cache": cache_pool, "prep": prep_pool, "ssm": ssm_pool, "swa": swa_pool}
            for name in STAGES:
                if name in ("ffn0", "ffn1"):
                    E.panel = len(panels) - N_FFN if name == "ffn1" else PROJ0 + 4
                    pool_split(pool, E, N_FFN)
                if name in body:
                    body[name](pool, E)
                if name == "attn":
                    pool.wait_ge(stored, 16 * stores[0])
                E.end_stage(name)
            pool.wait_ge(stored, 16 * stores[0])

        @block.sync
        def _(sp):
            sent = [0]

            def weights(upto):
                while sent[0] < upto:
                    n = sent[0]
                    if n >= SLOTS:
                        sp.wait_ge(*panel_done[n - SLOTS])
                    for dst, src in panels[n](wp[n % SLOTS]):
                        sp.dma_start(dst, src).then_inc(w_ready[n % SLOTS], 16)
                    sent[0] += 1

            load(sp, "setup_in")
            load(sp, "table_in")
            loaded(sp, "table_in")
            cache_sp(sp)
            weights(SLOTS)
            load_sp(sp)
            weights(PROJ0)
            load(sp, "prep_in", "proj0")
            hidden_sp(sp)
            load(sp, "ssm_in", "prep")
            load(sp, "ssm_state_in", "conv")
            cmp_sp(sp)
            load(sp, "bias_in", "cmp")
            sp.wait_ge(stage_end, END["proj0"])
            dec_pages(sp, 0)
            dec_sp(sp)
            sp.wait_ge(stage_end, END["dec"])
            n = PROJ0 + 4 + N_FFN
            weights(n + 5)
            load(sp, "bias1_in", "ffn0")
            weights(n + 5 + SLOTS)
            load(sp, "dec1_in", "proj1")
            load(sp, "new1_in", "swa")
            weights(len(panels))
            store_sp(sp)
            sp.wait_ge(sem("y_stored0"), 16 * (PT // 2 + 1))
            sp.wait_ge(sem("y_stored1"), 16 * (PT // 2))
            sp.wait_ge(sem("conv_stored"), 32)
            sp.wait_ge(sem("ssm_fin_stored"), 16)
            sp.wait_ge(sem("s0_stored"), 16 * NB)


def kernel(**inputs):
    import concourse.bacc as bacc
    from concourse.bass_utils import run_bass_kernel_spmd as run

    nc = bacc.Bacc("TRN2", target_bir_lowering=False, num_devices=1)
    arrays, d, const = {}, {}, {}
    for name in INPUTS:
        a = np.ascontiguousarray(inputs[name])
        arrays[f"in_{name}"] = a
        d[name] = nc.dram_tensor(f"in_{name}", a.shape, mybir.dt.from_np(a.dtype), kind="ExternalInput").ap()
    for name, a in constants().items():
        arrays[f"const_{name}"] = a
        const[name] = nc.dram_tensor(f"const_{name}", a.shape, mybir.dt.from_np(a.dtype), kind="ExternalInput").ap()
    for name, shape in OUTPUTS:
        d[name] = nc.dram_tensor(f"out_{name}", shape, F32, kind="ExternalOutput").ap()
    build(nc, d, const)
    got = run(nc, [arrays], core_ids=[0]).results[0]
    return tuple(got[f"out_{name}"] for name, _ in OUTPUTS)
```
